# Optimizing a Trainium2 kernel written in Bass

```python
import jax
import jax.numpy as jnp
from jax import lax
import numpy as np

D_MODEL = 1024
BATCH = 1
SEQ = 256
DEPTH = 2

GRID_W = 64
CTX_LEN = 256
D_INNER = 2 * D_MODEL
SSD_WIDTH = D_INNER // 2
SSD_HEAD_DIM = 64
SSD_HEADS = SSD_WIDTH // SSD_HEAD_DIM
SSD_GROUPS = 2
SSD_STATE = 128
SSD_TAPS = 5
SSD_CHUNK = 128
CONF_WIDTH = D_INNER // 4
CONF_TAPS = 31
SC_WIDTH = D_INNER // 4
SC_TAPS = 3
D_FF = 2816
N_MOD = 9
MACARON_WEIGHT = 0.5
EPS = 1e-6
GN = SSD_GROUPS * SSD_STATE
XBC_WIDTH = SSD_WIDTH + 2 * GN
SSD_IN = XBC_WIDTH + 2 * SSD_HEADS
IN_WIDTH = SSD_IN + SSD_WIDTH + 2 * CONF_WIDTH + 3 * SC_WIDTH

kernel_name = "hybrid_ssd_conformer_shortconv_dit_block"

def rmsnorm(x, g):
    xf = x.astype(jnp.float32)
    y = xf * lax.rsqrt(jnp.mean(xf * xf, axis=-1, keepdims=True) + EPS)
    return (y * g.astype(jnp.float32)).astype(x.dtype)

def layernorm(x, g, b):
    xf = x.astype(jnp.float32)
    mu = jnp.mean(xf, axis=-1, keepdims=True)
    var = jnp.mean(jnp.square(xf - mu), axis=-1, keepdims=True)
    y = (xf - mu) * lax.rsqrt(var + EPS)
    return (y * g.astype(jnp.float32) + b.astype(jnp.float32)).astype(x.dtype)

def dwconv(x, w, b):
    y = lax.conv_general_dilated(x, w[:, None, :].astype(x.dtype), window_strides=(1,), padding='SAME',
                                 dimension_numbers=('NWC', 'WIO', 'NWC'), feature_group_count=x.shape[-1])
    return y + b.astype(x.dtype)

def conv_along_rows(x, w, b):
    bsz, t, ch = x.shape
    rows = t // GRID_W
    return dwconv(x.reshape(bsz * rows, GRID_W, ch), w, b).reshape(bsz, t, ch)

def conv_along_cols(x, w, b):
    bsz, t, ch = x.shape
    rows = t // GRID_W
    xg = x.reshape(bsz, rows, GRID_W, ch).transpose(0, 2, 1, 3).reshape(bsz * GRID_W, rows, ch)
    y = dwconv(xg, w, b)
    return y.reshape(bsz, GRID_W, rows, ch).transpose(0, 2, 1, 3).reshape(bsz, t, ch)

def segsum(a):
    q = a.shape[-1]
    cs = jnp.cumsum(a, axis=-1)
    diff = cs[..., :, None] - cs[..., None, :]
    mask = jnp.tril(jnp.ones((q, q), dtype=bool))
    return jnp.where(mask, diff, -jnp.inf)

def ssd_scan(x, dt, A, B, C, h0):
    f32 = jnp.float32
    b, l, h, p = x.shape
    g, n = B.shape[-2:]
    r = h // g
    q = SSD_CHUNK
    nc = l // q
    xd = (x.astype(f32) * dt[..., None]).reshape(b, nc, q, g, r, p)
    Bc = B.astype(f32).reshape(b, nc, q, g, n)
    Cc = C.astype(f32).reshape(b, nc, q, g, n)
    a = (dt * A).reshape(b, nc, q, g, r).transpose(0, 3, 4, 1, 2)
    a_cum = jnp.cumsum(a, axis=-1)
    lmat = jnp.exp(segsum(a))
    cb = jnp.einsum('bclgn,bcsgn->bgcls', Cc, Bc)
    y_diag = jnp.einsum('bgcls,bgrcls,bcsgrp->bclgrp', cb, lmat, xd)
    decay_s = jnp.exp(a_cum[..., -1:] - a_cum)
    states = jnp.einsum('bcsgn,bgrcs,bcsgrp->bcgrpn', Bc, decay_s, xd)
    states = jnp.concatenate([h0.reshape(b, 1, g, r, p, n), states], axis=1)
    chunk_a = jnp.pad(a_cum[..., -1], ((0, 0), (0, 0), (0, 0), (1, 0)))
    chunk_decay = jnp.exp(segsum(chunk_a))
    states = jnp.einsum('bgrzc,bcgrpn->bzgrpn', chunk_decay, states)
    prev, final = states[:, :-1], states[:, -1]
    y_off = jnp.einsum('bclgn,bcgrpn,bgrcl->bclgrp', Cc, prev, jnp.exp(a_cum))
    y = (y_diag + y_off).reshape(b, l, h, p)
    return y, final.reshape(b, h, p, n)

def ssd_final_state(x, dt, A, B):
    f32 = jnp.float32
    b, l, h, p = x.shape
    g, n = B.shape[-2:]
    a_cum = jnp.cumsum(dt * A, axis=1)
    w = jnp.exp(a_cum[:, -1:] - a_cum) * dt
    xw = (x.astype(f32) * w[..., None]).reshape(b, l, g, h // g, p)
    st = jnp.einsum('blgn,blgrp->bgrpn', B.astype(f32), xw)
    return st.reshape(b, h, p, n)

def ssd_inputs(u, conv_w, conv_b, dt_bias, a_log):
    b, l, _ = u.shape
    xbc = jax.nn.silu(dwconv(u[..., :XBC_WIDTH], conv_w, conv_b))
    xs = xbc[..., :SSD_WIDTH].reshape(b, l, SSD_HEADS, SSD_HEAD_DIM)
    Bm = xbc[..., SSD_WIDTH:SSD_WIDTH + GN].reshape(b, l, SSD_GROUPS, SSD_STATE)
    Cm = xbc[..., SSD_WIDTH + GN:].reshape(b, l, SSD_GROUPS, SSD_STATE)
    dt_raw = u[..., XBC_WIDTH:].astype(jnp.float32).reshape(b, l, 2, SSD_HEADS)
    dt = jax.nn.softplus(dt_raw + dt_bias.astype(jnp.float32))
    A = -jnp.exp(a_log.astype(jnp.float32))
    return xs, Bm, Cm, dt, A

def flip_seq(t):
    return jnp.flip(t, axis=1)

def ssd_bidir(xs, Bm, Cm, dt, A, h0_f, h0_b):
    y_f, s_f = ssd_scan(xs, dt[:, :, 0], A[0], Bm, Cm, h0_f)
    y_b, s_b = ssd_scan(flip_seq(xs), flip_seq(dt[:, :, 1]), A[1], flip_seq(Bm), flip_seq(Cm), h0_b)
    return y_f + flip_seq(y_b), s_f, s_b

def mixer(u, h0_f, h0_b, conv_conf, conv_sc, lp):
    b, l, _ = u.shape
    o = SSD_IN
    z = u[..., o:o + SSD_WIDTH]
    o += SSD_WIDTH
    conf = u[..., o:o + 2 * CONF_WIDTH]
    o += 2 * CONF_WIDTH
    sc = u[..., o:]
    xs, Bm, Cm, dt, A = ssd_inputs(u[..., :SSD_IN], lp['ssd_conv_w'], lp['ssd_conv_b'], lp['dt_bias'], lp['a_log'])
    y, s_f, s_b = ssd_bidir(xs, Bm, Cm, dt, A, h0_f, h0_b)
    y = (y + lp['d_skip'].astype(jnp.float32)[:, None] * xs.astype(jnp.float32)).astype(u.dtype)
    y_ssd = rmsnorm(y.reshape(b, l, SSD_WIDTH) * jax.nn.silu(z), lp['ssd_norm'])
    v, gt = jnp.split(conf, 2, axis=-1)
    y_conf = jax.nn.silu(layernorm(conv_conf(v * jax.nn.sigmoid(gt), lp['conf_w'], lp['conf_b']), lp['ln_g'], lp['ln_b']))
    bg, cg, hh = jnp.split(sc, 3, axis=-1)
    y_sc = bg * conv_sc(cg * hh, lp['sc_w'], lp['sc_b'])
    return jnp.concatenate([y_ssd, y_conf, y_sc], axis=-1), s_f, s_b

def modulate(h, g_pre, shift, scale):
    return rmsnorm(h, g_pre) * (1 + scale) + shift

def gated_residual(h, y, g_post, gate, weight):
    return h + weight * gate * rmsnorm(y, g_post)

def swiglu_half(h, m, k, g_pre, g_post, wg, wu, wd):
    u = modulate(h, g_pre, m[3 * k], m[3 * k + 1])
    y = (jax.nn.silu(u @ wg) * (u @ wu)) @ wd
    return gated_residual(h, y, g_post, m[3 * k + 2], MACARON_WEIGHT)

def setup_inputs(seed: int = 0) -> dict:
    key = jax.random.key(seed)
    ks = iter(jax.random.split(key, 32))
    nrm = lambda shape, s: jax.random.normal(next(ks), shape, jnp.float32) * s
    L = DEPTH
    dt0 = jnp.exp(jax.random.uniform(next(ks), (L, 2, SSD_HEADS), jnp.float32, np.log(1e-3), np.log(1e-1)))
    return {
        'x': nrm((BATCH, SEQ, D_MODEL), 1.0),
        'c': nrm((BATCH, D_MODEL), 1.0),
        'ctx': nrm((BATCH, CTX_LEN, D_MODEL), 1.0),
        'c_ctx': nrm((D_MODEL,), 1.0),
        'w_mod': nrm((L, D_MODEL, N_MOD * D_MODEL), D_MODEL ** -0.5),
        'b_mod': nrm((L, N_MOD * D_MODEL), 0.02),
        'norm_pre': 1.0 + nrm((L, 3, D_MODEL), 0.05),
        'norm_post': 1.0 + nrm((L, 3, D_MODEL), 0.05),
        'ffn_w_gate': nrm((L, 2, D_MODEL, D_FF), D_MODEL ** -0.5),
        'ffn_w_up': nrm((L, 2, D_MODEL, D_FF), D_MODEL ** -0.5),
        'ffn_w_down': nrm((L, 2, D_FF, D_MODEL), D_FF ** -0.5),
        'w_in': nrm((L, D_MODEL, IN_WIDTH), D_MODEL ** -0.5),
        'ssd_conv_w': nrm((L, SSD_TAPS, XBC_WIDTH), SSD_TAPS ** -0.5),
        'ssd_conv_b': nrm((L, XBC_WIDTH), 0.02),
        'ssd_dt_bias': dt0 + jnp.log(-jnp.expm1(-dt0)),
        'ssd_a_log': jnp.log(jax.random.uniform(next(ks), (L, 2, SSD_HEADS), jnp.float32, 1.0, 16.0)),
        'ssd_d': 1.0 + nrm((L, SSD_HEADS), 0.1),
        'ssd_norm': 1.0 + nrm((L, SSD_WIDTH), 0.05),
        'conf_conv_w': nrm((L, CONF_TAPS, CONF_WIDTH), CONF_TAPS ** -0.5),
        'conf_conv_b': nrm((L, CONF_WIDTH), 0.02),
        'conf_ln_g': 1.0 + nrm((L, CONF_WIDTH), 0.05),
        'conf_ln_b': nrm((L, CONF_WIDTH), 0.02),
        'sc_conv_w': nrm((L, SC_TAPS, SC_WIDTH), SC_TAPS ** -0.5),
        'sc_conv_b': nrm((L, SC_WIDTH), 0.02),
        'w_out': nrm((L, D_INNER, D_MODEL), D_INNER ** -0.5),
    }

def reference(x, c, ctx, c_ctx, w_mod, b_mod, norm_pre, norm_post, ffn_w_gate, ffn_w_up, ffn_w_down,
              w_in, ssd_conv_w, ssd_conv_b, ssd_dt_bias, ssd_a_log, ssd_d, ssd_norm,
              conf_conv_w, conf_conv_b, conf_ln_g, conf_ln_b, sc_conv_w, sc_conv_b, w_out):
    bsz = x.shape[0]
    d = x.shape[-1]
    for i in range(DEPTH):
        last = i == DEPTH - 1
        mx = (jax.nn.silu(c) @ w_mod[i] + b_mod[i]).reshape(bsz, N_MOD, d).transpose(1, 0, 2)[:, :, None, :]
        mc = (jax.nn.silu(c_ctx) @ w_mod[i] + b_mod[i]).reshape(N_MOD, 1, 1, d)
        lp = {'ssd_conv_w': ssd_conv_w[i], 'ssd_conv_b': ssd_conv_b[i], 'dt_bias': ssd_dt_bias[i],
              'a_log': ssd_a_log[i], 'd_skip': ssd_d[i], 'ssd_norm': ssd_norm[i],
              'conf_w': conf_conv_w[i], 'conf_b': conf_conv_b[i], 'ln_g': conf_ln_g[i], 'ln_b': conf_ln_b[i],
              'sc_w': sc_conv_w[i], 'sc_b': sc_conv_b[i]}
        x = swiglu_half(x, mx, 0, norm_pre[i, 0], norm_post[i, 0], ffn_w_gate[i, 0], ffn_w_up[i, 0], ffn_w_down[i, 0])
        ctx = swiglu_half(ctx, mc, 0, norm_pre[i, 0], norm_post[i, 0], ffn_w_gate[i, 0], ffn_w_up[i, 0], ffn_w_down[i, 0])
        uc = modulate(ctx, norm_pre[i, 1], mc[3], mc[4])
        if last:
            xs, Bm, Cm, dt, A = ssd_inputs(uc @ w_in[i][:, :SSD_IN], lp['ssd_conv_w'], lp['ssd_conv_b'], lp['dt_bias'], lp['a_log'])
            s_f = ssd_final_state(xs, dt[:, :, 0], A[0], Bm)
            s_b = ssd_final_state(flip_seq(xs), flip_seq(dt[:, :, 1]), A[1], flip_seq(Bm))
        else:
            zero = jnp.zeros((bsz, SSD_HEADS, SSD_HEAD_DIM, SSD_STATE), jnp.float32)
            yc, s_f, s_b = mixer(uc @ w_in[i], zero, zero, dwconv, dwconv, lp)
            ctx = gated_residual(ctx, yc @ w_out[i], norm_post[i, 1], mc[5], 1.0)
            ctx = swiglu_half(ctx, mc, 2, norm_pre[i, 2], norm_post[i, 2], ffn_w_gate[i, 1], ffn_w_up[i, 1], ffn_w_down[i, 1])
        ux = modulate(x, norm_pre[i, 1], mx[3], mx[4])
        yx, _, _ = mixer(ux @ w_in[i], s_f, s_b, conv_along_rows, conv_along_cols, lp)
        x = gated_residual(x, yx @ w_out[i], norm_post[i, 1], mx[5], 1.0)
        x = swiglu_half(x, mx, 2, norm_pre[i, 2], norm_post[i, 2], ffn_w_gate[i, 1], ffn_w_up[i, 1], ffn_w_down[i, 1])
    return x


_drawn_inputs = setup_inputs


def setup_inputs(seed=0):
    import zlib

    import numpy as np

    out = dict(_drawn_inputs(seed))
    spreads = {}
    factors = {'ssd_conv_b': 7.398,
     'ssd_d': 6.263,
     'ssd_norm': 3.129,
     'conf_conv_b': 8.0,
     'conf_ln_g': 5.852,
     'conf_ln_b': 35.163,
     'sc_conv_b': 7.854,
     'ctx': 4.19}
    for name, (base, spread) in spreads.items():
        noise = np.random.default_rng([zlib.crc32(name.encode()), seed]).standard_normal(out[name].shape)
        drawn = base * np.exp(spread * noise) if base else spread * noise
        out[name] = jnp.asarray(drawn.astype(out[name].dtype))
    for name, factor in factors.items():
        out[name] = (out[name] * factor).astype(out[name].dtype)
    return out
```

```python
from contextlib import ExitStack

import concourse.bass as bass
from concourse import mybir

F32 = mybir.dt.float32
F32R = mybir.dt.float32r
BF16 = mybir.dt.bfloat16
ALU = mybir.AluOpType
ACT = mybir.ActivationFunctionType

P = 128
CTX = 256
TOK = 512
TT = TOK // P
GRID = 64
EPS = 1e-6
NEG = -1e30
FULL = (0, TOK)
LATENT = (CTX, TOK - CTX)


class Signal:

    def __init__(self, sem):
        self.sem, self.base, self.count = sem, 0, 0

    def inc(self, n=1):
        self.count += n
        return self.sem

    def at(self, k):
        return k + self.base if not isinstance(k, int) or k > 0 else self.base

    def landed(self, k):
        return 16 * k + self.base

    def own(self, but=0):
        return self.count - but


class Kern:

    def end_phase(self):
        for s in self.signals:
            s.base = s.count

    def loop(self, eng, first, end):
        return CountedLoop(self, eng, first, end)


class CountedLoop:

    def __init__(self, K, eng, first, end):
        self.K, self.trips, self.fori = K, end - first, eng.Fori(first, end)

    def __enter__(self):
        self.before = [s.count for s in self.K.signals]
        return self.fori.__enter__()

    def __exit__(self, *exc):
        for s, b in zip(self.K.signals, self.before):
            s.count += (s.count - b) * (self.trips - 1)
        return self.fori.__exit__(*exc)


def r32(ap):
    return ap.bitcast(F32)



def panel_src(w, k0, kn, c0):
    return w[k0 * P:(k0 + kn) * P, bass.ds(c0, 2 * P)].rearrange("(k p) n -> p k n", p=P)


def load_panel(K, sp, slot, src, kn):
    sp.dma_start(K.raw[:, slot, 0:kn, :], src).then_inc(K.raw_full[slot].inc(16), 16)


def weight_hi(K, act, panel_k, slot, half, kn, nth):
    act.wait_ge(K.raw_full[slot].sem, K.raw_full[slot].landed(panel_k))
    act.wait_ge(K.half_done.sem, K.half_done.at(nth - 1))
    ins = K.nc.scalar.activation(K.wh[:, half, 0:kn, :], K.raw[:, slot, 0:kn, half * P:half * P + P],
                                              ACT.Copy)
    ins.then_inc(K.hi_done.inc(), 1)


def weight_lo(K, dve, slot, half, kn, nth):
    dve.wait_ge(K.hi_done.sem, K.hi_done.at(nth + 1))
    ins = K.nc.vector.tensor_tensor(K.wl[:, half, 0:kn, :], K.raw[:, slot, 0:kn, half * P:half * P + P],
                                                 r32(K.wh[:, half, 0:kn, :]), ALU.subtract)
    ins.then_inc(K.lo_done.inc(), 1)


def product_half(K, pe, bank, half, kn, xh, xl, tok, first, last, nth):
    t0, tn = tok
    pe.wait_ge(K.lo_done.sem, K.lo_done.at(nth + 1))
    for k in range(kn):
        h, l = xh(k)[:, t0:t0 + tn], xl(k)[:, t0:t0 + tn]
        K.nc.tensor.matmul(bank[:, 0:tn], K.wh[:, half, k, :], h, start=first and k == 0, stop=False)
        K.nc.tensor.matmul(bank[:, 0:tn], K.wh[:, half, k, :], l, start=False, stop=False)
        ins = K.nc.tensor.matmul(bank[:, 0:tn], K.wl[:, half, k, :], h, start=False, stop=last and k == kn - 1)
    ins.then_inc(K.half_done.inc(), 1)



def load_mod(K, sp, w_mod, q, panel):
    sp.wait_ge(K.mod_lo.sem, K.mod_lo.at(2 * panel))
    sp.dma_start(K.raw_mod[:, :, :], panel_src(w_mod, 0, 8, P * q)).then_inc(K.mod_full.inc(16), 16)


def mod_hi(K, act, h, parity, panel):
    act.wait_ge(K.mod_full.sem, K.mod_full.landed(panel + 1))
    act.wait_ge(K.mod_mm.sem, K.mod_mm.at(h))
    ins = K.nc.scalar.activation(K.mh[:, :, :], K.raw_mod[:, :, parity * P:parity * P + P], ACT.Copy)
    ins.then_inc(K.mod_hi_done.inc(), 1)


def mod_lo(K, dve, h, parity):
    dve.wait_ge(K.mod_hi_done.sem, K.mod_hi_done.at(h + 1))
    ins = K.nc.vector.tensor_tensor(K.ml[:, :, :], K.raw_mod[:, :, parity * P:parity * P + P],
                                                r32(K.mh[:, :, :]), ALU.subtract)
    ins.then_inc(K.mod_lo.inc(), 1)


def mod_mm(K, pe, h, parity, panel, parts=None):
    pe.wait_ge(K.mod_lo.sem, K.mod_lo.at(h + 1))
    pe.wait_ge(K.mod_row.sem, K.mod_row.at(panel))
    wh, wl = parts or (K.mh, K.ml)
    for k in range(8):
        cond = K.cond[:, 4 * k:4 * k + P]
        for w in (wh, wl):
            ins = K.nc.tensor.matmul(K.bank[4][:, parity * P:parity * P + P], cond, w[:, k, :],
                                     start=k == 0 and w is wh, stop=k == 7 and w is wl)
    ins.then_inc(K.mod_mm.inc(), 1)


def mod_row(K, act, panel):
    act.wait_ge(K.mod_mm.sem, K.mod_mm.at(2 * panel + 2))
    act.wait_ge(K.mod_fold.sem, K.mod_fold.at(panel))
    K.nc.scalar.activation(K.rows[:, :], K.bank[4][0:4, 0:2 * P], ACT.Copy).then_inc(K.mod_row.inc(), 1)


def mod_fold(K, pe, panel):
    pe.wait_ge(K.mod_row.sem, K.mod_row.at(panel + 1))
    pe.wait_ge(K.mod_evac.sem, K.mod_evac.at(panel))
    for t in range(2):
        ins = K.nc.tensor.matmul(K.bank[7][:, 2 * t:2 * t + 2], K.rows[:, t * P:t * P + P], K.fold[:, :],
                                 start=True, stop=True)
    ins.then_inc(K.mod_fold.inc(), 1)


def mod_out(K, dve, layer, q, panel):
    dve.wait_ge(K.mod_fold.sem, K.mod_fold.at(panel + 1))
    bias = K.par[:, layer, 0, bass.ds(q, 2)].unsqueeze(2).to_broadcast([P, 2, 2])
    ins = K.nc.vector.tensor_tensor(K.mod[:, layer, bass.ds(q, 2), :],
                                                  K.bank[7][:, 0:4].rearrange("p (q s) -> p q s", s=2), bias, ALU.add)
    ins.then_inc(K.mod_evac.inc(), 1)



def stats_pe(K, pe, src, tok, j, n, nth):
    pe.wait_ge(K.sq_ready.sem, K.sq_ready.at(nth + 1))
    for t in range(tok[1] // P):
        ins = K.nc.tensor.matmul(K.bank[5][:, t:t + 1], src[:, t * P:t * P + P], K.ones[:, 0:1],
                                 start=j == 0 and t == 0, stop=j == n - 1, skip_group_check=True)
    ins.then_inc(K.stat_done.inc(), 1)


def rstd_dve(K, dve, tok, width, stats, nth):
    n = tok[1] // P
    dve.wait_ge(K.stat_done.sem, K.stat_done.at(stats))
    ins = K.nc.vector.tensor_scalar(K.ms[:, 0:n], K.bank[5][:, 0:n], 1.0 / width, EPS, ALU.mult, ALU.add)
    ins.then_inc(K.dve_step.inc(), 1)
    dve.wait_ge(K.dve_step.sem, K.dve_step.own())
    K.nc.vector.reciprocal(K.ms[:, 0:n], K.ms[:, 0:n]).then_inc(K.ms_ready.inc(), 1)
    dve.wait_ge(K.rstd_ready.sem, K.rstd_ready.at(nth))
    ins = K.nc.vector.tensor_tensor(
              K.diag[:, 0:n, :], K.ident[:, :].unsqueeze(1).to_broadcast([P, n, P]),
              K.rstd[:, 0:n].unsqueeze(2).to_broadcast([P, n, P]), ALU.mult)
    ins.then_inc(K.diag_ready.inc(), 1)


def rstd_act(K, act, tok, nth):
    n = tok[1] // P
    act.wait_ge(K.ms_ready.sem, K.ms_ready.at(nth))
    K.nc.scalar.activation(K.rstd[:, 0:n], K.ms[:, 0:n], ACT.Sqrt).then_inc(K.rstd_ready.inc(), 1)


def rstd_pe(K, pe, tok, nth):
    n = tok[1]
    pe.wait_ge(K.diag_ready.sem, K.diag_ready.at(nth))
    ins = K.nc.tensor.matmul(K.bank[6][:, 0:n], K.ones[:, :],
                                           K.diag[:, 0:n // P, :].rearrange("p t n -> p (t n)"), start=True, stop=True)
    ins.then_inc(K.rb_ready.inc(), 1)



def prenorm_act(K, act, tok, un, uh):
    t0, tn = tok
    for j in range(8):
        if j >= 2:
            act.wait_ge(K.stat_done.sem, K.stat_done.at(j - 1))
        ins = K.nc.scalar.activation(K.sq[:, j % 2, 0:tn], K.res[:, j, t0:t0 + tn], ACT.Square)
        ins.then_inc(K.sq_ready.inc(), 1)
    rstd_act(K, act, tok, 1)
    for j in range(8):
        act.wait_ge(K.un_ready.sem, K.un_ready.at(j + 1))
        K.nc.scalar.activation(uh[:, j, t0:t0 + tn], un[:, j % 2, 0:tn], ACT.Copy).then_inc(K.uh_ready.inc(), 1)


def prenorm_pe(K, pe, tok):
    for j in range(8):
        stats_pe(K, pe, K.sq[:, j % 2, :], tok, j, 8, j)
    rstd_pe(K, pe, tok, 1)
    pe.wait_ge(K.ul_ready.sem, K.ul_ready.at(8))


def prenorm_dve(K, dve, layer, which, tok, un_buf, uh, ul):
    t0, tn = tok
    nc = K.nc
    seqs = [s for s in range(2) if s * CTX >= t0]
    scale = K.mod[:, layer, 8 * (3 * which + 1):8 * (3 * which + 2), :]
    nc.vector.tensor_scalar(K.gain[:, :, :], scale, 1.0, None, ALU.add).then_inc(K.dve_step.inc(), 1)
    dve.wait_ge(K.dve_step.sem, K.dve_step.own())
    g = K.par[:, layer, 0, 72 + 8 * which:80 + 8 * which].unsqueeze(2).to_broadcast([P, 8, 2])
    nc.vector.tensor_tensor(K.gain[:, :, :], K.gain[:, :, :], g, ALU.mult).then_inc(K.dve_step.inc(), 1)
    dve.wait_ge(K.dve_step.sem, K.dve_step.own())
    rstd_dve(K, dve, tok, 1024, 8, 1)
    dve.wait_ge(K.rb_ready.sem, K.rb_ready.at(1))
    for j in range(8):
        un = un_buf[:, j % 2, :]
        ins = nc.vector.tensor_tensor(un[:, 0:tn], K.res[:, j, t0:t0 + tn], K.bank[6][:, 0:tn], ALU.mult)
        ins.then_inc(K.dve_step.inc(), 1)
        dve.wait_ge(K.dve_step.sem, K.dve_step.own())
        for s in seqs:
            a = s * CTX - t0
            ins = nc.vector.tensor_scalar(un[:, a:a + CTX], un[:, a:a + CTX], K.gain[:, j, s:s + 1],
                                          K.mod[:, layer, 24 * which + j, s:s + 1], ALU.mult, ALU.add)
            if s != seqs[-1]:
                ins.then_inc(K.dve_step.inc(), 1)
                dve.wait_ge(K.dve_step.sem, K.dve_step.own())
        ins.then_inc(K.un_ready.inc(), 1)
        dve.wait_ge(K.uh_ready.sem, K.uh_ready.at(j + 1))
        ins = nc.vector.tensor_tensor(ul[:, j, t0:t0 + tn], un[:, 0:tn], r32(uh[:, j, t0:t0 + tn]),
                                                    ALU.subtract)
        ins.then_inc(K.ul_ready.inc(), 1)



def post_gain_dve(K, dve, layer, which, weight):
    nc = K.nc
    gate = K.mod[:, layer, 8 * (3 * which + 2):8 * (3 * which + 3), :]
    nc.vector.tensor_scalar(K.pgain[:, :, :], gate, weight, None, ALU.mult).then_inc(K.dve_step.inc(), 1)
    dve.wait_ge(K.dve_step.sem, K.dve_step.own())
    g = K.par[:, layer, 0, 96 + 8 * which:104 + 8 * which].unsqueeze(2).to_broadcast([P, 8, 2])
    nc.vector.tensor_tensor(K.pgain[:, :, :], K.pgain[:, :, :], g, ALU.mult).then_inc(K.pgain_ready.inc(), 1)


def post_tile_act(K, act, bank, j, tok, y, stats):
    t0, tn = tok
    if stats + j >= 2:
        act.wait_ge(K.stat_done.sem, K.stat_done.at(stats + j - 1))
    K.nc.scalar.activation(K.sq[:, j % 2, 0:tn], bank[:, 0:tn], ACT.Square).then_inc(K.sq_ready.inc(), 1)
    for s in range(2):
        if s * CTX >= t0:
            a = s * CTX - t0
            ins = K.nc.scalar.activation(y[:, j, a:a + CTX], bank[:, a:a + CTX], ACT.Copy, scale=K.pgain[:, j, s:s + 1])
    ins.then_inc(K.y_ready.inc(), 1)


def residual_dve(K, dve, tok, y, stats, nth):
    t0, tn = tok
    rstd_dve(K, dve, tok, 1024, stats, nth)
    dve.wait_ge(K.y_ready.sem, K.y_ready.at(8))
    dve.wait_ge(K.rb_ready.sem, K.rb_ready.at(nth))
    for j in range(8):
        ins = K.nc.vector.tensor_tensor(y[:, j, 0:tn], y[:, j, 0:tn], K.bank[6][:, 0:tn], ALU.mult)
        ins.then_inc(K.dve_step.inc(), 1)
        dve.wait_ge(K.dve_step.sem, K.dve_step.own())
        ins = K.nc.vector.tensor_tensor(K.res[:, j, t0:t0 + tn], K.res[:, j, t0:t0 + tn], y[:, j, 0:tn], ALU.add)
        ins.then_inc(K.dve_step.inc(), 1)


class OutProduct:

    def __init__(self, K, w, parts, xh, xl, tok, xtok, y, halves, panels, stats, norms, mods=0,
                 mod_h=0, mod_layer=0, mod_q=0):
        self.K, self.w, self.parts, self.xh, self.xl, self.tok, self.xtok, self.y = K, w, parts, xh, xl, tok, xtok, y
        self.halves, self.panels, self.stats, self.norms = halves, panels, stats, norms
        self.mods, self.mod_h, self.mod_layer, self.mod_q = mods, mod_h, mod_layer, mod_q
        self.kstart = [sum(parts[:n]) for n in range(len(parts))]
        self.n_panels = 4 * len(parts)

    def src(self, p):
        part = p % len(self.parts)
        return panel_src(self.w, self.kstart[part], self.parts[part], 2 * P * (p // len(self.parts))), self.parts[part]

    def sp(self, sp, following):
        K = self.K
        for p in range(self.n_panels):
            if p < self.mods // 2:
                load_mod(K, sp, K.w_mod[self.mod_layer], self.mod_q + 2 * p, self.mod_h // 2 + p)
            if p + 2 < self.n_panels:
                src, kn = self.src(p + 2)
            elif p + 2 - self.n_panels < len(following):
                src, kn = following[p + 2 - self.n_panels]
            else:
                continue
            sp.wait_ge(K.lo_done.sem, K.lo_done.at(self.halves + 2 * p + 2))
            load_panel(K, sp, p % 2, src, kn)

    def pe(self, pe, bank_free):
        K, n = self.K, 0
        last = len(self.parts) - 1
        for p in range(self.n_panels):
            pair, part = p // len(self.parts), p % len(self.parts)
            k0 = self.kstart[part]
            for half in range(2):
                j = 2 * pair + half
                if part == 0 and pair >= 2:
                    pe.wait_ge(K.y_ready.sem, K.y_ready.at(j - 3))
                elif part == 0:
                    bank_free(pair)
                product_half(K, pe, K.bank[2 * (pair % 2) + half], half, self.parts[part], lambda k: self.xh(k0 + k),
                             lambda k: self.xl(k0 + k), self.xtok, part == 0, part == last, self.halves + n)
                h = self.mod_h + n
                if n < self.mods:
                    mod_mm(K, pe, h, half, h // 2)
                if half == 1 and 2 <= h and n <= self.mods:
                    mod_fold(K, pe, h // 2 - 1)
                if part == last and pair >= 1:
                    stats_pe(K, pe, K.sq[:, half, :], self.tok, j - 2, 8, self.stats + j - 2)
                n += 1
        if self.mods:
            mod_fold(K, pe, (self.mod_h + self.mods) // 2 - 1)
        for j in (6, 7):
            stats_pe(K, pe, K.sq[:, j % 2, :], self.tok, j, 8, self.stats + j)
        rstd_pe(K, pe, self.tok, self.norms)

    def act(self, act, skip=0):
        K = self.K
        n_parts = len(self.parts)
        for n in range(2 * self.n_panels + 2):
            p, half, h = n // 2, n % 2, self.mod_h + n
            if skip <= n < 2 * self.n_panels:
                weight_hi(K, act, self.panels + p // 2, p % 2, half, self.parts[p % n_parts], self.halves + n)
            if n == 0:
                act.wait_ge(K.pgain_ready.sem, K.pgain_ready.at(1))
            if 1 <= n <= self.mods:
                mod_hi(K, act, h - 1, 1 - half, (h - 1) // 2)
            if half == 1 and h - 1 >= 2 and n <= self.mods + 1 and self.mods:
                mod_row(K, act, (h - 1) // 2 - 1)
            if n >= 2 and (p - 1) % n_parts == n_parts - 1:
                j = 2 * ((p - 1) // n_parts) + half
                act.wait_ge(K.half_done.sem, K.half_done.at(self.halves + n - 1))
                post_tile_act(K, act, K.bank[2 * (j // 2 % 2) + j % 2], j, self.tok, self.y, self.stats)
        rstd_act(K, act, self.tok, self.norms)

    def dve(self, dve, skip=0):
        K = self.K
        for n in range(2 * self.n_panels + 1):
            p, half, h = n // 2, n % 2, self.mod_h + n
            if skip <= n < 2 * self.n_panels:
                weight_lo(K, dve, p % 2, half, self.parts[p % len(self.parts)], self.halves + n)
            if 1 <= n <= self.mods:
                mod_lo(K, dve, h - 1, 1 - half)
                if half == 1 and (h - 1) // 2 >= 2:
                    self.mod_out(dve, (h - 1) // 2 - 2)
        if self.mods:
            for back in (2, 1):
                self.mod_out(dve, (self.mod_h + self.mods) // 2 - back)
        residual_dve(K, dve, self.tok, self.y, self.stats + 8, self.norms)

    def mod_out(self, dve, panel):
        mod_out(self.K, dve, self.mod_layer, self.mod_q + 2 * panel - self.mod_h, panel)



def feed_forward(K, layer, which, tok, mod_layer, mod_q, mods_loop, mods_down, following):
    nc = K.nc
    ff = which // 2
    w_gate, w_up, w_down = K.w_gate[layer, ff], K.w_up[layer, ff], K.w_down[layer, ff]
    w_mod = K.w_mod[mod_layer] if mod_layer is not None else None
    t0, tn = tok
    FT = K.d_ff // P
    pairs = FT // 2
    with ExitStack() as mem:
        tag = f"{layer}{which}"
        if mods_loop or mods_down:
            K.raw_mod = mem.enter_context(nc.sbuf_tensor("raw_mod" + tag, [P, 8, 2 * P], F32))
            K.mh = mem.enter_context(nc.sbuf_tensor("mh" + tag, [P, 8, P], F32R))
            K.ml = mem.enter_context(nc.sbuf_tensor("ml" + tag, [P, 8, P], F32R))
        hh = mem.enter_context(nc.sbuf_tensor("hh" + tag, [P, FT, tn], F32R))
        hl = mem.enter_context(nc.sbuf_tensor("hl" + tag, [P, FT, tn], F32R))
        with ExitStack() as up_mem:
            uh = up_mem.enter_context(nc.sbuf_tensor("uh" + tag, [P, 8, TOK], F32R))
            ul = up_mem.enter_context(nc.sbuf_tensor("ul" + tag, [P, 8, TOK], F32R))
            sil = up_mem.enter_context(nc.sbuf_tensor("sil" + tag, [P, 2, TOK], F32))
            hf = up_mem.enter_context(nc.sbuf_tensor("hf" + tag, [P, 2, TOK], F32))
        y = mem.enter_context(nc.sbuf_tensor("y" + tag, [P, 8, TOK], F32))
        out = OutProduct(K, w_down, (8, 8, FT - 16), lambda k: hh[:, k, :], lambda k: hl[:, k, :], tok, (0, tn), y,
                         4 * pairs, pairs, 8, 2, mods_down, 4 * pairs if mods_loop else 0, mod_layer,
                         mod_q + (4 * pairs if mods_loop else 0))
        block = mem.enter_context(nc.Block(no_gpsimd_drain=True))

        @block.sync
        def _(sp):
            def next_panels(i, gate, up):
                sp.wait_ge(K.lo_done.sem, K.lo_done.at(4 * i + 2))
                load_panel(K, sp, 0, *gate)
                if mods_loop:
                    load_mod(K, sp, w_mod, mod_q + 4 * i + 2, 2 * i + 1)
                sp.wait_ge(K.lo_done.sem, K.lo_done.at(4 * i + 4))
                load_panel(K, sp, 1, *up)

            if mods_loop:
                load_mod(K, sp, w_mod, mod_q, 0)
            with K.loop(sp, 0, pairs - 1) as i:
                next_panels(i, (panel_src(w_gate, 0, 8, 2 * P * i + 2 * P), 8), (panel_src(w_up, 0, 8, 2 * P * i + 2 * P), 8))
                if mods_loop:
                    load_mod(K, sp, w_mod, mod_q + 4 * i + 4, 2 * i + 2)
            next_panels(pairs - 1, out.src(0), out.src(1))
            out.sp(sp, following)

        @block.tensor
        def _(pe):
            prenorm_pe(K, pe, tok)

            def trip(i, first):
                for half in range(4):
                    if half % 2 == 0:
                        pe.wait_ge((K.silu_done, K.prod_done)[half // 2].sem, (K.silu_done, K.prod_done)[half // 2].at(2 * i))
                    product_half(K, pe, K.bank[half], half % 2, 8, lambda k: uh[:, k, :], lambda k: ul[:, k, :], tok,
                                 True, True, 4 * i + half)
                    if mods_loop:
                        mod_mm(K, pe, 4 * i + half, half % 2, 2 * i + half // 2)
                        if half % 2 and not (first and half == 1):
                            mod_fold(K, pe, 2 * i - 1 + half // 2)
            trip(0, True)
            with K.loop(pe, 1, pairs) as i:
                trip(i, False)

            def bank_free(pair):
                pe.wait_ge((K.silu_done, K.prod_done)[pair].sem, (K.silu_done, K.prod_done)[pair].at(FT))
                pe.wait_ge(K.hl_done.sem, K.hl_done.at(FT))
            out.pe(pe, bank_free)

        @block.scalar
        def _(act):
            prenorm_act(K, act, tok, sil, uh)

            def hidden_hi(f, at):
                act.wait_ge(K.prod_done.sem, K.prod_done.at(f + 1))
                ins = nc.scalar.activation(hh[:, bass.ds(f, 1), :].rearrange("p a n -> p (a n)"), hf[:, at, 0:tn], ACT.Copy)
                ins.then_inc(K.hh_done.inc(), 1)

            def silu(i, j):
                act.wait_ge(K.half_done.sem, K.half_done.at(4 * i + j + 1))
                act.wait_ge(K.prod_done.sem, K.prod_done.at(2 * i + j - 1))
                nc.scalar.activation(sil[:, j, 0:tn], K.bank[j][:, 0:tn], ACT.Silu).then_inc(K.silu_done.inc(), 1)

            def mod(i, n):
                if mods_loop:
                    mod_hi(K, act, 4 * i + n, n % 2, 2 * i + n // 2)

            def trip(i, first, last):
                weight_hi(K, act, i, 0, 1, 8, 4 * i + 1)
                mod(i, 0)
                if not first:
                    if mods_loop:
                        mod_row(K, act, 2 * i - 1)
                    hidden_hi(2 * i - 1, 1)
                weight_hi(K, act, i, 1, 0, 8, 4 * i + 2)
                mod(i, 1)
                silu(i, 0)
                weight_hi(K, act, i, 1, 1, 8, 4 * i + 3)
                mod(i, 2)
                if mods_loop:
                    mod_row(K, act, 2 * i)
                silu(i, 1)
                if not last:
                    weight_hi(K, act, i + 1, 0, 0, 8, 4 * i + 4)
                else:
                    weight_hi(K, act, pairs, 0, 0, out.parts[0], 4 * pairs)
                mod(i, 3)
                hidden_hi(2 * i, 0)

            weight_hi(K, act, 0, 0, 0, 8, 0)
            trip(0, True, False)
            with K.loop(act, 1, pairs - 1) as i:
                trip(i, False, False)
            trip(pairs - 1, False, True)
            weight_hi(K, act, pairs, 0, 1, out.parts[0], 4 * pairs + 1)
            hidden_hi(FT - 1, 1)
            out.act(act, skip=2)

        @block.vector
        def _(dve):
            prenorm_dve(K, dve, layer, which, tok, sil, uh, ul)

            def product(i, j):
                dve.wait_ge(K.silu_done.sem, K.silu_done.at(2 * i + j + 1))
                dve.wait_ge(K.half_done.sem, K.half_done.at(4 * i + 2 + j + 1))
                ins = nc.vector.tensor_tensor(hf[:, j, 0:tn], sil[:, j, 0:tn], K.bank[2 + j][:, 0:tn], ALU.mult)
                ins.then_inc(K.prod_done.inc(), 1)

            def hidden_lo(f, at):
                dve.wait_ge(K.hh_done.sem, K.hh_done.at(f + 1))
                h = bass.ds(f, 1)
                ins = nc.vector.tensor_tensor(hl[:, h, :].rearrange("p a n -> p (a n)"), hf[:, at, 0:tn],
                                                           r32(hh[:, h, :]).rearrange("p a n -> p (a n)"), ALU.subtract)
                ins.then_inc(K.hl_done.inc(), 1)

            def mod(i, n, first):
                if mods_loop:
                    mod_lo(K, dve, 4 * i + n, n % 2)
                    if n % 2 == 0 and not first:
                        mod_out(K, dve, mod_layer, mod_q + 2 * (2 * i - 2 + n // 2), 2 * i - 2 + n // 2)

            def trip(i, first, last):
                weight_lo(K, dve, 0, 1, 8, 4 * i + 1)
                mod(i, 0, first)
                if not first:
                    hidden_lo(2 * i - 1, 1)
                weight_lo(K, dve, 1, 0, 8, 4 * i + 2)
                mod(i, 1, first)
                weight_lo(K, dve, 1, 1, 8, 4 * i + 3)
                mod(i, 2, first)
                if not last:
                    weight_lo(K, dve, 0, 0, 8, 4 * i + 4)
                else:
                    weight_lo(K, dve, 0, 0, out.parts[0], 4 * pairs)
                mod(i, 3, first)
                product(i, 0)
                hidden_lo(2 * i, 0)
                product(i, 1)

            weight_lo(K, dve, 0, 0, 8, 0)
            trip(0, True, False)
            with K.loop(dve, 1, pairs - 1) as i:
                trip(i, False, False)
            trip(pairs - 1, False, True)
            weight_lo(K, dve, 0, 1, out.parts[0], 4 * pairs + 1)
            hidden_lo(FT - 1, 1)
            post_gain_dve(K, dve, layer, which, 0.5)
            out.dve(dve, skip=2)
    K.end_phase()



XBC_T, Z_T, GRP_T = 12, 8, 4
DT0 = XBC_T * P
Z0 = DT0 + 32
CONF0 = Z0 + Z_T * P
SC0 = CONF0 + 2 * GRP_T * P
CONF_HALO, SC_TAPS, XBC_TAPS, CONF_TAPS = 15, 3, 5, 31
ROWS = (TOK - CTX) // GRID

HALVES = [(kind, 2 * pair + half) for kind, pair in
          (("gate", 0), ("value", 0), ("gate", 1), ("value", 1), ("z", 0), ("z", 1), ("z", 2), ("z", 3),
           ("sc_c", 0), ("sc_h", 0), ("sc_b", 0), ("sc_c", 1), ("sc_h", 1), ("sc_b", 1),
           ("xbc", 0), ("xbc", 1), ("xbc", 2), ("xbc", 3), ("xbc", 4), ("xbc", 5)) for half in range(2)]
COLUMN = {"value": CONF0, "gate": CONF0 + GRP_T * P, "z": Z0, "sc_b": SC0, "sc_c": SC0 + GRP_T * P,
          "sc_h": SC0 + 2 * GRP_T * P, "xbc": 0}
READER = {"gate": "act", "z": "act", "sc_c": "act", "xbc": "act", "value": "dve", "sc_h": "dve", "sc_b": "dve"}
NH = len(HALVES)
CONV_FROM, CONV_STEP = 5, 6
LN_MEAN, LN_CENTRE, LN_SQ, LN_RSTD, LN_APPLY = 28, 30, 31, 36, 38


def reads(n, who):
    return sum(READER[kind] == who for kind, _ in HALVES[:n + 1])


def w_in_panel(K, layer, p):
    kind, tile = HALVES[2 * p]
    return panel_src(K.w_in[layer], 0, 8, COLUMN[kind] + P * tile), 8


def mixer_first(K, layer):
    return [w_in_panel(K, layer, 0), w_in_panel(K, layer, 1)]


def project(K, M, layer, last, following):
    nc = K.nc
    part = LATENT if last else FULL
    p0, pn = part
    seqs = (1,) if last else (0, 1)
    with ExitStack() as mem:
        def sb(name, shape, dt=F32):
            return mem.enter_context(nc.sbuf_tensor(f"{name}_{layer}", shape, dt))
        uh, ul = sb("mix_uh", [P, 8, TOK], F32R), sb("mix_ul", [P, 8, TOK], F32R)
        cpad = sb("conf_pad_ctx", [P, GRP_T, CTX + 2 * CONF_HALO])
        xpad = sb("conf_pad_x", [P, GRP_T, ROWS, GRID + 2 * CONF_HALO])
        conf = sb("conf_out", [P, GRP_T, TOK])
        spc = sb("sc_pad_ctx", [P, 2, CTX + 2])
        spx = sb("sc_pad_x", [P, 2, TOK - CTX + 2 * GRID])
        gate = sb("gate", [P, 2, TOK])
        bpad = sb("xbc_pad", [P, 2, 2, CTX + 4])
        acc = sb("conv_acc", [P, 2, TOK])
        wdt = sb("wdt", [P, 8, 32])
        wdh, wdl = sb("wdh", [P, 8, 32], F32R), sb("wdl", [P, 8, 32], F32R)
        block = mem.enter_context(nc.Block(no_gpsimd_drain=True))
        par = K.par[:, layer]

        @block.sync
        def _(sp):
            src = K.w_in[layer][:, DT0:DT0 + 32].rearrange("(k p) n -> p k n", p=P)
            sp.dma_start(wdt[:, :, :], src).then_inc(K.dtw_in.inc(16), 16)
            for p in range(NH // 2):
                panel = w_in_panel(K, layer, p + 2) if p + 2 < NH // 2 else following[p + 2 - NH // 2]
                sp.wait_ge(K.lo_done.sem, K.lo_done.at(2 * p + 2))
                load_panel(K, sp, p % 2, *panel)

        @block.gpsimd
        def _(pool):
            for pad in (cpad, xpad, spc, spx, bpad):
                nc.gpsimd.memset(pad[:], 0.0).then_inc(K.pads_zero.inc(), 1)

        @block.tensor
        def _(pe):
            prenorm_pe(K, pe, FULL)
            for n, (kind, tile) in enumerate(HALVES):
                if n >= 4:
                    who = READER[HALVES[n - 4][0]]
                    read = K.act_read if who == "act" else K.dve_read
                    pe.wait_ge(read.sem, read.at(reads(n - 4, who)))
                product_half(K, pe, K.bank[n % 4], n % 2, 8, lambda k: uh[:, k, :], lambda k: ul[:, k, :],
                             FULL if kind == "xbc" else part, True, True, n)
                if n == 20:
                    pe.wait_ge(K.dtw_ready.sem, K.dtw_ready.at(1))
                    for t in range(TT):
                        for k in range(8):
                            tok = slice(t * P, t * P + P)
                            for x, w in ((uh, wdh), (ul, wdh), (uh, wdl)):
                                ins = nc.tensor.matmul(K.bank[4][:, 32 * t:32 * t + 32], x[:, k, tok], w[:, k, :],
                                                       start=k == 0 and w is wdh and x is uh, stop=k == 7 and w is wdl)
                    ins.then_inc(K.dt_raw.inc(), 1)
                if n == LN_MEAN:
                    pe.wait_ge(K.conv_done.sem, K.conv_done.at(GRP_T * len(seqs)))
                    for t in range(GRP_T):
                        ins = nc.tensor.matmul(K.bank[7][:, 0:pn], K.ones[:, :], conf[:, t, p0:p0 + pn], start=t == 0, stop=t == GRP_T - 1)
                    ins.then_inc(K.mean_ready.inc(), 1)
                if n in (LN_SQ, LN_SQ + 2):
                    for t in (0, 1) if n == LN_SQ else (2, 3):
                        stats_pe(K, pe, K.sq[:, t % 2, :], part, t, GRP_T, 8 + t)
                if n == LN_RSTD:
                    rstd_pe(K, pe, part, 2)

        @block.scalar
        def _(act):
            prenorm_act(K, act, FULL, acc, uh)
            act.wait_ge(K.pads_zero.sem, K.pads_zero.at(5))
            for n in range(NH + 2):
                if n < NH:
                    weight_hi(K, act, n // 4, n // 2 % 2, n % 2, 8, n)
                if n == 2:
                    act.wait_ge(K.dtw_in.sem, K.dtw_in.at(16))
                    nc.scalar.activation(wdh[:, :, :], wdt[:, :, :], ACT.Copy).then_inc(K.dtw_hi.inc(), 1)
                if n == LN_SQ or n == LN_SQ + 1:
                    for t in (0, 1) if n == LN_SQ else (2, 3):
                        act.wait_ge(K.cent_ready.sem, K.cent_ready.at(t + 1))
                        act.wait_ge(K.stat_done.sem, K.stat_done.at(8 + t - 1))
                        ins = nc.scalar.activation(K.sq[:, t % 2, 0:pn], conf[:, t, p0:p0 + pn], ACT.Square)
                        ins.then_inc(K.sq_ready.inc(), 1)
                if n == LN_RSTD:
                    rstd_act(K, act, part, 2)
                if n == LN_APPLY:
                    for t in range(GRP_T):
                        act.wait_ge(K.ln_ready.sem, K.ln_ready.at(t + 1))
                        ins = nc.scalar.activation(conf[:, t, p0:p0 + pn], conf[:, t, p0:p0 + pn], ACT.Silu,
                                                                        scale=par[:, 2, 76 + t:77 + t], bias=par[:, 2, 80 + t:81 + t])
                        ins.then_inc(K.act_step.inc(), 1)
                        act.wait_ge(K.act_step.sem, K.act_step.own())
                        ins = nc.scalar.activation(M.yc_h[:, t, p0:p0 + pn], conf[:, t, p0:p0 + pn], ACT.Copy)
                        ins.then_inc(K.ln_hi.inc(), 1)
                if n < 2:
                    continue
                kind, tile = HALVES[n - 2]
                bank = K.bank[(n - 2) % 4]
                if READER[kind] == "act":
                    act.wait_ge(K.half_done.sem, K.half_done.at(n - 1))
                if kind == "gate":
                    if n >= 6:
                        act.wait_ge(K.dve_read.sem, K.dve_read.at(tile - 1))
                    ins = nc.scalar.activation(gate[:, tile % 2, 0:pn], bank[:, 0:pn], ACT.Sigmoid)
                    ins.then_inc(K.act_read.inc(), 1)
                elif kind == "sc_c":
                    act.wait_ge(K.dve_read.sem, K.dve_read.at(reads(n - 6, "dve")))
                    ins = nc.scalar.activation(gate[:, tile % 2, 0:pn], bank[:, 0:pn], ACT.Copy)
                    ins.then_inc(K.act_read.inc(), 1)
                elif kind == "z":
                    ins = nc.scalar.activation(M.z[:, tile, p0:p0 + pn], bank[:, 0:pn], ACT.Silu)
                    ins.then_inc(K.act_read.inc(), 1)
                elif kind == "sc_b":
                    act.wait_ge(K.dve_read.sem, K.dve_read.at(reads(n - 2, "dve")))
                    ins = nc.scalar.activation(M.ys_h[:, tile, p0:p0 + pn], acc[:, tile % 2, 0:pn], ACT.Copy)
                    ins.then_inc(K.ys_hi.inc(), 1)
                elif kind == "xbc":
                    if tile >= 2:
                        act.wait_ge(K.xbc_conv.sem, K.xbc_conv.at(tile - 1))
                    ins = nc.scalar.activation(bpad[:, tile % 2, :, 2:2 + CTX],
                                                             bank[:, :].rearrange("p (s n) -> p s n", s=2), ACT.Copy)
                    ins.then_inc(K.act_read.inc(), 1)
                    if tile >= 1:
                        act.wait_ge(K.xbc_conv.sem, K.xbc_conv.at(tile))
                        ins = nc.scalar.activation(M.xbc[:, tile - 1, :], acc[:, (tile - 1) % 2, :], ACT.Silu)
                        ins.then_inc(K.xbc_out.inc(), 1)
            act.wait_ge(K.xbc_conv.sem, K.xbc_conv.at(XBC_T))
            ins = nc.scalar.activation(M.xbc[:, XBC_T - 1, :], acc[:, (XBC_T - 1) % 2, :], ACT.Silu)
            ins.then_inc(K.xbc_out.inc(), 1)

        @block.vector
        def _(dve):
            def taps(tensors, weights, bias, steps, signal=None):
                for k in steps:
                    for i, (out, src) in enumerate(tensors):
                        if k == 0:
                            ins = nc.vector.tensor_scalar(out, src(k), weights(k), bias, ALU.mult, ALU.add)
                        else:
                            dve.wait_ge(K.dve_step.sem, K.dve_step.own(len(tensors) - 1 - (i if signal else 0)))
                            ins = nc.vector.scalar_tensor_tensor(out, src(k), weights(k), out, ALU.mult, ALU.add)
                        ins.then_inc((signal or K.dve_step).inc(), 1)

            def conf_tap(t, k):
                ctx = (conf[:, t, 0:CTX], lambda k: cpad[:, t, k:k + CTX])
                lat = (conf[:, t, CTX:TOK].rearrange("p (r c) -> p r c", c=GRID), lambda k: xpad[:, t, :, k:k + GRID])
                taps([lat] if last else [ctx, lat], lambda k: par[:, 1, 4 * k + t:4 * k + t + 1], par[:, 2, 72 + t:73 + t], [k],
                     K.conv_done if k == CONF_TAPS - 1 else None)

            prenorm_dve(K, dve, layer, 1, FULL, acc, uh, ul)
            for n in range(NH + 2):
                if n < NH:
                    weight_lo(K, dve, n // 2 % 2, n % 2, 8, n)
                if n == 2:
                    dve.wait_ge(K.dtw_hi.sem, K.dtw_hi.at(1))
                    ins = nc.vector.tensor_tensor(wdl[:, :, :], wdt[:, :, :], r32(wdh[:, :, :]), ALU.subtract)
                    ins.then_inc(K.dtw_ready.inc(), 1)
                    dve.wait_ge(K.pads_zero.sem, K.pads_zero.at(5))
                if n >= 2:
                    kind, tile = HALVES[n - 2]
                    bank = K.bank[(n - 2) % 4]
                    if READER[kind] == "dve":
                        dve.wait_ge(K.half_done.sem, K.half_done.at(n - 1))
                    if kind in ("value", "sc_h"):
                        dve.wait_ge(K.act_read.sem, K.act_read.at(reads(n - 4, "act")))
                        for s in seqs:
                            a = s * CTX - p0
                            src, g = bank[:, a:a + CTX], gate[:, tile % 2, a:a + CTX]
                            if kind == "value" and s == 0:
                                out = cpad[:, tile, CONF_HALO:CONF_HALO + CTX]
                            elif kind == "value":
                                out = xpad[:, tile, :, CONF_HALO:CONF_HALO + GRID]
                                src, g = (v.rearrange("p (r c) -> p r c", c=GRID) for v in (src, g))
                            elif s == 0:
                                out = spc[:, tile % 2, 1:1 + CTX]
                            else:
                                out = spx[:, tile % 2, GRID:GRID + CTX]
                            ins = nc.vector.tensor_tensor(out, src, g, ALU.mult)
                            if s == 0:
                                ins.then_inc(K.dve_step.inc(), 1)
                                dve.wait_ge(K.dve_step.sem, K.dve_step.own())
                        ins.then_inc(K.dve_read.inc(), 1)
                    elif kind == "sc_b":
                        j, buf = tile, tile % 2
                        dve.wait_ge(K.dve_read.sem, K.dve_read.own())
                        ctx = (acc[:, buf, 0:CTX], lambda k: spc[:, buf, k:k + CTX])
                        lat = (acc[:, buf, CTX - p0:TOK - p0], lambda k: spx[:, buf, k * GRID:k * GRID + CTX])
                        taps([lat] if last else [ctx, lat], lambda k: par[:, 2, 84 + 4 * k + j:85 + 4 * k + j],
                             par[:, 2, 96 + j:97 + j], range(SC_TAPS))
                        dve.wait_ge(K.dve_step.sem, K.dve_step.own())
                        ins = nc.vector.tensor_tensor(acc[:, buf, 0:pn], acc[:, buf, 0:pn], bank[:, 0:pn], ALU.mult)
                        ins.then_inc(K.dve_read.inc(), 1)
                if n >= 3 and HALVES[n - 3][0] == "sc_b":
                    t = HALVES[n - 3][1]
                    dve.wait_ge(K.ys_hi.sem, K.ys_hi.at(t + 1))
                    ins = nc.vector.tensor_tensor(M.ys_l[:, t, p0:p0 + pn], acc[:, t % 2, 0:pn],
                                                             r32(M.ys_h[:, t, p0:p0 + pn]), ALU.subtract)
                    ins.then_inc(K.ys_lo.inc(), 1)
                if n == 23:
                    dve.wait_ge(K.dt_raw.sem, K.dt_raw.at(1))
                    bias = K.dtb[:, layer, :].unsqueeze(1).to_broadcast([P, TT, 32])
                    ins = nc.vector.tensor_tensor(M.dt[:, :, :], K.bank[4][:, 0:P].rearrange("p (t h) -> p t h", t=TT), bias, ALU.add)
                    ins.then_inc(K.dt_out.inc(), 1)
                for i in range(CONV_STEP * (n - CONV_FROM), min(CONV_STEP * (n - CONV_FROM + 1), GRP_T * CONF_TAPS)):
                    if i >= 0:
                        t, k = i // CONF_TAPS, i % CONF_TAPS
                        if k == 0:
                            dve.wait_ge(K.dve_read.sem, K.dve_read.at(t + 1))
                        conf_tap(t, k)
                if n == LN_CENTRE:
                    dve.wait_ge(K.mean_ready.sem, K.mean_ready.at(1))
                    for t in range(GRP_T):
                        ins = nc.vector.scalar_tensor_tensor(conf[:, t, p0:p0 + pn], K.bank[7][:, 0:pn], -1.0 / (GRP_T * P),
                                                                             conf[:, t, p0:p0 + pn], ALU.mult, ALU.add)
                        ins.then_inc(K.cent_ready.inc(), 1)
                if n == LN_RSTD:
                    rstd_dve(K, dve, part, GRP_T * P, 8 + GRP_T, 2)
                if n == LN_APPLY:
                    dve.wait_ge(K.rb_ready.sem, K.rb_ready.at(2))
                    for t in range(GRP_T):
                        ins = nc.vector.tensor_tensor(conf[:, t, p0:p0 + pn], conf[:, t, p0:p0 + pn], K.bank[6][:, 0:pn], ALU.mult)
                        ins.then_inc(K.ln_ready.inc(), 1)
                if n == LN_APPLY + 1:
                    for t in range(GRP_T):
                        dve.wait_ge(K.ln_hi.sem, K.ln_hi.at(t + 1))
                        ins = nc.vector.tensor_tensor(M.yc_l[:, t, p0:p0 + pn], conf[:, t, p0:p0 + pn],
                                                                 r32(M.yc_h[:, t, p0:p0 + pn]), ALU.subtract)
                        ins.then_inc(K.yc_lo.inc(), 1)
                if n >= 2 and HALVES[n - 2][0] == "xbc":
                    t = HALVES[n - 2][1]
                    dve.wait_ge(K.act_read.sem, K.act_read.at(reads(n - 2, "act")))
                    if t >= 2:
                        dve.wait_ge(K.xbc_out.sem, K.xbc_out.at(t - 1))
                    else:
                        dve.wait_ge(K.ys_lo.sem, K.ys_lo.own())
                    view = acc[:, t % 2, :].rearrange("p (s n) -> p s n", s=2)
                    taps([(view, lambda k: bpad[:, t % 2, :, k:k + CTX])],
                         lambda k: par[:, 2, 12 * k + t:12 * k + t + 1], par[:, 2, 60 + t:61 + t], range(XBC_TAPS - 1))
                    k = XBC_TAPS - 1
                    dve.wait_ge(K.dve_step.sem, K.dve_step.own())
                    ins = nc.vector.scalar_tensor_tensor(view, bpad[:, t % 2, :, k:k + CTX], par[:, 2, 12 * k + t:12 * k + t + 1],
                                                                       view, ALU.mult, ALU.add)
                    ins.then_inc(K.xbc_conv.inc(), 1)
    K.end_phase()



HEADS, HD, GH = 16, 64, 8
CHUNKS = 2


class ScanPlan:

    def __init__(self, last):
        self.seqs = (0, 1)
        self.with_y = {0: not last, 1: True}
        self.states = {0: [(0, 0), (1, 0), (1, 1), (0, 1)], 1: [(0, 0), (1, 1)]}

    @staticmethod
    def prev(seq, c, d):
        first = c == 0 if d == 0 else c == 1
        if first:
            return None if seq == 0 else "init"
        return "mid"


def scan(K, M, layer, last):
    nc = K.nc
    plan = ScanPlan(last)
    with ExitStack() as mem:
        def sb(name, shape, dt=F32):
            return mem.enter_context(nc.sbuf_tensor(f"{name}_{layer}", shape, dt))
        small = lambda name: sb(name, [P, TT, 2, HEADS])
        t_abs, t_e, t_u, t_ln, t_d, t_z = (small(n) for n in ("dt_abs", "dt_e", "dt_u", "dt_ln", "dt_d", "dt_z"))
        dt, a = small("dt_f"), small("dt_a")
        ea = sb("exp_alog", [P, 32])
        cum = sb("cum", [P, 2, TT, HEADS])
        neg = sb("neg_cum", [P, 2, TT, HEADS])
        tot = sb("tot", [P, TT, 2, HEADS])
        dec = sb("dec", [P, TT, 2, HEADS])
        ecum, etot = sb("exp_cum", [P, 2, TT, HEADS]), sb("exp_tot", [P, TT, 2, HEADS])
        xd = sb("xd", [P, CHUNKS, 2, HEADS, HD])
        xw = sb("xw", [P, HEADS, HD])
        btm = sb("b_tm", [P, CHUNKS, 2 * P])
        init = sb("state_init", [P, 2, HEADS, HD])
        mid = sb("state_mid", [P, 2, HEADS, HD])
        cbt = sb("cb", [P, 2, P])
        e = sb("decay", [P, 2, 4, P])
        m = sb("weights", [P, 2, 4, P])
        ytm = sb("y_tm", [P, HEADS, HD])
        tmp = sb("off", [P, 2, GH, HD])
        gt = sb("gated", [P, 4, P])
        block = mem.enter_context(nc.Block(no_gpsimd_drain=True))
        bh = lambda ap, n: ap.unsqueeze(2).to_broadcast([P, n, HD])
        fm = lambda tile, t: M.xbc[:, tile, t * P:t * P + P]
        state = {"init": init, "mid": mid}

        @block.tensor
        def _(pe):
            pe.wait_ge(K.dt_ready.sem, K.dt_ready.at(1))
            for d in range(2):
                nc.tensor.matmul(K.bank[4][:, 64 * d:64 * d + 64], K.tri[:, d, :], a[:, :, d, :], start=True, stop=True)
            ins = nc.tensor.matmul(K.bank[4][:, P:2 * P], K.ones[:, :], a[:, :, :, :].rearrange("p t d h -> p (t d h)"),
                                                  start=True, stop=True)
            ins.then_inc(K.cum_ready.inc(), 1)
            turns = states = units = offs = gs = 0
            for seq in plan.seqs:
                for c in range(CHUNKS):
                    t = 2 * seq + c
                    pe.wait_ge(K.ytm_ready.sem, K.ytm_ready.at(gs))
                    pe.wait_ge(K.xd_ready.sem, K.xd_ready.at(4 * turns))
                    for j in range(8):
                        ins = nc.tensor.transpose(K.bank[j // 4][:, j % 4 * P:j % 4 * P + P], fm(j, t), K.ident[:, :])
                    ins.then_inc(K.xs_turned.inc(), 1)
                    pe.wait_ge(K.cb_ready.sem, K.cb_ready.at(units // 8))
                    pe.wait_ge(K.b_ready.sem, K.b_ready.at(turns))
                    for g in range(2):
                        ins = nc.tensor.transpose(K.bank[5][:, g * P:g * P + P], fm(8 + g, t), K.ident[:, :])
                    ins.then_inc(K.b_turned.inc(), 1)
                    turns += 1
                pe.wait_ge(K.b_ready.sem, K.b_ready.at(turns))
                pe.wait_ge(K.e_ready.sem, K.e_ready.at(units))
                for c, d in plan.states[seq]:
                    pe.wait_ge(K.xw_ready.sem, K.xw_ready.at(states + 1))
                    pe.wait_ge(K.st_ready.sem, K.st_ready.at(states))
                    for g in range(2):
                        ins = nc.tensor.matmul(K.bank[2 + g][:, :], btm[:, c, g * P:g * P + P],
                                               xw[:, GH * g:GH * g + GH, :].rearrange("p h n -> p (h n)"), start=True, stop=True)
                    ins.then_inc(K.state_mm.inc(), 1)
                    states += 1
                pe.wait_ge(K.st_ready.sem, K.st_ready.at(states))
                if not plan.with_y[seq]:
                    continue
                pe.wait_ge(K.xd_ready.sem, K.xd_ready.at(4 * turns))
                for c in range(CHUNKS):
                    t = 2 * seq + c
                    pe.wait_ge(K.cb_ready.sem, K.cb_ready.at(units // 8))
                    for g in range(2):
                        ins = nc.tensor.matmul(K.bank[5][:, g * P:g * P + P], fm(8 + g, t), fm(10 + g, t), start=True, stop=True)
                    ins.then_inc(K.cb_mm.inc(), 1)

                    def decay(u):
                        g, d, h = u // 4, u % 2, 4 * (u // 2)
                        bank = K.bank[2 + u % 2]
                        pe.wait_ge(K.e_ready.sem, K.e_ready.at(units + u - 1))
                        nc.tensor.matmul(bank[:, :], K.identb[:, :], K.mask[:, d, :].unsqueeze(1).to_broadcast([P, 4, P]),
                                         start=True, stop=False, skip_group_check=True)
                        for i in range(4):
                            ins = nc.tensor.matmul(bank[:, i * P:i * P + P], a[:, t, d, h + i:h + i + 1].to_broadcast([P, P]),
                                                   K.tri[:, d, :], start=False, stop=True, skip_group_check=True)
                        ins.then_inc(K.diff_ready.inc(), 1)

                    def off(g):
                        nonlocal offs
                        for d in range(2):
                            prev = plan.prev(seq, c, d)
                            if prev:
                                pe.wait_ge(K.off_used.sem, K.off_used.at(offs - 1))
                                ins = nc.tensor.matmul(
                                          K.bank[6 + offs % 2][:, :], fm(10 + g, t),
                                          state[prev][:, d, GH * g:GH * g + GH, :].rearrange("p h n -> p (h n)"), start=True, stop=True)
                                ins.then_inc(K.off_mm.inc(), 1)
                                offs += 1

                    def y_turn(g):
                        pe.wait_ge(K.ytm_ready.sem, K.ytm_ready.at(gs + g + 1))
                        pe.wait_ge(K.g_ready.sem, K.g_ready.at(gs + g))
                        for i in range(4):
                            h = GH * g + 2 * i
                            ins = nc.tensor.transpose(K.bank[4][:, i * P:i * P + P],
                                                      ytm[:, h:h + 2, :].rearrange("p h n -> p (h n)"), K.ident[:, :])
                        ins.then_inc(K.y_turned.inc(), 1)

                    decay(0)
                    decay(1)
                    off(0)
                    for u in range(8):
                        g, d = u // 4, u % 2
                        pe.wait_ge(K.m_ready.sem, K.m_ready.at(units + u + 1))
                        if u % 4 == 0:
                            pe.wait_ge(K.ytm_ready.sem, K.ytm_ready.at(gs + g - 1))
                        for i in range(4):
                            h = 4 * (u // 2) + i
                            ins = nc.tensor.matmul(K.bank[g][:, (h - GH * g) * HD:(h - GH * g + 1) * HD], m[:, u % 2, i, :],
                                                   xd[:, c, d, h, :], start=u % 4 == 0 and i == 0, stop=u % 4 >= 2,
                                                   skip_group_check=True)
                        ins.then_inc(K.y_mm.inc(), 1)
                        if u + 2 < 8:
                            decay(u + 2)
                        if u == 3:
                            off(1)
                        if u == 6:
                            y_turn(0)
                    y_turn(1)
                    units += 8
                    gs += 2

        @block.scalar
        def _(act):
            flat = lambda ap: ap.rearrange("p t d h -> p (t d h)")
            act.wait_ge(K.dt_abs.sem, K.dt_abs.at(1))
            nc.scalar.activation(flat(t_e[:]), flat(t_abs[:]), ACT.Exp, scale=-1.0).then_inc(K.dt_exp.inc(), 1)
            nc.scalar.activation(ea[:, :], K.alog[:, layer, :], ACT.Exp).then_inc(K.a_exp.inc(), 1)
            act.wait_ge(K.dt_u.sem, K.dt_u.at(1))
            nc.scalar.activation(flat(t_ln[:]), flat(t_u[:]), ACT.Ln).then_inc(K.dt_ln.inc(), 1)
            act.wait_ge(K.cum_read.sem, K.cum_read.at(1))
            nc.scalar.activation(flat(dec[:]), flat(dec[:]), ACT.Exp)
            nc.scalar.activation(flat(ecum[:]), flat(cum[:]), ACT.Exp)
            nc.scalar.activation(flat(etot[:]), flat(tot[:]), ACT.Exp).then_inc(K.decay_ready.inc(), 1)
            turns = units = 0
            for seq in plan.seqs:
                for c in range(CHUNKS):
                    act.wait_ge(K.b_turned.sem, K.b_turned.at(turns + 1))
                    nc.scalar.activation(btm[:, c, :], K.bank[5][:, 0:2 * P], ACT.Copy).then_inc(K.b_ready.inc(), 1)
                    turns += 1
                if not plan.with_y[seq]:
                    continue
                for c in range(CHUNKS):
                    t = 2 * seq + c
                    act.wait_ge(K.cb_mm.sem, K.cb_mm.at(units // 8 + 1))
                    act.wait_ge(K.m_ready.sem, K.m_ready.at(units))
                    ins = nc.scalar.activation(cbt[:, :, :].rearrange("p g l -> p (g l)"), K.bank[5][:, 0:2 * P], ACT.Copy)
                    ins.then_inc(K.cb_ready.inc(), 1)
                    for u in range(8):
                        d = u % 2
                        act.wait_ge(K.diff_ready.sem, K.diff_ready.at(units + u + 1))
                        act.wait_ge(K.m_ready.sem, K.m_ready.at(units + u - 1))
                        for i in range(4):
                            h = 4 * (u // 2) + i
                            ins = nc.scalar.activation(e[:, u % 2, i, :], K.bank[2 + u % 2][:, i * P:i * P + P], ACT.Exp,
                                                       bias=neg[:, d, t, h:h + 1])
                        ins.then_inc(K.e_ready.inc(), 1)
                    units += 8

        @block.gpsimd
        def _(pool):
            turns = states = 0
            for seq in plan.seqs:
                turns += CHUNKS
                for c, d in plan.states[seq]:
                    pool.wait_ge(K.decay_ready.sem, K.decay_ready.at(1))
                    pool.wait_ge(K.xd_ready.sem, K.xd_ready.at(4 * turns))
                    pool.wait_ge(K.state_mm.sem, K.state_mm.at(states))
                    ins = nc.gpsimd.tensor_tensor(xw[:, :, :], xd[:, c, d, :, :], bh(dec[:, 2 * seq + c, d, :], HEADS), ALU.mult)
                    ins.then_inc(K.xw_ready.inc(), 1)
                    states += 1

        @block.vector
        def _(dve):
            V = nc.vector
            flat = lambda ap: ap.rearrange("p t d h -> p (t d h)")
            raw = M.dt[:, :, :].rearrange("p t h -> p (t h)")
            V.scalar_tensor_tensor(flat(t_abs[:]), raw, -1.0, raw, ALU.mult, ALU.max).then_inc(K.dt_abs.inc(), 1)
            dve.wait_ge(K.dt_exp.sem, K.dt_exp.at(1))
            V.tensor_scalar(flat(t_u[:]), flat(t_e[:]), 1.0, None, ALU.add).then_inc(K.dt_u.inc(), 1)
            dve.wait_ge(K.dt_u.sem, K.dt_u.own())
            V.tensor_scalar(flat(t_d[:]), flat(t_u[:]), -1.0, None, ALU.add).then_inc(K.dve_step.inc(), 1)
            dve.wait_ge(K.dve_step.sem, K.dve_step.own())
            V.tensor_scalar(flat(t_z[:]), flat(t_d[:]), 0.0, None, ALU.is_equal).then_inc(K.dve_step.inc(), 1)
            dve.wait_ge(K.dve_step.sem, K.dve_step.own())
            V.tensor_tensor(flat(t_d[:]), flat(t_d[:]), flat(t_z[:]), ALU.add).then_inc(K.dve_step.inc(), 1)
            dve.wait_ge(K.dve_step.sem, K.dve_step.own())
            V.reciprocal(flat(t_d[:]), flat(t_d[:])).then_inc(K.dve_step.inc(), 1)
            dve.wait_ge(K.dve_step.sem, K.dve_step.own())
            V.tensor_tensor(flat(t_d[:]), flat(t_d[:]), flat(t_e[:]), ALU.mult).then_inc(K.dve_step.inc(), 1)
            dve.wait_ge(K.dve_step.sem, K.dve_step.own())
            dve.wait_ge(K.dt_ln.sem, K.dt_ln.at(1))
            V.tensor_tensor(flat(t_ln[:]), flat(t_ln[:]), flat(t_d[:]), ALU.mult).then_inc(K.dve_step.inc(), 1)
            dve.wait_ge(K.dve_step.sem, K.dve_step.own())
            V.tensor_tensor(flat(t_z[:]), flat(t_z[:]), flat(t_e[:]), ALU.mult).then_inc(K.dve_step.inc(), 1)
            dve.wait_ge(K.dve_step.sem, K.dve_step.own())
            V.tensor_tensor(flat(t_ln[:]), flat(t_ln[:]), flat(t_z[:]), ALU.add).then_inc(K.dve_step.inc(), 1)
            dve.wait_ge(K.dve_step.sem, K.dve_step.own())
            ins = V.scalar_tensor_tensor(flat(dt[:]), raw, 0.0, flat(t_ln[:]), ALU.max, ALU.add)
            ins.then_inc(K.dve_step.inc(), 1)
            dve.wait_ge(K.dve_step.sem, K.dve_step.own())
            dve.wait_ge(K.a_exp.sem, K.a_exp.at(1))
            ins = V.scalar_tensor_tensor(a[:].rearrange("p t d h -> p t (d h)"), dt[:].rearrange("p t d h -> p t (d h)"), -1.0,
                                                       ea[:, :].unsqueeze(1).to_broadcast([P, TT, 32]), ALU.mult, ALU.mult)
            ins.then_inc(K.dt_ready.inc(), 1)
            dve.wait_ge(K.cum_ready.sem, K.cum_ready.at(1))
            V.tensor_copy(flat(cum[:]), K.bank[4][:, 0:P]).then_inc(K.dve_step.inc(), 1)
            dve.wait_ge(K.dve_step.sem, K.dve_step.own())
            V.tensor_copy(flat(tot[:]), K.bank[4][:, P:2 * P]).then_inc(K.dve_step.inc(), 1)
            dve.wait_ge(K.dve_step.sem, K.dve_step.own())
            V.tensor_scalar(flat(neg[:]), flat(cum[:]), -1.0, None, ALU.mult).then_inc(K.dve_step.inc(), 1)
            dve.wait_ge(K.dve_step.sem, K.dve_step.own())
            for d in range(2):
                ins = V.tensor_tensor(dec[:, :, d, :], tot[:, :, d, :], neg[:, d, :, :], ALU.add)
            ins.then_inc(K.cum_read.inc(), 1)

            turns = states = units = offs = gs = 0
            for seq in plan.seqs:
                for c in range(CHUNKS):
                    dve.wait_ge(K.xs_turned.sem, K.xs_turned.at(turns + 1))
                    for d in range(2):
                        for g in range(2):
                            ins = V.tensor_tensor(
                                      xd[:, c, d, GH * g:GH * g + GH, :], K.bank[g][:, :].rearrange("p (h n) -> p h n", n=HD),
                                      bh(dt[:, 2 * seq + c, d, GH * g:GH * g + GH], GH), ALU.mult)
                            ins.then_inc(K.xd_ready.inc(), 1)
                    turns += 1
                for c, d in plan.states[seq]:
                    prev = plan.prev(seq, c, d)
                    target = mid if (c == 0) == (d == 0) else init
                    if prev:
                        dve.wait_ge(K.decay_ready.sem, K.decay_ready.at(1))
                        dve.wait_ge(K.st_ready.sem, K.st_ready.own())
                        ins = V.tensor_tensor(target[:, d, :, :], state[prev][:, d, :, :], bh(etot[:, 2 * seq + c, d, :], HEADS), ALU.mult)
                        ins.then_inc(K.dve_step.inc(), 1)
                        dve.wait_ge(K.dve_step.sem, K.dve_step.own())
                    dve.wait_ge(K.state_mm.sem, K.state_mm.at(states + 1))
                    for g in range(2):
                        half = target[:, d, GH * g:GH * g + GH, :].rearrange("p h n -> p (h n)")
                        ins = V.tensor_tensor(half, half, K.bank[2 + g][:, :], ALU.add) if prev else V.tensor_copy(half, K.bank[2 + g][:, :])
                    ins.then_inc(K.st_ready.inc(), 1)
                    states += 1
                if not plan.with_y[seq]:
                    continue
                for c in range(CHUNKS):
                    t = 2 * seq + c

                    def sums(g):
                        nonlocal offs
                        y = ytm[:, GH * g:GH * g + GH, :]
                        y_flat = y.rearrange("p h n -> p (h n)")
                        dve.wait_ge(K.y_mm.sem, K.y_mm.at(units + 4 * g + 4))
                        dve.wait_ge(K.y_turned.sem, K.y_turned.at(gs + g - 1))
                        entering = [d for d in range(2) if plan.prev(seq, c, d)]
                        for d in entering:
                            dve.wait_ge(K.off_mm.sem, K.off_mm.at(offs + 1))
                            ins = V.tensor_tensor(tmp[:, d, :, :], K.bank[6 + offs % 2][:, :].rearrange("p (h n) -> p h n", n=HD),
                                                                bh(ecum[:, d, t, GH * g:GH * g + GH], GH), ALU.mult)
                            ins.then_inc(K.off_used.inc(), 1)
                            dve.wait_ge(K.off_used.sem, K.off_used.own())
                            offs += 1
                            add = tmp[:, d, :, :].rearrange("p h n -> p (h n)")
                            within = K.bank[g][:, :] if d == entering[0] else y_flat
                            ins = V.tensor_tensor(y_flat, add, within, ALU.add)
                            if d == entering[-1]:
                                ins.then_inc(K.ytm_ready.inc(), 1)
                            else:
                                ins.then_inc(K.dve_step.inc(), 1)
                                dve.wait_ge(K.dve_step.sem, K.dve_step.own())

                    def gated(g):
                        dve.wait_ge(K.y_turned.sem, K.y_turned.at(gs + g + 1))
                        for i in range(4):
                            ins = V.scalar_tensor_tensor(gt[:, i, :], fm(4 * g + i, t), K.dskip[:, layer, 4 * g + i:4 * g + i + 1],
                                                         K.bank[4][:, i * P:i * P + P], ALU.mult, ALU.add)
                        ins.then_inc(K.g_ready.inc(), 1)
                        dve.wait_ge(K.g_ready.sem, K.g_ready.own())
                        z = M.z[:, 4 * g:4 * g + 4, t * P:t * P + P]
                        V.tensor_tensor(z, z, gt[:, :, :], ALU.mult).then_inc(K.dve_step.inc(), 1)

                    for u in range(8):
                        dve.wait_ge(K.cb_ready.sem, K.cb_ready.at(units // 8 + 1))
                        dve.wait_ge(K.e_ready.sem, K.e_ready.at(units + u + 1))
                        dve.wait_ge(K.y_mm.sem, K.y_mm.at(units + u - 1))
                        ins = V.tensor_tensor(m[:, u % 2, :, :], e[:, u % 2, :, :],
                                                           cbt[:, u // 4, :].unsqueeze(1).to_broadcast([P, 4, P]), ALU.mult)
                        ins.then_inc(K.m_ready.inc(), 1)
                        if u == 5:
                            sums(0)
                    gated(0)
                    sums(1)
                    gated(1)
                    units += 8
                    gs += 2
    K.end_phase()



def mix_out(K, M, layer, last, following):
    nc = K.nc
    tok = LATENT if last else FULL
    t0, tn = tok
    with ExitStack() as mem:
        def sb(name, shape, dt=F32):
            return mem.enter_context(nc.sbuf_tensor(f"{name}_{layer}", shape, dt))
        yd_h, yd_l = sb("yd_h", [P, 8, TOK], F32R), sb("yd_l", [P, 8, TOK], F32R)
        y = sb("mix_y", [P, 8, TOK])
        parts_of = lambda k: (yd_h, yd_l, k) if k < 8 else (M.yc_h, M.yc_l, k - 8) if k < 12 else (M.ys_h, M.ys_l, k - 12)
        out = OutProduct(K, K.w_out[layer], (8, 8), lambda k: parts_of(k)[0][:, parts_of(k)[2], :],
                         lambda k: parts_of(k)[1][:, parts_of(k)[2], :], tok, tok, y, 0, 0, 8, 2)
        block = mem.enter_context(nc.Block(no_gpsimd_drain=True))
        gain = K.par[:, layer, 2, 100:108]

        @block.sync
        def _(sp):
            out.sp(sp, following)

        @block.tensor
        def _(pe):
            for j in range(8):
                stats_pe(K, pe, K.sq[:, j % 2, :], tok, j, 8, j)
            rstd_pe(K, pe, tok, 1)
            pe.wait_ge(K.yl_ready.sem, K.yl_ready.at(8))
            out.pe(pe, lambda pair: None)

        @block.scalar
        def _(act):
            for j in range(8):
                act.wait_ge(K.stat_done.sem, K.stat_done.at(j - 1))
                ins = nc.scalar.activation(K.sq[:, j % 2, 0:tn], M.z[:, j, t0:t0 + tn], ACT.Square)
                ins.then_inc(K.sq_ready.inc(), 1)
            rstd_act(K, act, tok, 1)
            for j in range(8):
                act.wait_ge(K.yn_ready.sem, K.yn_ready.at(j + 1))
                ins = nc.scalar.activation(yd_h[:, j, t0:t0 + tn], M.z[:, j, t0:t0 + tn], ACT.Copy, scale=gain[:, j:j + 1])
                ins.then_inc(K.yh_ready.inc(), 1)
            out.act(act)

        @block.vector
        def _(dve):
            post_gain_dve(K, dve, layer, 1, 1.0)
            rstd_dve(K, dve, tok, 8 * P, 8, 1)
            dve.wait_ge(K.rb_ready.sem, K.rb_ready.at(1))
            for j in range(8):
                z = M.z[:, j, t0:t0 + tn]
                nc.vector.tensor_tensor(z, z, K.bank[6][:, 0:tn], ALU.mult).then_inc(K.yn_ready.inc(), 1)
                dve.wait_ge(K.yh_ready.sem, K.yh_ready.at(j + 1))
                ins = nc.vector.scalar_tensor_tensor(yd_l[:, j, t0:t0 + tn], z, gain[:, j:j + 1],
                                                                   r32(yd_h[:, j, t0:t0 + tn]), ALU.mult, ALU.subtract)
                ins.then_inc(K.yl_ready.inc(), 1)
            out.dve(dve)
    K.end_phase()


def mixer(K, layer, last, following):
    nc = K.nc
    M = Kern()
    with ExitStack() as mem:
        def sb(name, shape, dt=F32):
            return mem.enter_context(nc.sbuf_tensor(f"{name}_{layer}", shape, dt))
        M.xbc = sb("xbc", [P, XBC_T, TOK])
        M.z = sb("z", [P, Z_T, TOK])
        M.yc_h, M.yc_l = sb("yc_h", [P, GRP_T, TOK], F32R), sb("yc_l", [P, GRP_T, TOK], F32R)
        M.ys_h, M.ys_l = sb("ys_h", [P, GRP_T, TOK], F32R), sb("ys_l", [P, GRP_T, TOK], F32R)
        M.dt = sb("dt_raw", [P, TT, 32])
        w_out_first = [(panel_src(K.w_out[layer], 8 * part, 8, 0), 8) for part in range(2)]
        project(K, M, layer, last, w_out_first)
        if K.stop == "proj":
            return
        scan(K, M, layer, last)
        mix_out(K, M, layer, last, following)



PACKS = 3


def param_rows(K, layer):
    I = K.inputs
    rows = lambda ap: ap.rearrange("(a p) -> a p", p=P)
    return [
        (0, 0, rows(I["b_mod"][layer])),
        (0, 72, I["norm_pre"][layer].rearrange("w (a p) -> (w a) p", p=P)),
        (0, 96, I["norm_post"][layer].rearrange("w (a p) -> (w a) p", p=P)),
        (1, 0, I["conf_conv_w"][layer].rearrange("k (a p) -> (k a) p", p=P)),
        (2, 0, I["ssd_conv_w"][layer].rearrange("k (a p) -> (k a) p", p=P)),
        (2, 60, rows(I["ssd_conv_b"][layer])),
        (2, 72, rows(I["conf_conv_b"][layer])),
        (2, 76, rows(I["conf_ln_g"][layer])),
        (2, 80, rows(I["conf_ln_b"][layer])),
        (2, 84, I["sc_conv_w"][layer].rearrange("k (a p) -> (k a) p", p=P)),
        (2, 96, rows(I["sc_conv_b"][layer])),
        (2, 100, rows(I["ssd_norm"][layer])),
    ]


PACK_ROWS = (120, 124, 108)


def opening(K, following):
    nc, I = K.nc, K.inputs
    L = K.layers
    with ExitStack() as mem:
        xt = mem.enter_context(nc.sbuf_tensor("xt", [P, TT, 8 * P], F32))
        pr = mem.enter_context(nc.sbuf_tensor("pr", [P, L * PACKS, P], F32))
        cr = mem.enter_context(nc.sbuf_tensor("cr", [16, P], F32))
        block = mem.enter_context(nc.Block(no_gpsimd_drain=True))
        x_tiles = [I["ctx"][0, t * P:(t + 1) * P, :] for t in range(2)] + [I["x"][0, t * P:(t + 1) * P, :] for t in range(2)]

        @block.sync
        def _(sp):
            sp.dma_start(cr[0:8, :], I["c_ctx"].rearrange("(a p) -> a p", p=P)).then_inc(K.cond_in.inc(16), 16)
            sp.dma_start(cr[8:16, :], I["c"][0].rearrange("(a p) -> a p", p=P)).then_inc(K.cond_in.inc(16), 16)
            for n in range(2):
                load_panel(K, sp, n, panel_src(K.w_mod[0], 0, 8, 2 * P * n), 8)
            for n in range(2, 8):
                sp.wait_ge(K.mod_lo.sem, K.mod_lo.at(2 * n - 2))
                load_panel(K, sp, n % 2, panel_src(K.w_mod[0], 0, 8, 2 * P * n), 8)
            for slot, panel in enumerate(following):
                sp.wait_ge(K.mod_lo.sem, K.mod_lo.at(14 + 2 * slot))
                load_panel(K, sp, slot, *panel)

        @block.gpsimd
        def _(pool):
            def select(out, pattern, base, mult, op, fill, after):
                pool.wait_ge(K.const_step.sem, after)
                return nc.gpsimd.affine_select(out=out, in_=out, compare_op=op, fill=fill, base=base,
                                               pattern=pattern, channel_multiplier=mult)
            nc.gpsimd.memset(K.ones[:, :], 1.0).then_inc(K.const_step.inc(), 1)
            nc.gpsimd.memset(K.ident[:, :], 0.0).then_inc(K.const_step.inc(), 1)
            nc.gpsimd.memset(K.tri[:, 0, :], 1.0).then_inc(K.const_step.inc(), 1)
            nc.gpsimd.memset(K.tri[:, 1, :], 1.0).then_inc(K.const_step.inc(), 1)
            nc.gpsimd.memset(K.mask[:, 0, :], 0.0).then_inc(K.const_step.inc(), 1)
            nc.gpsimd.memset(K.mask[:, 1, :], 0.0).then_inc(K.const_step.inc(), 1)
            nc.gpsimd.memset(K.identb[:, :], 0.0).then_inc(K.const_step.inc(), 1)
            nc.gpsimd.memset(K.cond[:, :].bitcast(F32), 0.0).then_inc(K.const_step.inc(), 1)
            nc.gpsimd.memset(K.fold[:, :], 0.0).then_inc(K.const_step.inc(), 1)
            n = K.const_step.count
            line = [[-1, P]]
            select(K.ident[:, :], line, 0, 1, ALU.not_equal, 1.0, n).then_inc(K.const_step.inc(), 1)
            select(K.identb[:, :], line, 0, 1, ALU.not_equal, 1.0, n).then_inc(K.const_step.inc(), 1)
            select(K.fold[:, :], [[-1, 2]], 0, 1, ALU.not_equal, 1.0, n).then_inc(K.const_step.inc(), 1)
            select(K.fold[:, :], [[-1, 2]], -2, 1, ALU.not_equal, 1.0, n + 3).then_inc(K.const_step.inc(), 1)
            for d, (step, mult) in enumerate((([[1, P]], -1), (line, 1))):
                select(K.tri[:, d, :], step, 0, mult, ALU.is_ge, 0.0, n).then_inc(K.const_step.inc(), 1)
                select(K.mask[:, d, :], step, 0, mult, ALU.is_ge, NEG, n).then_inc(K.const_step.inc(), 1)

        @block.tensor
        def _(pe):
            pe.wait_ge(K.const_step.sem, K.const_step.at(17))
            pe.wait_ge(K.cond_in.sem, K.cond_in.at(32))
            nc.tensor.transpose(K.bank[0][:, 0:16], cr[:, :], K.ident[0:16, 0:16]).then_inc(K.turn.inc(), 1)
            pe.wait_ge(K.params_in.sem, K.params_in.at(16 * L * len(param_rows(K, 0))))
            for n in range(L * PACKS):
                rows = PACK_ROWS[n % PACKS]
                if n >= 2:
                    pe.wait_ge(K.turned.sem, K.turned.at(n))
                ins = nc.tensor.transpose(K.bank[1 + n % 2][:, 0:rows], pr[0:rows, n, :], K.ident[0:rows, 0:rows])
                ins.then_inc(K.turn.inc(), 1)
            pe.wait_ge(K.cond_ready.sem, K.cond_ready.at(1))
            for h in range(16):
                mod_mm(K, pe, h, h % 2, h // 2, (K.wh[:, h % 2], K.wl[:, h % 2]))
                if h % 2 and h > 1:
                    mod_fold(K, pe, h // 2 - 1)
            mod_fold(K, pe, 7)
            pe.wait_ge(K.x_in.sem, K.x_in.at(16 * TT))
            for j in range(8):
                if j >= 4:
                    pe.wait_ge(K.turned.sem, K.turned.at(1 + L * PACKS + j - 3))
                elif j == 0:
                    pe.wait_ge(K.turned.sem, K.turned.at(1 + L * PACKS))
                b = (0, 1, 2, 3)[j % 4]
                for t in range(TT):
                    ins = nc.tensor.transpose(K.bank[b][:, t * P:t * P + P], xt[:, t, j * P:j * P + P], K.ident[:, :])
                ins.then_inc(K.turn.inc(), 1)

        @block.scalar
        def _(act):
            for layer in range(L):
                for pack, row, src in param_rows(K, layer):
                    act.dma_start(pr[row:row + src.shape[0], layer * PACKS + pack, :], src).then_inc(K.params_in.inc(16), 16)
            for t in range(TT):
                act.dma_start(xt[:, t, :], x_tiles[t]).then_inc(K.x_in.inc(16), 16)
            for layer in range(L):
                row = I["ssd_d"][layer].rearrange("(o h) -> o h", o=1).to_broadcast([P, 16])
                act.dma_start(K.dload[:, layer, :], row).then_inc(K.small_in.inc(16), 16)
            for layer in range(L):
                for src, dst in ((I["ssd_dt_bias"], K.dtb), (I["ssd_a_log"], K.alog)):
                    row = src[layer].rearrange("(o d) h -> o (d h)", o=1).to_broadcast([P, 32])
                    act.dma_start(dst[:, layer, :], row).then_inc(K.small_in.inc(16), 16)
            act.wait_ge(K.turn.sem, K.turn.at(1))
            act.wait_ge(K.const_step.sem, K.const_step.at(17))
            ins = nc.scalar.activation(K.condf[:, :, :], K.bank[0][:, 0:16].rearrange("p (s k) -> p k s", k=8), ACT.Silu)
            ins.then_inc(K.act_step.inc(), 1)
            act.wait_ge(K.act_step.sem, K.act_step.own())
            cond = K.cond[:, 0:32].rearrange("p (k c) -> p k c", c=4)
            nc.scalar.activation(cond[:, :, 0:2], K.condf[:, :, :], ACT.Copy).then_inc(K.turned.inc(), 1)
            for n in range(L * PACKS):
                act.wait_ge(K.turn.sem, K.turn.at(2 + n))
                rows = PACK_ROWS[n % PACKS]
                ins = nc.scalar.activation(K.par[:, n // PACKS, n % PACKS, 0:rows], K.bank[1 + n % 2][:, 0:rows], ACT.Copy)
                ins.then_inc(K.turned.inc(), 1)
            for h in range(16):
                act.wait_ge(K.raw_full[h // 2 % 2].sem, K.raw_full[h // 2 % 2].landed(h // 4 + 1))
                act.wait_ge(K.mod_mm.sem, K.mod_mm.at(h - 1))
                ins = nc.scalar.activation(K.wh[:, h % 2, :, :], K.raw[:, h // 2 % 2, :, h % 2 * P:h % 2 * P + P], ACT.Copy)
                ins.then_inc(K.mod_hi_done.inc(), 1)
                if h % 2 == 0 and h:
                    mod_row(K, act, h // 2 - 1)
            mod_row(K, act, 7)
            for j in range(8):
                act.wait_ge(K.turn.sem, K.turn.at(2 + L * PACKS + j))
                ins = nc.scalar.activation(K.res[:, j, :], K.bank[(0, 1, 2, 3)[j % 4]][:, :], ACT.Copy)
                ins.then_inc(K.turned.inc(), 1)

        @block.vector
        def _(dve):
            dve.wait_ge(K.turned.sem, K.turned.at(1))
            cond = K.cond[:, 0:32].rearrange("p (k c) -> p k c", c=4)
            ins = nc.vector.tensor_tensor(cond[:, :, 2:4], K.condf[:, :, :], r32(cond[:, :, 0:2]), ALU.subtract)
            ins.then_inc(K.cond_ready.inc(), 1)
            dve.wait_ge(K.turned.sem, K.turned.at(1 + L * PACKS))
            for h in range(16):
                dve.wait_ge(K.mod_hi_done.sem, K.mod_hi_done.at(h + 1))
                ins = nc.vector.tensor_tensor(K.wl[:, h % 2, :, :], K.raw[:, h // 2 % 2, :, h % 2 * P:h % 2 * P + P],
                                                          r32(K.wh[:, h % 2, :, :]), ALU.subtract)
                ins.then_inc(K.mod_lo.inc(), 1)
                if h % 2 == 0 and h >= 4:
                    mod_out(K, dve, 0, h - 4, h // 2 - 2)
            for panel in (6, 7):
                mod_out(K, dve, 0, 2 * panel, panel)
            dve.wait_ge(K.small_in.sem, K.small_in.at(16 * 3 * L))
            for half in range(2):
                h = slice(64 * half, 64 * half + 64)
                d = K.dload[h, :, :].rearrange("p l (j two) -> p l two j", two=2)[:, :, half, :]
                nc.vector.tensor_copy(K.dskip[h, :, :], d).then_inc(K.small_seen.inc(), 1)
    K.end_phase()


def closing(K):
    nc = K.nc
    with ExitStack() as mem:
        ot = mem.enter_context(nc.sbuf_tensor("ot", [P, 2, 8 * P], F32))
        block = mem.enter_context(nc.Block(no_gpsimd_drain=True))

        @block.tensor
        def _(pe):
            for t in range(2):
                for g in range(2):
                    for q in range(4):
                        j = 4 * g + q
                        ins = nc.tensor.transpose(K.bank[2 * t + g][:, q * P:q * P + P],
                                                  K.res[:, j, CTX + t * P:CTX + t * P + P], K.ident[:, :])
                    ins.then_inc(K.turn.inc(), 1)

        @block.scalar
        def _(act):
            for n in range(4):
                act.wait_ge(K.turn.sem, K.turn.at(n + 1))
                ins = nc.scalar.activation(ot[:, n // 2, n % 2 * 512:n % 2 * 512 + 512], K.bank[n][:, :], ACT.Copy)
                ins.then_inc(K.turned.inc(), 1)

        @block.sync
        def _(sp):
            for t in range(2):
                sp.wait_ge(K.turned.sem, K.turned.at(2 * t + 2))
                sp.dma_start(K.out[0, t * P:(t + 1) * P, :], ot[:, t, :]).then_inc(K.stored.inc(16), 16)
            sp.wait_ge(K.stored.sem, K.stored.at(32))
    K.end_phase()



def hybrid_block(nc, inputs, out, stop=None):
    K = Kern()
    K.nc, K.inputs, K.out = nc, inputs, out
    K.stop = stop
    K.layers = inputs["w_mod"].shape[0]
    K.d_ff = inputs["ffn_w_gate"].shape[3]
    K.w_mod, K.w_gate, K.w_up, K.w_down = (inputs[n] for n in ("w_mod", "ffn_w_gate", "ffn_w_up", "ffn_w_down"))
    K.w_in, K.w_out = inputs["w_in"], inputs["w_out"]
    assert inputs["w_mod"].shape[1] == 8 * P and K.d_ff % (2 * P) == 0 and 16 * P < K.d_ff <= 24 * P
    L = K.layers
    with ExitStack() as ctx:
        def sb(name, shape, dt=F32):
            return ctx.enter_context(nc.sbuf_tensor(name, shape, dt))

        K.signals = []

        def signal(name):
            K.signals.append(Signal(ctx.enter_context(nc.semaphore(name))))
            return K.signals[-1]

        K.a_exp = signal("a_exp")
        K.act_read = signal("act_read")
        K.act_step = signal("act_step")
        K.b_ready = signal("b_ready")
        K.b_turned = signal("b_turned")
        K.cb_mm = signal("cb_mm")
        K.cb_ready = signal("cb_ready")
        K.cent_ready = signal("cent_ready")
        K.cond_in = signal("cond_in")
        K.cond_ready = signal("cond_ready")
        K.const_step = signal("const_step")
        K.conv_done = signal("conv_done")
        K.cum_read = signal("cum_read")
        K.cum_ready = signal("cum_ready")
        K.decay_ready = signal("decay_ready")
        K.diag_ready = signal("diag_ready")
        K.diff_ready = signal("diff_ready")
        K.dt_abs = signal("dt_abs")
        K.dt_exp = signal("dt_exp")
        K.dt_ln = signal("dt_ln")
        K.dt_out = signal("dt_out")
        K.dt_raw = signal("dt_raw")
        K.dt_ready = signal("dt_ready")
        K.dt_u = signal("dt_u")
        K.dtw_hi = signal("dtw_hi")
        K.dtw_in = signal("dtw_in")
        K.dtw_ready = signal("dtw_ready")
        K.dve_read = signal("dve_read")
        K.dve_step = signal("dve_step")
        K.e_ready = signal("e_ready")
        K.g_ready = signal("g_ready")
        K.half_done = signal("half_done")
        K.hh_done = signal("hh_done")
        K.hi_done = signal("hi_done")
        K.hl_done = signal("hl_done")
        K.ln_hi = signal("ln_hi")
        K.ln_ready = signal("ln_ready")
        K.lo_done = signal("lo_done")
        K.m_ready = signal("m_ready")
        K.mean_ready = signal("mean_ready")
        K.mod_evac = signal("mod_evac")
        K.mod_fold = signal("mod_fold")
        K.mod_hi_done = signal("mod_hi_done")
        K.mod_lo = signal("mod_lo")
        K.mod_mm = signal("mod_mm")
        K.mod_row = signal("mod_row")
        K.ms_ready = signal("ms_ready")
        K.off_mm = signal("off_mm")
        K.off_used = signal("off_used")
        K.pads_zero = signal("pads_zero")
        K.params_in = signal("params_in")
        K.pgain_ready = signal("pgain_ready")
        K.prod_done = signal("prod_done")
        K.rb_ready = signal("rb_ready")
        K.rstd_ready = signal("rstd_ready")
        K.silu_done = signal("silu_done")
        K.small_in = signal("small_in")
        K.small_seen = signal("small_seen")
        K.sq_ready = signal("sq_ready")
        K.st_ready = signal("st_ready")
        K.stat_done = signal("stat_done")
        K.state_mm = signal("state_mm")
        K.stored = signal("stored")
        K.turn = signal("turn")
        K.turned = signal("turned")
        K.uh_ready = signal("uh_ready")
        K.ul_ready = signal("ul_ready")
        K.un_ready = signal("un_ready")
        K.x_in = signal("x_in")
        K.xbc_conv = signal("xbc_conv")
        K.xbc_out = signal("xbc_out")
        K.xd_ready = signal("xd_ready")
        K.xs_turned = signal("xs_turned")
        K.xw_ready = signal("xw_ready")
        K.y_mm = signal("y_mm")
        K.y_ready = signal("y_ready")
        K.y_turned = signal("y_turned")
        K.yc_lo = signal("yc_lo")
        K.yh_ready = signal("yh_ready")
        K.yl_ready = signal("yl_ready")
        K.yn_ready = signal("yn_ready")
        K.ys_hi = signal("ys_hi")
        K.ys_lo = signal("ys_lo")
        K.ytm_ready = signal("ytm_ready")
        K.raw_full = [signal(f"raw_full{n}") for n in range(2)]
        K.mod_full = signal("mod_full")
        K.bank = [ctx.enter_context(nc.psum_tensor(f"bank{n}", [P, 512], F32)) for n in range(8)]
        K.res = sb("res", [P, 8, TOK])
        K.raw = sb("raw", [P, 2, 8, 2 * P])
        K.wh = sb("wh", [P, 2, 8, P], F32R)
        K.wl = sb("wl", [P, 2, 8, P], F32R)
        K.sq = sb("sq", [P, 2, TOK])
        K.diag = sb("diag", [P, TT, P])
        K.par = sb("par", [P, L, PACKS, P])
        K.mod = sb("mod", [P, L, 72, 2])
        K.condf = sb("condf", [P, 8, 2])
        K.cond = sb("cond", [P, 28 + P], F32R)
        K.rows = sb("rows", [4, 2 * P])
        K.fold = sb("fold", [4, 2])
        K.gain, K.pgain = sb("gain", [P, 8, 2]), sb("pgain", [P, 8, 2])
        K.ms, K.rstd = sb("ms", [P, TT]), sb("rstd", [P, TT])
        K.ident, K.ones = sb("ident", [P, P]), sb("ones", [P, P])
        K.identb = sb("identb", [P, P], BF16)
        K.tri = sb("tri", [P, 2, P])
        K.mask = sb("mask", [P, 2, P], BF16)
        K.dskip = sb("dskip", [P, L, 8])
        K.dload = sb("dload", [P, L, 16])
        K.dtb, K.alog = sb("dtb", [P, L, 32]), sb("alog", [P, L, 32])

        def ff_first(layer, ff):
            return [(panel_src(w[layer, ff], 0, 8, 0), 8) for w in (K.w_gate, K.w_up)]

        opening(K, ff_first(0, 0))
        for layer in range(L):
            last = layer == L - 1
            feed_forward(K, layer, 0, FULL, layer, 16 if layer == 0 else 68, layer == 0,
                         12 if layer == 0 else 4, mixer_first(K, layer))
            if stop == "ff":
                break
            mixer(K, layer, last, ff_first(layer, 1))
            if stop in ('mix', 'proj'):
                break
            after = ff_first(layer + 1, 0) if not last else []
            feed_forward(K, layer, 2, LATENT if last else FULL, None if last else layer + 1, 0, not last,
                         0 if last else 24, after)
            if stop == "layer":
                break
        closing(K)


NAMES = ["x", "c", "ctx", "c_ctx", "w_mod", "b_mod", "norm_pre", "norm_post", "ffn_w_gate", "ffn_w_up", "ffn_w_down",
         "w_in", "ssd_conv_w", "ssd_conv_b", "ssd_dt_bias", "ssd_a_log", "ssd_d", "ssd_norm", "conf_conv_w",
         "conf_conv_b", "conf_ln_g", "conf_ln_b", "sc_conv_w", "sc_conv_b", "w_out"]


def kernel(**inputs):
    import numpy as np
    import concourse.bacc as bacc
    from concourse.bass_utils import run_bass_kernel_spmd

    nc = bacc.Bacc("TRN2", target_bir_lowering=False, num_devices=1)
    arrays, aps = {}, {}
    for name in NAMES:
        a = np.ascontiguousarray(inputs[name])
        arrays[f"in_{name}"] = a
        aps[name] = nc.dram_tensor(f"in_{name}", a.shape, mybir.dt.from_np(a.dtype), kind="ExternalInput").ap()
    out = nc.dram_tensor("out_x", inputs["x"].shape, F32, kind="ExternalOutput").ap()
    hybrid_block(nc, aps, out)
    return run_bass_kernel_spmd(nc, [arrays], core_ids=[0]).results[0]["out_x"]
```

```python
from contextlib import ExitStack

import concourse.bass as bass
from concourse import mybir

F32 = mybir.dt.float32
F32R = mybir.dt.float32r
BF16 = mybir.dt.bfloat16
ALU = mybir.AluOpType
ACT = mybir.ActivationFunctionType

P = 128
CTX = 256
TOK = 512
TT = TOK // P
GRID = 64
EPS = 1e-6
NEG = -1e30
FULL = (0, TOK)
LATENT = (CTX, TOK - CTX)


class Signal:

    def __init__(self, sem):
        self.sem, self.base, self.count = sem, 0, 0

    def inc(self, n=1):
        self.count += n
        return self.sem

    def at(self, k):
        return k + self.base if not isinstance(k, int) or k > 0 else self.base

    def landed(self, k):
        return 16 * k + self.base

    def own(self, but=0):
        return self.count - but


class Kern:

    def end_phase(self):
        for s in self.signals:
            s.base = s.count

    def loop(self, eng, first, end):
        return CountedLoop(self, eng, first, end)


class CountedLoop:

    def __init__(self, K, eng, first, end):
        self.K, self.trips, self.fori = K, end - first, eng.Fori(first, end)

    def __enter__(self):
        self.before = [s.count for s in self.K.signals]
        return self.fori.__enter__()

    def __exit__(self, *exc):
        for s, b in zip(self.K.signals, self.before):
            s.count += (s.count - b) * (self.trips - 1)
        return self.fori.__exit__(*exc)


def r32(ap):
    return ap.bitcast(F32)



def panel_src(w, k0, kn, c0):
    return w[k0 * P:(k0 + kn) * P, bass.ds(c0, 2 * P)].rearrange("(k p) n -> p k n", p=P)


def load_panel(K, sp, slot, src, kn):
    sp.dma_start(K.raw[:, slot, 0:kn, :], src).then_inc(K.raw_full[slot].inc(16), 16)


def weight_hi(K, act, panel_k, slot, half, kn, nth):
    act.wait_ge(K.raw_full[slot].sem, K.raw_full[slot].landed(panel_k))
    act.wait_ge(K.half_done.sem, K.half_done.at(nth - 1))
    ins = K.nc.scalar.activation(K.wh[:, half, 0:kn, :], K.raw[:, slot, 0:kn, half * P:half * P + P],
                                              ACT.Copy)
    ins.then_inc(K.hi_done.inc(), 1)


def weight_lo(K, dve, slot, half, kn, nth):
    dve.wait_ge(K.hi_done.sem, K.hi_done.at(nth + 1))
    ins = K.nc.vector.tensor_tensor(K.wl[:, half, 0:kn, :], K.raw[:, slot, 0:kn, half * P:half * P + P],
                                                 r32(K.wh[:, half, 0:kn, :]), ALU.subtract)
    ins.then_inc(K.lo_done.inc(), 1)


def product_half(K, pe, bank, half, kn, xh, xl, tok, first, last, nth, ready=None):
    t0, tn = tok
    pe.wait_ge(K.lo_done.sem, K.lo_done.at(nth + 1))
    for k in range(kn):
        if ready:
            pe.wait_ge(ready[0].sem, ready[0].at(ready[1] + k + 1))
        h, l = xh(k)[:, t0:t0 + tn], xl(k)[:, t0:t0 + tn]
        K.nc.tensor.matmul(bank[:, 0:tn], K.wh[:, half, k, :], h, start=first and k == 0, stop=False)
        K.nc.tensor.matmul(bank[:, 0:tn], K.wh[:, half, k, :], l, start=False, stop=False)
        ins = K.nc.tensor.matmul(bank[:, 0:tn], K.wl[:, half, k, :], h, start=False, stop=last and k == kn - 1)
    ins.then_inc(K.half_done.inc(), 1)



def load_mod(K, sp, w_mod, q, panel):
    sp.wait_ge(K.mod_lo.sem, K.mod_lo.at(2 * panel))
    sp.dma_start(K.raw_mod[:, :, :], panel_src(w_mod, 0, 8, P * q)).then_inc(K.mod_full.inc(16), 16)


def mod_hi(K, act, h, parity, panel):
    act.wait_ge(K.mod_full.sem, K.mod_full.landed(panel + 1))
    act.wait_ge(K.mod_mm.sem, K.mod_mm.at(h))
    ins = K.nc.scalar.activation(K.mod_split[:, 0], K.raw_mod[:, :, parity * P:parity * P + P], ACT.Copy)
    ins.then_inc(K.mod_hi_done.inc(), 1)


def mod_lo(K, dve, h, parity):
    dve.wait_ge(K.mod_hi_done.sem, K.mod_hi_done.at(h + 1))
    ins = K.nc.vector.tensor_tensor(K.mod_split[:, 1], K.raw_mod[:, :, parity * P:parity * P + P],
                                                r32(K.mod_split[:, 0]), ALU.subtract)
    ins.then_inc(K.mod_lo.inc(), 1)


def mod_mm(K, pe, h, parity, panel, split):
    pe.wait_ge(K.mod_lo.sem, K.mod_lo.at(h + 1))
    pe.wait_ge(K.mod_row.sem, K.mod_row.at(panel))
    for k in range(8):
        cond = K.cond[:, 4 * k:4 * k + P]
        out = K.bank[4][:, parity * 2 * P:(parity + 1) * 2 * P].rearrange("p (w n) -> p w n", w=2)
        ins = K.nc.tensor.matmul(out, cond, split[:, :, k, :], start=k == 0, stop=k == 7)
    ins.then_inc(K.mod_mm.inc(), 1)


def mod_row(K, act, panel):
    act.wait_ge(K.mod_mm.sem, K.mod_mm.at(2 * panel + 2))
    act.wait_ge(K.mod_fold.sem, K.mod_fold.at(panel))
    K.nc.scalar.activation(K.rows[:, :], K.bank[4][0:4, :], ACT.Copy).then_inc(K.mod_row.inc(), 1)


def mod_fold(K, pe, panel):
    pe.wait_ge(K.mod_row.sem, K.mod_row.at(panel + 1))
    pe.wait_ge(K.mod_evac.sem, K.mod_evac.at(panel))
    for t in range(2):
        for w in range(2):
            ins = K.nc.tensor.matmul(K.bank[7][:, 2 * t:2 * t + 2], K.rows[:, (2 * t + w) * P:(2 * t + w + 1) * P],
                                     K.fold[:, :], start=w == 0, stop=w == 1)
    ins.then_inc(K.mod_fold.inc(), 1)


def mod_out(K, dve, layer, q, panel):
    dve.wait_ge(K.mod_fold.sem, K.mod_fold.at(panel + 1))
    bias = K.par[:, layer, 0, bass.ds(q, 2)].unsqueeze(2).to_broadcast([P, 2, 2])
    ins = K.nc.vector.tensor_tensor(K.mod[:, layer, bass.ds(q, 2), :],
                                                  K.bank[7][:, 0:4].rearrange("p (q s) -> p q s", s=2), bias, ALU.add)
    ins.then_inc(K.mod_evac.inc(), 1)



def stats_pe(K, pe, src, tok, j, n, nth):
    pe.wait_ge(K.sq_ready.sem, K.sq_ready.at(nth + 1))
    for t in range(tok[1] // P):
        ins = K.nc.tensor.matmul(K.bank[5][:, t:t + 1], src[:, t * P:t * P + P], K.ones[:, 0:1],
                                 start=j == 0 and t == 0, stop=j == n - 1, skip_group_check=True)
    ins.then_inc(K.stat_done.inc(), 1)


def rstd_dve(K, dve, tok, width, stats, nth):
    n = tok[1] // P
    dve.wait_ge(K.stat_done.sem, K.stat_done.at(stats))
    ins = K.nc.vector.tensor_scalar(K.ms[:, 0:n], K.bank[5][:, 0:n], 1.0 / width, EPS, ALU.mult, ALU.add)
    ins.then_inc(K.dve_step.inc(), 1)
    dve.wait_ge(K.dve_step.sem, K.dve_step.own())
    K.nc.vector.reciprocal(K.ms[:, 0:n], K.ms[:, 0:n]).then_inc(K.ms_ready.inc(), 1)
    dve.wait_ge(K.rstd_ready.sem, K.rstd_ready.at(nth))
    ins = K.nc.vector.tensor_tensor(
              K.diag[:, 0:n, :], K.ident[:, :].unsqueeze(1).to_broadcast([P, n, P]),
              K.rstd[:, 0:n].unsqueeze(2).to_broadcast([P, n, P]), ALU.mult)
    ins.then_inc(K.diag_ready.inc(), 1)


def rstd_act(K, act, tok, nth):
    n = tok[1] // P
    act.wait_ge(K.ms_ready.sem, K.ms_ready.at(nth))
    K.nc.scalar.activation(K.rstd[:, 0:n], K.ms[:, 0:n], ACT.Sqrt).then_inc(K.rstd_ready.inc(), 1)


def rstd_pe(K, pe, tok, nth):
    n = tok[1]
    pe.wait_ge(K.diag_ready.sem, K.diag_ready.at(nth))
    ins = K.nc.tensor.matmul(K.bank[6][:, 0:n], K.ones[:, :],
                                           K.diag[:, 0:n // P, :].rearrange("p t n -> p (t n)"), start=True, stop=True)
    ins.then_inc(K.rb_ready.inc(), 1)



def next_rms_act(K, act, tok, stats, nth):
    t0, tn = tok
    for j in range(8):
        act.wait_ge(K.res_ready.sem, K.res_ready.at(j + 1))
        act.wait_ge(K.stat_done.sem, K.stat_done.at(stats + j - 1))
        ins = K.nc.scalar.activation(K.sq[:, j % 2, 0:tn], K.res[:, j, t0:t0 + tn], ACT.Square)
        ins.then_inc(K.sq_ready.inc(), 1)
    rstd_act(K, act, tok, nth)


def next_rms_pe(K, pe, tok, stats, nth):
    for j in range(8):
        stats_pe(K, pe, K.sq[:, j % 2, :], tok, j, 8, stats + j)
    rstd_pe(K, pe, tok, nth)


def next_rms_dve(K, dve, tok, stats, nth):
    rstd_dve(K, dve, tok, 1024, stats + 8, nth)



def prenorm_act(K, act, layer, which, tok, un_buf, uh):
    t0, tn = tok
    weight_hi(K, act, 0, 0, 0, 8, 0)
    for j in range(8):
        un = un_buf[:, j % 2, :]
        act.wait_ge(K.un_ready.sem, K.un_ready.at(j + 1))
        for s in range(2):
            if s * CTX >= t0:
                a = s * CTX - t0
                ins = K.nc.scalar.activation(un[:, a:a + CTX], un[:, a:a + CTX], ACT.Identity, scale=K.gain[:, j, s:s + 1],
                                             bias=K.mod[:, layer, 24 * which + j, s:s + 1])
                ins.then_inc(K.act_step.inc(), 1)
        act.wait_ge(K.act_step.sem, K.act_step.own())
        K.nc.scalar.activation(uh[:, j, t0:t0 + tn], un[:, 0:tn], ACT.Copy).then_inc(K.uh_ready.inc(), 1)
        if j == 4:
            weight_hi(K, act, 0, 0, 1, 8, 1)


def prenorm_dve(K, dve, layer, which, tok, un_buf, uh, ul):
    t0, tn = tok
    nc = K.nc

    def normed(j):
        dve.wait_ge(K.ul_ready.sem, K.ul_ready.own())
        ins = nc.vector.tensor_tensor(un_buf[:, j % 2, 0:tn], K.res[:, j, t0:t0 + tn], K.bank[6][:, 0:tn], ALU.mult)
        ins.then_inc(K.un_ready.inc(), 1)

    scale = K.mod[:, layer, 8 * (3 * which + 1):8 * (3 * which + 2), :]
    nc.vector.tensor_scalar(K.gain[:, :, :], scale, 1.0, None, ALU.add).then_inc(K.dve_step.inc(), 1)
    dve.wait_ge(K.dve_step.sem, K.dve_step.own())
    g = K.par[:, layer, 0, 72 + 8 * which:80 + 8 * which].unsqueeze(2).to_broadcast([P, 8, 2])
    nc.vector.tensor_tensor(K.gain[:, :, :], K.gain[:, :, :], g, ALU.mult).then_inc(K.dve_step.inc(), 1)
    dve.wait_ge(K.dve_step.sem, K.dve_step.own())
    normed(0)
    weight_lo(K, dve, 0, 0, 8, 0)
    for j in range(8):
        if j < 7:
            normed(j + 1)
        dve.wait_ge(K.uh_ready.sem, K.uh_ready.at(j + 1))
        ins = nc.vector.tensor_tensor(ul[:, j, t0:t0 + tn], un_buf[:, j % 2, 0:tn], r32(uh[:, j, t0:t0 + tn]), ALU.subtract)
        ins.then_inc(K.ul_ready.inc(), 1)
        if j == 5:
            weight_lo(K, dve, 0, 1, 8, 1)



def post_gain_dve(K, dve, layer, which, weight):
    nc = K.nc
    gate = K.mod[:, layer, 8 * (3 * which + 2):8 * (3 * which + 3), :]
    nc.vector.tensor_scalar(K.pgain[:, :, :], gate, weight, None, ALU.mult).then_inc(K.dve_step.inc(), 1)
    dve.wait_ge(K.dve_step.sem, K.dve_step.own())
    g = K.par[:, layer, 0, 96 + 8 * which:104 + 8 * which].unsqueeze(2).to_broadcast([P, 8, 2])
    nc.vector.tensor_tensor(K.pgain[:, :, :], K.pgain[:, :, :], g, ALU.mult).then_inc(K.pgain_ready.inc(), 1)


def post_tile_act(K, act, bank, j, tok, y, stats):
    t0, tn = tok
    if stats + j >= 2:
        act.wait_ge(K.stat_done.sem, K.stat_done.at(stats + j - 1))
    K.nc.scalar.activation(K.sq[:, j % 2, 0:tn], bank[:, 0:tn], ACT.Square).then_inc(K.sq_ready.inc(), 1)
    for s in range(2):
        if s * CTX >= t0:
            a = s * CTX - t0
            ins = K.nc.scalar.activation(y[:, j, a:a + CTX], bank[:, a:a + CTX], ACT.Copy, scale=K.pgain[:, j, s:s + 1])
    ins.then_inc(K.y_ready.inc(), 1)


def residual_dve(K, dve, tok, y, stats, nth):
    t0, tn = tok
    rstd_dve(K, dve, tok, 1024, stats, nth)
    dve.wait_ge(K.y_ready.sem, K.y_ready.at(8))
    dve.wait_ge(K.rb_ready.sem, K.rb_ready.at(nth))
    for j in range(9):
        if j < 8:
            K.nc.vector.tensor_tensor(y[:, j, 0:tn], y[:, j, 0:tn], K.bank[6][:, 0:tn], ALU.mult).then_inc(K.dve_step.inc(), 1)
        if j > 0:
            i = j - 1
            dve.wait_ge(K.dve_step.sem, K.dve_step.own(j < 8))
            ins = K.nc.vector.tensor_tensor(K.res[:, i, t0:t0 + tn], K.res[:, i, t0:t0 + tn], y[:, i, 0:tn], ALU.add)
            ins.then_inc(K.res_ready.inc(), 1)


class OutProduct:

    def __init__(self, K, w, parts, order, xh, xl, tok, xtok, y, halves, panels, stats, norms, norm_follows, mods=0,
                 mod_h=0, mod_layer=0, mod_q=0):
        self.K, self.w, self.parts, self.xh, self.xl, self.tok, self.xtok, self.y = K, w, parts, xh, xl, tok, xtok, y
        self.order = order
        self.halves, self.panels, self.stats, self.norms = halves, panels, stats, norms
        self.mods, self.mod_h, self.mod_layer, self.mod_q = mods, mod_h, mod_layer, mod_q
        self.norm_follows = norm_follows
        self.kstart = [sum(parts[:n]) for n in range(len(parts))]
        self.n_panels = len(order)
        self.first = [p == min(q for q in range(len(order)) if order[q][0] == order[p][0]) for p in range(len(order))]
        self.last = [p == max(q for q in range(len(order)) if order[q][0] == order[p][0]) for p in range(len(order))]

    def src(self, p):
        pair, part = self.order[p]
        return panel_src(self.w, self.kstart[part], self.parts[part], 2 * P * pair), self.parts[part]

    def sp(self, sp, following):
        K = self.K
        for p in range(self.n_panels):
            if p < self.mods // 2:
                load_mod(K, sp, K.w_mod[self.mod_layer], self.mod_q + 2 * p, self.mod_h // 2 + p)
            if p + 2 < self.n_panels:
                src, kn = self.src(p + 2)
            elif p + 2 - self.n_panels < len(following):
                src, kn = following[p + 2 - self.n_panels]
            else:
                continue
            sp.wait_ge(K.lo_done.sem, K.lo_done.at(self.halves + 2 * p + 2))
            load_panel(K, sp, p % 2, src, kn)

    def pe(self, pe, bank_free, before, ready):
        K, n = self.K, 0
        for p, (pair, part) in enumerate(self.order):
            k0 = self.kstart[part]
            for half in range(2):
                j = 2 * pair + half
                if self.first[p] and pair >= 2:
                    pe.wait_ge(K.y_ready.sem, K.y_ready.at(j - 3))
                elif self.first[p]:
                    bank_free(pair)
                before(n)
                product_half(K, pe, K.bank[2 * (pair % 2) + half], half, self.parts[part], lambda k: self.xh(k0 + k),
                             lambda k: self.xl(k0 + k), self.xtok, self.first[p], self.last[p], self.halves + n,
                             ready.get(n))
                h = self.mod_h + n
                if n < self.mods:
                    mod_mm(K, pe, h, half, h // 2, K.mod_split)
                if half == 1 and 2 <= h and n <= self.mods:
                    mod_fold(K, pe, h // 2 - 1)
                if self.last[p] and pair >= 1:
                    stats_pe(K, pe, K.sq[:, half, :], self.tok, j - 2, 8, self.stats + j - 2)
                n += 1
        if self.mods:
            mod_fold(K, pe, (self.mod_h + self.mods) // 2 - 1)
        for j in (6, 7):
            stats_pe(K, pe, K.sq[:, j % 2, :], self.tok, j, 8, self.stats + j)
        rstd_pe(K, pe, self.tok, self.norms)
        if self.norm_follows:
            next_rms_pe(K, pe, self.tok, self.stats + 8, self.norms + 1)

    def act(self, act, skip=0):
        K = self.K
        for n in range(2 * self.n_panels + 2):
            p, half, h = n // 2, n % 2, self.mod_h + n
            if skip <= n < 2 * self.n_panels:
                weight_hi(K, act, self.panels + p // 2, p % 2, half, self.parts[self.order[p][1]], self.halves + n)
            if n == 0:
                act.wait_ge(K.pgain_ready.sem, K.pgain_ready.at(1))
            if 1 <= n <= self.mods:
                mod_hi(K, act, h - 1, 1 - half, (h - 1) // 2)
            if half == 1 and h - 1 >= 2 and n <= self.mods + 1 and self.mods:
                mod_row(K, act, (h - 1) // 2 - 1)
            if n >= 2 and self.last[p - 1]:
                j = 2 * self.order[p - 1][0] + half
                act.wait_ge(K.half_done.sem, K.half_done.at(self.halves + n - 1))
                post_tile_act(K, act, K.bank[2 * (j // 2 % 2) + j % 2], j, self.tok, self.y, self.stats)
        rstd_act(K, act, self.tok, self.norms)
        if self.norm_follows:
            next_rms_act(K, act, self.tok, self.stats + 8, self.norms + 1)

    def dve(self, dve, skip=0):
        K = self.K
        for n in range(2 * self.n_panels + 1):
            p, half, h = n // 2, n % 2, self.mod_h + n
            if skip <= n < 2 * self.n_panels:
                weight_lo(K, dve, p % 2, half, self.parts[self.order[p][1]], self.halves + n)
            if 1 <= n <= self.mods:
                mod_lo(K, dve, h - 1, 1 - half)
                if half == 1 and (h - 1) // 2 >= 2:
                    self.mod_out(dve, (h - 1) // 2 - 2)
        if self.mods:
            for back in (2, 1):
                self.mod_out(dve, (self.mod_h + self.mods) // 2 - back)
        residual_dve(K, dve, self.tok, self.y, self.stats + 8, self.norms)
        if self.norm_follows:
            next_rms_dve(K, dve, self.tok, self.stats + 8, self.norms + 1)

    def mod_out(self, dve, panel):
        mod_out(self.K, dve, self.mod_layer, self.mod_q + 2 * panel - self.mod_h, panel)



def feed_forward(K, layer, which, tok, mod_layer, mod_q, mods_loop, mods_down, following):
    nc = K.nc
    ff = which // 2
    w_gate, w_up, w_down = K.w_gate[layer, ff], K.w_up[layer, ff], K.w_down[layer, ff]
    w_mod = K.w_mod[mod_layer] if mod_layer is not None else None
    t0, tn = tok
    FT = K.d_ff // P
    pairs = FT // 2
    with ExitStack() as mem:
        tag = f"{layer}{which}"
        if mods_loop or mods_down:
            K.raw_mod = mem.enter_context(nc.sbuf_tensor("raw_mod" + tag, [P, 8, 2 * P], F32))
            K.mod_split = mem.enter_context(nc.sbuf_tensor("mod_split" + tag, [P, 2, 8, P], F32R))
        hh = mem.enter_context(nc.sbuf_tensor("hh" + tag, [P, FT, tn], F32R))
        hl = mem.enter_context(nc.sbuf_tensor("hl" + tag, [P, FT, tn], F32R))
        with ExitStack() as up_mem:
            uh = up_mem.enter_context(nc.sbuf_tensor("uh" + tag, [P, 8, TOK], F32R))
            ul = up_mem.enter_context(nc.sbuf_tensor("ul" + tag, [P, 8, TOK], F32R))
            sil = up_mem.enter_context(nc.sbuf_tensor("sil" + tag, [P, 2, TOK], F32))
            hf = up_mem.enter_context(nc.sbuf_tensor("hf" + tag, [P, 2, TOK], F32))
        y = mem.enter_context(nc.sbuf_tensor("y" + tag, [P, 8, TOK], F32))
        out = OutProduct(K, w_down, (8, 8, FT - 16), [(pair, part) for pair in range(4) for part in range(3)], lambda k: hh[:, k, :], lambda k: hl[:, k, :], tok, (0, tn), y,
                         4 * pairs, pairs, 0, 1, bool(following), mods_down, 4 * pairs if mods_loop else 0, mod_layer,
                         mod_q + (4 * pairs if mods_loop else 0))
        block = mem.enter_context(nc.Block(no_gpsimd_drain=True))

        @block.sync
        def _(sp):
            def next_panels(i, gate, up):
                sp.wait_ge(K.lo_done.sem, K.lo_done.at(4 * i + 2))
                load_panel(K, sp, 0, *gate)
                if mods_loop:
                    load_mod(K, sp, w_mod, mod_q + 4 * i + 2, 2 * i + 1)
                sp.wait_ge(K.lo_done.sem, K.lo_done.at(4 * i + 4))
                load_panel(K, sp, 1, *up)

            if mods_loop:
                load_mod(K, sp, w_mod, mod_q, 0)
            with K.loop(sp, 0, pairs - 1) as i:
                next_panels(i, (panel_src(w_gate, 0, 8, 2 * P * i + 2 * P), 8), (panel_src(w_up, 0, 8, 2 * P * i + 2 * P), 8))
                if mods_loop:
                    load_mod(K, sp, w_mod, mod_q + 4 * i + 4, 2 * i + 2)
            next_panels(pairs - 1, out.src(0), out.src(1))
            out.sp(sp, following)

        @block.tensor
        def _(pe):
            def trip(i, first):
                for half in range(4):
                    if half % 2 == 0:
                        pe.wait_ge((K.silu_done, K.prod_done)[half // 2].sem, (K.silu_done, K.prod_done)[half // 2].at(2 * i))
                    product_half(K, pe, K.bank[half], half % 2, 8, lambda k: uh[:, k, :], lambda k: ul[:, k, :], tok,
                                 True, True, 4 * i + half, (K.ul_ready, 0) if first and half == 0 else None)
                    if mods_loop:
                        mod_mm(K, pe, 4 * i + half, half % 2, 2 * i + half // 2, K.mod_split)
                        if half % 2 and not (first and half == 1):
                            mod_fold(K, pe, 2 * i - 1 + half // 2)
            trip(0, True)
            with K.loop(pe, 1, pairs) as i:
                trip(i, False)

            def bank_free(pair):
                pe.wait_ge((K.silu_done, K.prod_done)[pair].sem, (K.silu_done, K.prod_done)[pair].at(FT))
                pe.wait_ge(K.hl_done.sem, K.hl_done.at(FT))
            out.pe(pe, bank_free, lambda n: None, {})

        @block.scalar
        def _(act):
            prenorm_act(K, act, layer, which, tok, sil, uh)

            def hidden_hi(f, at):
                act.wait_ge(K.prod_done.sem, K.prod_done.at(f + 1))
                ins = nc.scalar.activation(hh[:, bass.ds(f, 1), :].rearrange("p a n -> p (a n)"), hf[:, at, 0:tn], ACT.Copy)
                ins.then_inc(K.hh_done.inc(), 1)

            def silu(i, j):
                act.wait_ge(K.half_done.sem, K.half_done.at(4 * i + j + 1))
                act.wait_ge(K.prod_done.sem, K.prod_done.at(2 * i + j - 1))
                nc.scalar.activation(sil[:, j, 0:tn], K.bank[j][:, 0:tn], ACT.Silu).then_inc(K.silu_done.inc(), 1)

            def mod(i, n):
                if mods_loop:
                    mod_hi(K, act, 4 * i + n, n % 2, 2 * i + n // 2)

            def trip(i, first, last):
                if not first:
                    weight_hi(K, act, i, 0, 1, 8, 4 * i + 1)
                mod(i, 0)
                if not first:
                    if mods_loop:
                        mod_row(K, act, 2 * i - 1)
                    hidden_hi(2 * i - 1, 1)
                weight_hi(K, act, i, 1, 0, 8, 4 * i + 2)
                mod(i, 1)
                silu(i, 0)
                weight_hi(K, act, i, 1, 1, 8, 4 * i + 3)
                mod(i, 2)
                if mods_loop:
                    mod_row(K, act, 2 * i)
                silu(i, 1)
                if not last:
                    weight_hi(K, act, i + 1, 0, 0, 8, 4 * i + 4)
                else:
                    weight_hi(K, act, pairs, 0, 0, out.parts[0], 4 * pairs)
                mod(i, 3)
                hidden_hi(2 * i, 0)

            trip(0, True, False)
            with K.loop(act, 1, pairs - 1) as i:
                trip(i, False, False)
            trip(pairs - 1, False, True)
            weight_hi(K, act, pairs, 0, 1, out.parts[0], 4 * pairs + 1)
            hidden_hi(FT - 1, 1)
            out.act(act, skip=2)

        @block.vector
        def _(dve):
            prenorm_dve(K, dve, layer, which, tok, sil, uh, ul)

            def product(i, j):
                dve.wait_ge(K.silu_done.sem, K.silu_done.at(2 * i + j + 1))
                dve.wait_ge(K.half_done.sem, K.half_done.at(4 * i + 2 + j + 1))
                ins = nc.vector.tensor_tensor(hf[:, j, 0:tn], sil[:, j, 0:tn], K.bank[2 + j][:, 0:tn], ALU.mult)
                ins.then_inc(K.prod_done.inc(), 1)

            def hidden_lo(f, at):
                dve.wait_ge(K.hh_done.sem, K.hh_done.at(f + 1))
                h = bass.ds(f, 1)
                ins = nc.vector.tensor_tensor(hl[:, h, :].rearrange("p a n -> p (a n)"), hf[:, at, 0:tn],
                                                           r32(hh[:, h, :]).rearrange("p a n -> p (a n)"), ALU.subtract)
                ins.then_inc(K.hl_done.inc(), 1)

            def mod(i, n, first):
                if mods_loop:
                    mod_lo(K, dve, 4 * i + n, n % 2)
                    if n % 2 == 0 and not first:
                        mod_out(K, dve, mod_layer, mod_q + 2 * (2 * i - 2 + n // 2), 2 * i - 2 + n // 2)

            def trip(i, first, last):
                if not first:
                    weight_lo(K, dve, 0, 1, 8, 4 * i + 1)
                mod(i, 0, first)
                if not first:
                    hidden_lo(2 * i - 1, 1)
                weight_lo(K, dve, 1, 0, 8, 4 * i + 2)
                mod(i, 1, first)
                weight_lo(K, dve, 1, 1, 8, 4 * i + 3)
                mod(i, 2, first)
                if not last:
                    weight_lo(K, dve, 0, 0, 8, 4 * i + 4)
                else:
                    weight_lo(K, dve, 0, 0, out.parts[0], 4 * pairs)
                mod(i, 3, first)
                product(i, 0)
                hidden_lo(2 * i, 0)
                product(i, 1)

            trip(0, True, False)
            with K.loop(dve, 1, pairs - 1) as i:
                trip(i, False, False)
            trip(pairs - 1, False, True)
            weight_lo(K, dve, 0, 1, out.parts[0], 4 * pairs + 1)
            hidden_lo(FT - 1, 1)
            post_gain_dve(K, dve, layer, which, 0.5)
            out.dve(dve, skip=2)
    K.end_phase()



XBC_T, Z_T, GRP_T = 12, 8, 4
DT0 = XBC_T * P
Z0 = DT0 + 32
CONF0 = Z0 + Z_T * P
SC0 = CONF0 + 2 * GRP_T * P
CONF_HALO, SC_TAPS, XBC_TAPS, CONF_TAPS = 15, 3, 5, 31
ROWS = (TOK - CTX) // GRID

HALVES = [(kind, 2 * pair + half) for kind, pair in
          (("gate", 0), ("value", 0), ("gate", 1), ("value", 1), ("z", 0), ("z", 1), ("z", 2), ("z", 3),
           ("sc_c", 0), ("sc_h", 0), ("sc_b", 0), ("sc_c", 1), ("sc_h", 1), ("sc_b", 1),
           ("xbc", 0), ("xbc", 1), ("xbc", 2), ("xbc", 3), ("xbc", 4), ("xbc", 5)) for half in range(2)]
COLUMN = {"value": CONF0, "gate": CONF0 + GRP_T * P, "z": Z0, "sc_b": SC0, "sc_c": SC0 + GRP_T * P,
          "sc_h": SC0 + 2 * GRP_T * P, "xbc": 0}
READER = {"gate": "act", "z": "act", "sc_c": "act", "xbc": "act", "value": "dve", "sc_h": "dve", "sc_b": "dve"}
NH = len(HALVES)
CONV_FROM, CONV_STEP = 5, 6
LN_MEAN, LN_CENTRE, LN_SQ, LN_RSTD, LN_APPLY = 28, 30, 31, 36, 38


def reads(n, who):
    return sum(READER[kind] == who for kind, _ in HALVES[:n + 1])


def w_in_panel(K, layer, p):
    kind, tile = HALVES[2 * p]
    return panel_src(K.w_in[layer], 0, 8, COLUMN[kind] + P * tile), 8


def mixer_first(K, layer):
    return [w_in_panel(K, layer, 0), w_in_panel(K, layer, 1)]


def project(K, M, layer, last, following):
    nc = K.nc
    part = LATENT if last else FULL
    p0, pn = part
    seqs = (1,) if last else (0, 1)
    with ExitStack() as mem:
        def sb(name, shape, dt=F32):
            return mem.enter_context(nc.sbuf_tensor(f"{name}_{layer}", shape, dt))
        uh, ul = sb("mix_uh", [P, 8, TOK], F32R), sb("mix_ul", [P, 8, TOK], F32R)
        cpad = sb("conf_pad_ctx", [P, GRP_T, CTX + 2 * CONF_HALO])
        xpad = sb("conf_pad_x", [P, GRP_T, ROWS, GRID + 2 * CONF_HALO])
        conf = M.yc
        spc = sb("sc_pad_ctx", [P, 2, CTX + 2])
        spx = sb("sc_pad_x", [P, 2, TOK - CTX + 2 * GRID])
        gate = sb("gate", [P, 2, TOK])
        bpad = sb("xbc_pad", [P, 2, 2, CTX + 4])
        acc = sb("conv_acc", [P, 2, TOK])
        wdt = sb("wdt", [P, 8, 32])
        wdh, wdl = sb("wdh", [P, 8, 32], F32R), sb("wdl", [P, 8, 32], F32R)
        block = mem.enter_context(nc.Block(no_gpsimd_drain=True))
        par = K.par[:, layer]

        @block.sync
        def _(sp):
            src = K.w_in[layer][:, DT0:DT0 + 32].rearrange("(k p) n -> p k n", p=P)
            sp.dma_start(wdt[:, :, :], src).then_inc(K.dtw_in.inc(16), 16)
            for p in range(NH // 2):
                panel = w_in_panel(K, layer, p + 2) if p + 2 < NH // 2 else following[p + 2 - NH // 2]
                sp.wait_ge(K.lo_done.sem, K.lo_done.at(2 * p + 2))
                load_panel(K, sp, p % 2, *panel)

        @block.gpsimd
        def _(pool):
            for pad in (cpad, xpad, spc, spx, bpad):
                nc.gpsimd.memset(pad[:], 0.0).then_inc(K.pads_zero.inc(), 1)

        @block.tensor
        def _(pe):
            for n, (kind, tile) in enumerate(HALVES):
                if n >= 4:
                    who = READER[HALVES[n - 4][0]]
                    read = K.act_read if who == "act" else K.dve_read
                    pe.wait_ge(read.sem, read.at(reads(n - 4, who)))
                product_half(K, pe, K.bank[n % 4], n % 2, 8, lambda k: uh[:, k, :], lambda k: ul[:, k, :],
                             FULL if kind == "xbc" else part, True, True, n, (K.ul_ready, 0) if n == 0 else None)
                if n == 20:
                    pe.wait_ge(K.dtw_ready.sem, K.dtw_ready.at(1))
                    for t in range(TT):
                        for k in range(8):
                            tok = slice(t * P, t * P + P)
                            for x, w in ((uh, wdh), (ul, wdh), (uh, wdl)):
                                ins = nc.tensor.matmul(K.bank[4][:, 32 * t:32 * t + 32], x[:, k, tok], w[:, k, :],
                                                       start=k == 0 and w is wdh and x is uh, stop=k == 7 and w is wdl)
                    ins.then_inc(K.dt_raw.inc(), 1)
                if n == LN_MEAN:
                    pe.wait_ge(K.conv_done.sem, K.conv_done.at(GRP_T * len(seqs)))
                    for t in range(GRP_T):
                        ins = nc.tensor.matmul(K.bank[7][:, 0:pn], K.ones[:, :], conf[:, t, p0:p0 + pn], start=t == 0, stop=t == GRP_T - 1)
                    ins.then_inc(K.mean_ready.inc(), 1)
                if n in (LN_SQ, LN_SQ + 2):
                    for t in (0, 1) if n == LN_SQ else (2, 3):
                        stats_pe(K, pe, K.sq[:, t % 2, :], part, t, GRP_T, t)
                if n == LN_RSTD:
                    rstd_pe(K, pe, part, 1)

        @block.scalar
        def _(act):
            prenorm_act(K, act, layer, 1, FULL, acc, uh)
            act.wait_ge(K.pads_zero.sem, K.pads_zero.at(5))
            for n in range(NH + 2):
                if 2 <= n < NH:
                    weight_hi(K, act, n // 4, n // 2 % 2, n % 2, 8, n)
                if n == 2:
                    act.wait_ge(K.dtw_in.sem, K.dtw_in.at(16))
                    nc.scalar.activation(wdh[:, :, :], wdt[:, :, :], ACT.Copy).then_inc(K.dtw_hi.inc(), 1)
                if n == LN_SQ or n == LN_SQ + 1:
                    for t in (0, 1) if n == LN_SQ else (2, 3):
                        act.wait_ge(K.cent_ready.sem, K.cent_ready.at(t + 1))
                        act.wait_ge(K.stat_done.sem, K.stat_done.at(t - 1))
                        ins = nc.scalar.activation(K.sq[:, t % 2, 0:pn], conf[:, t, p0:p0 + pn], ACT.Square)
                        ins.then_inc(K.sq_ready.inc(), 1)
                if n == LN_RSTD:
                    rstd_act(K, act, part, 1)
                if n == LN_APPLY:
                    for t in range(GRP_T):
                        act.wait_ge(K.ln_ready.sem, K.ln_ready.at(t + 1))
                        ins = nc.scalar.activation(conf[:, t, p0:p0 + pn], conf[:, t, p0:p0 + pn], ACT.Silu,
                                                                        scale=par[:, 2, 76 + t:77 + t], bias=par[:, 2, 80 + t:81 + t])
                        ins.then_inc(K.act_step.inc(), 1)
                if n < 2:
                    continue
                kind, tile = HALVES[n - 2]
                bank = K.bank[(n - 2) % 4]
                if READER[kind] == "act":
                    act.wait_ge(K.half_done.sem, K.half_done.at(n - 1))
                if kind == "gate":
                    if n >= 6:
                        act.wait_ge(K.dve_read.sem, K.dve_read.at(tile - 1))
                    ins = nc.scalar.activation(gate[:, tile % 2, 0:pn], bank[:, 0:pn], ACT.Sigmoid)
                    ins.then_inc(K.act_read.inc(), 1)
                elif kind == "sc_c":
                    act.wait_ge(K.dve_read.sem, K.dve_read.at(reads(n - 6, "dve")))
                    ins = nc.scalar.activation(gate[:, tile % 2, 0:pn], bank[:, 0:pn], ACT.Copy)
                    ins.then_inc(K.act_read.inc(), 1)
                elif kind == "z":
                    ins = nc.scalar.activation(M.z[:, tile, p0:p0 + pn], bank[:, 0:pn], ACT.Silu)
                    ins.then_inc(K.act_read.inc(), 1)
                elif kind == "xbc":
                    if tile >= 2:
                        act.wait_ge(K.xbc_conv.sem, K.xbc_conv.at(tile - 1))
                    ins = nc.scalar.activation(bpad[:, tile % 2, :, 2:2 + CTX],
                                                             bank[:, :].rearrange("p (s n) -> p s n", s=2), ACT.Copy)
                    ins.then_inc(K.act_read.inc(), 1)
                    if tile >= 1:
                        act.wait_ge(K.xbc_conv.sem, K.xbc_conv.at(tile))
                        ins = nc.scalar.activation(M.xbc[:, tile - 1, :], acc[:, (tile - 1) % 2, :], ACT.Silu)
                        ins.then_inc(K.xbc_out.inc(), 1)
            act.wait_ge(K.xbc_conv.sem, K.xbc_conv.at(XBC_T))
            ins = nc.scalar.activation(M.xbc[:, XBC_T - 1, :], acc[:, (XBC_T - 1) % 2, :], ACT.Silu)
            ins.then_inc(K.xbc_out.inc(), 1)

        @block.vector
        def _(dve):
            def taps(tensors, weights, bias, steps, signal=None):
                for k in steps:
                    for i, (out, src) in enumerate(tensors):
                        if k == 0:
                            ins = nc.vector.tensor_scalar(out, src(k), weights(k), bias, ALU.mult, ALU.add)
                        else:
                            dve.wait_ge(K.dve_step.sem, K.dve_step.own(len(tensors) - 1 - (i if signal else 0)))
                            ins = nc.vector.scalar_tensor_tensor(out, src(k), weights(k), out, ALU.mult, ALU.add)
                        ins.then_inc((signal or K.dve_step).inc(), 1)

            def conf_tap(t, k):
                ctx = (conf[:, t, 0:CTX], lambda k: cpad[:, t, k:k + CTX])
                lat = (conf[:, t, CTX:TOK].rearrange("p (r c) -> p r c", c=GRID), lambda k: xpad[:, t, :, k:k + GRID])
                taps([lat] if last else [ctx, lat], lambda k: par[:, 1, 4 * k + t:4 * k + t + 1], par[:, 2, 72 + t:73 + t], [k],
                     K.conv_done if k == CONF_TAPS - 1 else None)

            prenorm_dve(K, dve, layer, 1, FULL, acc, uh, ul)
            for n in range(NH + 2):
                if 2 <= n < NH:
                    weight_lo(K, dve, n // 2 % 2, n % 2, 8, n)
                if n == 2:
                    dve.wait_ge(K.dtw_hi.sem, K.dtw_hi.at(1))
                    ins = nc.vector.tensor_tensor(wdl[:, :, :], wdt[:, :, :], r32(wdh[:, :, :]), ALU.subtract)
                    ins.then_inc(K.dtw_ready.inc(), 1)
                    dve.wait_ge(K.pads_zero.sem, K.pads_zero.at(5))
                if n >= 2:
                    kind, tile = HALVES[n - 2]
                    bank = K.bank[(n - 2) % 4]
                    if READER[kind] == "dve":
                        dve.wait_ge(K.half_done.sem, K.half_done.at(n - 1))
                    if kind in ("value", "sc_h"):
                        dve.wait_ge(K.act_read.sem, K.act_read.at(reads(n - 4, "act")))
                        for s in seqs:
                            a = s * CTX - p0
                            src, g = bank[:, a:a + CTX], gate[:, tile % 2, a:a + CTX]
                            if kind == "value" and s == 0:
                                out = cpad[:, tile, CONF_HALO:CONF_HALO + CTX]
                            elif kind == "value":
                                out = xpad[:, tile, :, CONF_HALO:CONF_HALO + GRID]
                                src, g = (v.rearrange("p (r c) -> p r c", c=GRID) for v in (src, g))
                            elif s == 0:
                                out = spc[:, tile % 2, 1:1 + CTX]
                            else:
                                out = spx[:, tile % 2, GRID:GRID + CTX]
                            ins = nc.vector.tensor_tensor(out, src, g, ALU.mult)
                            if s == 0:
                                ins.then_inc(K.dve_step.inc(), 1)
                                dve.wait_ge(K.dve_step.sem, K.dve_step.own())
                        ins.then_inc(K.dve_read.inc(), 1)
                    elif kind == "sc_b":
                        j, buf = tile, tile % 2
                        dve.wait_ge(K.dve_read.sem, K.dve_read.own())
                        ctx = (M.ys[:, j, 0:CTX], lambda k: spc[:, buf, k:k + CTX])
                        lat = (M.ys[:, j, CTX:TOK], lambda k: spx[:, buf, k * GRID:k * GRID + CTX])
                        taps([lat] if last else [ctx, lat], lambda k: par[:, 2, 84 + 4 * k + j:85 + 4 * k + j],
                             par[:, 2, 96 + j:97 + j], range(SC_TAPS))
                        dve.wait_ge(K.dve_step.sem, K.dve_step.own())
                        ins = nc.vector.tensor_tensor(M.ys[:, j, p0:p0 + pn], M.ys[:, j, p0:p0 + pn], bank[:, 0:pn], ALU.mult)
                        ins.then_inc(K.dve_read.inc(), 1)
                if n == 23:
                    dve.wait_ge(K.dt_raw.sem, K.dt_raw.at(1))
                    bias = K.dtb[:, layer, :].unsqueeze(1).to_broadcast([P, TT, 32])
                    ins = nc.vector.tensor_tensor(M.dt[:, :, :], K.bank[4][:, 0:P].rearrange("p (t h) -> p t h", t=TT), bias, ALU.add)
                    ins.then_inc(K.dt_out.inc(), 1)
                for i in range(CONV_STEP * (n - CONV_FROM), min(CONV_STEP * (n - CONV_FROM + 1), GRP_T * CONF_TAPS)):
                    if i >= 0:
                        t, k = i // CONF_TAPS, i % CONF_TAPS
                        if k == 0:
                            dve.wait_ge(K.dve_read.sem, K.dve_read.at(t + 1))
                        conf_tap(t, k)
                if n == LN_CENTRE:
                    dve.wait_ge(K.mean_ready.sem, K.mean_ready.at(1))
                    for t in range(GRP_T):
                        ins = nc.vector.scalar_tensor_tensor(conf[:, t, p0:p0 + pn], K.bank[7][:, 0:pn], -1.0 / (GRP_T * P),
                                                                             conf[:, t, p0:p0 + pn], ALU.mult, ALU.add)
                        ins.then_inc(K.cent_ready.inc(), 1)
                if n == LN_RSTD:
                    rstd_dve(K, dve, part, GRP_T * P, GRP_T, 1)
                if n == LN_APPLY:
                    dve.wait_ge(K.rb_ready.sem, K.rb_ready.at(1))
                    for t in range(GRP_T):
                        ins = nc.vector.tensor_tensor(conf[:, t, p0:p0 + pn], conf[:, t, p0:p0 + pn], K.bank[6][:, 0:pn], ALU.mult)
                        ins.then_inc(K.ln_ready.inc(), 1)
                if n >= 2 and HALVES[n - 2][0] == "xbc":
                    t = HALVES[n - 2][1]
                    dve.wait_ge(K.act_read.sem, K.act_read.at(reads(n - 2, "act")))
                    if t >= 2:
                        dve.wait_ge(K.xbc_out.sem, K.xbc_out.at(t - 1))
                    view = acc[:, t % 2, :].rearrange("p (s n) -> p s n", s=2)
                    taps([(view, lambda k: bpad[:, t % 2, :, k:k + CTX])],
                         lambda k: par[:, 2, 12 * k + t:12 * k + t + 1], par[:, 2, 60 + t:61 + t], range(XBC_TAPS - 1))
                    k = XBC_TAPS - 1
                    dve.wait_ge(K.dve_step.sem, K.dve_step.own())
                    ins = nc.vector.scalar_tensor_tensor(view, bpad[:, t % 2, :, k:k + CTX], par[:, 2, 12 * k + t:12 * k + t + 1],
                                                                       view, ALU.mult, ALU.add)
                    ins.then_inc(K.xbc_conv.inc(), 1)
    K.end_phase()



HEADS, HD, GH = 16, 64, 8
CHUNKS = 2


class ScanPlan:

    def __init__(self, last):
        self.seqs = (0, 1)
        self.with_y = {0: not last, 1: True}
        self.states = {0: [(0, 0), (1, 0), (1, 1), (0, 1)], 1: [(0, 0), (1, 1)]}

    @staticmethod
    def prev(seq, c, d):
        first = c == 0 if d == 0 else c == 1
        if first:
            return None if seq == 0 else "init"
        return "mid"


def scan(K, M, layer, last):
    nc = K.nc
    plan = ScanPlan(last)
    with ExitStack() as mem:
        def sb(name, shape, dt=F32):
            return mem.enter_context(nc.sbuf_tensor(f"{name}_{layer}", shape, dt))
        small = lambda name: sb(name, [P, TT, 2, HEADS])
        t_abs, t_e, t_u, t_ln, t_d, t_z = (small(n) for n in ("dt_abs", "dt_e", "dt_u", "dt_ln", "dt_d", "dt_z"))
        dt, a = small("dt_f"), small("dt_a")
        ea = sb("exp_alog", [P, 32])
        cum = sb("cum", [P, 2, TT, HEADS])
        neg = sb("neg_cum", [P, 2, TT, HEADS])
        tot = sb("tot", [P, TT, 2, HEADS])
        dec = sb("dec", [P, TT, 2, HEADS])
        ecum, etot = sb("exp_cum", [P, 2, TT, HEADS]), sb("exp_tot", [P, TT, 2, HEADS])
        xd = sb("xd", [P, CHUNKS, 2, HEADS, HD])
        xw = sb("xw", [P, HEADS, HD])
        btm = sb("b_tm", [P, CHUNKS, 2 * P])
        init = sb("state_init", [P, 2, HEADS, HD])
        mid = sb("state_mid", [P, 2, HEADS, HD])
        cbt = sb("cb", [P, 2, P])
        e = sb("decay", [P, 2, 4, P])
        m = sb("weights", [P, 2, 4, P])
        ytm = sb("y_tm", [P, HEADS, HD])
        tmp = sb("off", [P, 2, GH, HD])
        gt = sb("gated", [P, 4, P])
        block = mem.enter_context(nc.Block(no_gpsimd_drain=True))
        bh = lambda ap, n: ap.unsqueeze(2).to_broadcast([P, n, HD])
        fm = lambda tile, t: M.xbc[:, tile, t * P:t * P + P]
        state = {"init": init, "mid": mid}

        @block.tensor
        def _(pe):
            pe.wait_ge(K.dt_ready.sem, K.dt_ready.at(1))
            for d in range(2):
                nc.tensor.matmul(K.bank[4][:, 64 * d:64 * d + 64], K.tri[:, d, :], a[:, :, d, :], start=True, stop=True)
            ins = nc.tensor.matmul(K.bank[4][:, P:2 * P], K.ones[:, :], a[:, :, :, :].rearrange("p t d h -> p (t d h)"),
                                                  start=True, stop=True)
            ins.then_inc(K.cum_ready.inc(), 1)
            turns = states = units = offs = gs = 0
            for seq in plan.seqs:
                for c in range(CHUNKS):
                    t = 2 * seq + c
                    pe.wait_ge(K.ytm_ready.sem, K.ytm_ready.at(gs))
                    pe.wait_ge(K.xd_ready.sem, K.xd_ready.at(4 * turns))
                    for j in range(8):
                        ins = nc.tensor.transpose(K.bank[j // 4][:, j % 4 * P:j % 4 * P + P], fm(j, t), K.ident[:, :])
                    ins.then_inc(K.xs_turned.inc(), 1)
                    pe.wait_ge(K.cb_ready.sem, K.cb_ready.at(units // 8))
                    pe.wait_ge(K.b_ready.sem, K.b_ready.at(turns))
                    for g in range(2):
                        ins = nc.tensor.transpose(K.bank[5][:, g * P:g * P + P], fm(8 + g, t), K.ident[:, :])
                    ins.then_inc(K.b_turned.inc(), 1)
                    turns += 1
                pe.wait_ge(K.b_ready.sem, K.b_ready.at(turns))
                pe.wait_ge(K.e_ready.sem, K.e_ready.at(units))
                for c, d in plan.states[seq]:
                    pe.wait_ge(K.xw_ready.sem, K.xw_ready.at(states + 1))
                    pe.wait_ge(K.st_ready.sem, K.st_ready.at(states))
                    for g in range(2):
                        ins = nc.tensor.matmul(K.bank[2 + g][:, :], btm[:, c, g * P:g * P + P],
                                               xw[:, GH * g:GH * g + GH, :].rearrange("p h n -> p (h n)"), start=True, stop=True)
                    ins.then_inc(K.state_mm.inc(), 1)
                    states += 1
                pe.wait_ge(K.st_ready.sem, K.st_ready.at(states))
                if not plan.with_y[seq]:
                    continue
                pe.wait_ge(K.xd_ready.sem, K.xd_ready.at(4 * turns))
                for c in range(CHUNKS):
                    t = 2 * seq + c
                    pe.wait_ge(K.cb_ready.sem, K.cb_ready.at(units // 8))
                    for g in range(2):
                        ins = nc.tensor.matmul(K.bank[5][:, g * P:g * P + P], fm(8 + g, t), fm(10 + g, t), start=True, stop=True)
                    ins.then_inc(K.cb_mm.inc(), 1)

                    def decay(u):
                        g, d, h = u // 4, u % 2, 4 * (u // 2)
                        bank = K.bank[2 + u % 2]
                        pe.wait_ge(K.e_ready.sem, K.e_ready.at(units + u - 1))
                        nc.tensor.matmul(bank[:, :], K.identb[:, :], K.mask[:, d, :].unsqueeze(1).to_broadcast([P, 4, P]),
                                         start=True, stop=False, skip_group_check=True)
                        for i in range(4):
                            ins = nc.tensor.matmul(bank[:, i * P:i * P + P], a[:, t, d, h + i:h + i + 1].to_broadcast([P, P]),
                                                   K.tri[:, d, :], start=False, stop=True, skip_group_check=True)
                        ins.then_inc(K.diff_ready.inc(), 1)

                    def off(g):
                        nonlocal offs
                        for d in range(2):
                            prev = plan.prev(seq, c, d)
                            if prev:
                                pe.wait_ge(K.off_used.sem, K.off_used.at(offs - 1))
                                ins = nc.tensor.matmul(
                                          K.bank[6 + offs % 2][:, :], fm(10 + g, t),
                                          state[prev][:, d, GH * g:GH * g + GH, :].rearrange("p h n -> p (h n)"), start=True, stop=True)
                                ins.then_inc(K.off_mm.inc(), 1)
                                offs += 1

                    def y_turn(g):
                        pe.wait_ge(K.ytm_ready.sem, K.ytm_ready.at(gs + g + 1))
                        pe.wait_ge(K.g_ready.sem, K.g_ready.at(gs + g))
                        for i in range(4):
                            h = GH * g + 2 * i
                            ins = nc.tensor.transpose(K.bank[4][:, i * P:i * P + P],
                                                      ytm[:, h:h + 2, :].rearrange("p h n -> p (h n)"), K.ident[:, :])
                        ins.then_inc(K.y_turned.inc(), 1)

                    decay(0)
                    decay(1)
                    off(0)
                    for u in range(8):
                        g, d = u // 4, u % 2
                        pe.wait_ge(K.m_ready.sem, K.m_ready.at(units + u + 1))
                        if u % 4 == 0:
                            pe.wait_ge(K.ytm_ready.sem, K.ytm_ready.at(gs + g - 1))
                        for i in range(4):
                            h = 4 * (u // 2) + i
                            ins = nc.tensor.matmul(K.bank[g][:, (h - GH * g) * HD:(h - GH * g + 1) * HD], m[:, u % 2, i, :],
                                                   xd[:, c, d, h, :], start=u % 4 == 0 and i == 0, stop=u % 4 >= 2,
                                                   skip_group_check=True)
                        ins.then_inc(K.y_mm.inc(), 1)
                        if u + 2 < 8:
                            decay(u + 2)
                        if u == 3:
                            off(1)
                        if u == 6:
                            y_turn(0)
                    y_turn(1)
                    units += 8
                    gs += 2

        @block.scalar
        def _(act):
            flat = lambda ap: ap.rearrange("p t d h -> p (t d h)")
            act.wait_ge(K.dt_abs.sem, K.dt_abs.at(1))
            nc.scalar.activation(flat(t_e[:]), flat(t_abs[:]), ACT.Exp, scale=-1.0).then_inc(K.dt_exp.inc(), 1)
            nc.scalar.activation(ea[:, :], K.alog[:, layer, :], ACT.Exp).then_inc(K.a_exp.inc(), 1)
            act.wait_ge(K.dt_u.sem, K.dt_u.at(1))
            nc.scalar.activation(flat(t_ln[:]), flat(t_u[:]), ACT.Ln).then_inc(K.dt_ln.inc(), 1)
            act.wait_ge(K.cum_read.sem, K.cum_read.at(1))
            nc.scalar.activation(flat(dec[:]), flat(dec[:]), ACT.Exp)
            nc.scalar.activation(flat(ecum[:]), flat(cum[:]), ACT.Exp)
            nc.scalar.activation(flat(etot[:]), flat(tot[:]), ACT.Exp).then_inc(K.decay_ready.inc(), 1)
            turns = units = 0
            for seq in plan.seqs:
                for c in range(CHUNKS):
                    act.wait_ge(K.b_turned.sem, K.b_turned.at(turns + 1))
                    nc.scalar.activation(btm[:, c, :], K.bank[5][:, 0:2 * P], ACT.Copy).then_inc(K.b_ready.inc(), 1)
                    turns += 1
                if not plan.with_y[seq]:
                    continue
                for c in range(CHUNKS):
                    t = 2 * seq + c
                    act.wait_ge(K.cb_mm.sem, K.cb_mm.at(units // 8 + 1))
                    act.wait_ge(K.m_ready.sem, K.m_ready.at(units))
                    ins = nc.scalar.activation(cbt[:, :, :].rearrange("p g l -> p (g l)"), K.bank[5][:, 0:2 * P], ACT.Copy)
                    ins.then_inc(K.cb_ready.inc(), 1)
                    for u in range(8):
                        d = u % 2
                        act.wait_ge(K.diff_ready.sem, K.diff_ready.at(units + u + 1))
                        act.wait_ge(K.m_ready.sem, K.m_ready.at(units + u - 1))
                        for i in range(4):
                            h = 4 * (u // 2) + i
                            ins = nc.scalar.activation(e[:, u % 2, i, :], K.bank[2 + u % 2][:, i * P:i * P + P], ACT.Exp,
                                                       bias=neg[:, d, t, h:h + 1])
                        ins.then_inc(K.e_ready.inc(), 1)
                    units += 8

        @block.gpsimd
        def _(pool):
            turns = states = 0
            for seq in plan.seqs:
                turns += CHUNKS
                for c, d in plan.states[seq]:
                    pool.wait_ge(K.decay_ready.sem, K.decay_ready.at(1))
                    pool.wait_ge(K.xd_ready.sem, K.xd_ready.at(4 * turns))
                    pool.wait_ge(K.state_mm.sem, K.state_mm.at(states))
                    ins = nc.gpsimd.tensor_tensor(xw[:, :, :], xd[:, c, d, :, :], bh(dec[:, 2 * seq + c, d, :], HEADS), ALU.mult)
                    ins.then_inc(K.xw_ready.inc(), 1)
                    states += 1

        @block.vector
        def _(dve):
            V = nc.vector
            flat = lambda ap: ap.rearrange("p t d h -> p (t d h)")
            raw = M.dt[:, :, :].rearrange("p t h -> p (t h)")
            V.scalar_tensor_tensor(flat(t_abs[:]), raw, -1.0, raw, ALU.mult, ALU.max).then_inc(K.dt_abs.inc(), 1)
            dve.wait_ge(K.dt_exp.sem, K.dt_exp.at(1))
            V.tensor_scalar(flat(t_u[:]), flat(t_e[:]), 1.0, None, ALU.add).then_inc(K.dt_u.inc(), 1)
            dve.wait_ge(K.dt_u.sem, K.dt_u.own())
            V.tensor_scalar(flat(t_d[:]), flat(t_u[:]), -1.0, None, ALU.add).then_inc(K.dve_step.inc(), 1)
            dve.wait_ge(K.dve_step.sem, K.dve_step.own())
            V.tensor_scalar(flat(t_z[:]), flat(t_d[:]), 0.0, None, ALU.is_equal).then_inc(K.dve_step.inc(), 1)
            dve.wait_ge(K.dve_step.sem, K.dve_step.own())
            V.tensor_tensor(flat(t_d[:]), flat(t_d[:]), flat(t_z[:]), ALU.add).then_inc(K.dve_step.inc(), 1)
            dve.wait_ge(K.dve_step.sem, K.dve_step.own())
            V.reciprocal(flat(t_d[:]), flat(t_d[:])).then_inc(K.dve_step.inc(), 1)
            dve.wait_ge(K.dve_step.sem, K.dve_step.own())
            V.tensor_tensor(flat(t_d[:]), flat(t_d[:]), flat(t_e[:]), ALU.mult).then_inc(K.dve_step.inc(), 1)
            dve.wait_ge(K.dve_step.sem, K.dve_step.own())
            dve.wait_ge(K.dt_ln.sem, K.dt_ln.at(1))
            V.tensor_tensor(flat(t_ln[:]), flat(t_ln[:]), flat(t_d[:]), ALU.mult).then_inc(K.dve_step.inc(), 1)
            dve.wait_ge(K.dve_step.sem, K.dve_step.own())
            V.tensor_tensor(flat(t_z[:]), flat(t_z[:]), flat(t_e[:]), ALU.mult).then_inc(K.dve_step.inc(), 1)
            dve.wait_ge(K.dve_step.sem, K.dve_step.own())
            V.tensor_tensor(flat(t_ln[:]), flat(t_ln[:]), flat(t_z[:]), ALU.add).then_inc(K.dve_step.inc(), 1)
            dve.wait_ge(K.dve_step.sem, K.dve_step.own())
            ins = V.scalar_tensor_tensor(flat(dt[:]), raw, 0.0, flat(t_ln[:]), ALU.max, ALU.add)
            ins.then_inc(K.dve_step.inc(), 1)
            dve.wait_ge(K.dve_step.sem, K.dve_step.own())
            dve.wait_ge(K.a_exp.sem, K.a_exp.at(1))
            ins = V.scalar_tensor_tensor(a[:].rearrange("p t d h -> p t (d h)"), dt[:].rearrange("p t d h -> p t (d h)"), -1.0,
                                                       ea[:, :].unsqueeze(1).to_broadcast([P, TT, 32]), ALU.mult, ALU.mult)
            ins.then_inc(K.dt_ready.inc(), 1)
            dve.wait_ge(K.cum_ready.sem, K.cum_ready.at(1))
            V.tensor_copy(flat(cum[:]), K.bank[4][:, 0:P]).then_inc(K.dve_step.inc(), 1)
            dve.wait_ge(K.dve_step.sem, K.dve_step.own())
            V.tensor_copy(flat(tot[:]), K.bank[4][:, P:2 * P]).then_inc(K.dve_step.inc(), 1)
            dve.wait_ge(K.dve_step.sem, K.dve_step.own())
            V.tensor_scalar(flat(neg[:]), flat(cum[:]), -1.0, None, ALU.mult).then_inc(K.dve_step.inc(), 1)
            dve.wait_ge(K.dve_step.sem, K.dve_step.own())
            for d in range(2):
                ins = V.tensor_tensor(dec[:, :, d, :], tot[:, :, d, :], neg[:, d, :, :], ALU.add)
            ins.then_inc(K.cum_read.inc(), 1)

            turns = states = units = offs = gs = 0
            for seq in plan.seqs:
                for c in range(CHUNKS):
                    dve.wait_ge(K.xs_turned.sem, K.xs_turned.at(turns + 1))
                    for d in range(2):
                        for g in range(2):
                            ins = V.tensor_tensor(
                                      xd[:, c, d, GH * g:GH * g + GH, :], K.bank[g][:, :].rearrange("p (h n) -> p h n", n=HD),
                                      bh(dt[:, 2 * seq + c, d, GH * g:GH * g + GH], GH), ALU.mult)
                            ins.then_inc(K.xd_ready.inc(), 1)
                    turns += 1
                for c, d in plan.states[seq]:
                    prev = plan.prev(seq, c, d)
                    target = mid if (c == 0) == (d == 0) else init
                    if prev:
                        dve.wait_ge(K.decay_ready.sem, K.decay_ready.at(1))
                        dve.wait_ge(K.st_ready.sem, K.st_ready.own())
                        ins = V.tensor_tensor(target[:, d, :, :], state[prev][:, d, :, :], bh(etot[:, 2 * seq + c, d, :], HEADS), ALU.mult)
                        ins.then_inc(K.dve_step.inc(), 1)
                        dve.wait_ge(K.dve_step.sem, K.dve_step.own())
                    dve.wait_ge(K.state_mm.sem, K.state_mm.at(states + 1))
                    for g in range(2):
                        half = target[:, d, GH * g:GH * g + GH, :].rearrange("p h n -> p (h n)")
                        ins = V.tensor_tensor(half, half, K.bank[2 + g][:, :], ALU.add) if prev else V.tensor_copy(half, K.bank[2 + g][:, :])
                    ins.then_inc(K.st_ready.inc(), 1)
                    states += 1
                if not plan.with_y[seq]:
                    continue
                for c in range(CHUNKS):
                    t = 2 * seq + c

                    def sums(g):
                        nonlocal offs
                        y = ytm[:, GH * g:GH * g + GH, :]
                        y_flat = y.rearrange("p h n -> p (h n)")
                        dve.wait_ge(K.y_mm.sem, K.y_mm.at(units + 4 * g + 4))
                        dve.wait_ge(K.y_turned.sem, K.y_turned.at(gs + g - 1))
                        entering = [d for d in range(2) if plan.prev(seq, c, d)]
                        for d in entering:
                            dve.wait_ge(K.off_mm.sem, K.off_mm.at(offs + 1))
                            ins = V.tensor_tensor(tmp[:, d, :, :], K.bank[6 + offs % 2][:, :].rearrange("p (h n) -> p h n", n=HD),
                                                                bh(ecum[:, d, t, GH * g:GH * g + GH], GH), ALU.mult)
                            ins.then_inc(K.off_used.inc(), 1)
                            dve.wait_ge(K.off_used.sem, K.off_used.own())
                            offs += 1
                            add = tmp[:, d, :, :].rearrange("p h n -> p (h n)")
                            within = K.bank[g][:, :] if d == entering[0] else y_flat
                            ins = V.tensor_tensor(y_flat, add, within, ALU.add)
                            if d == entering[-1]:
                                ins.then_inc(K.ytm_ready.inc(), 1)
                            else:
                                ins.then_inc(K.dve_step.inc(), 1)
                                dve.wait_ge(K.dve_step.sem, K.dve_step.own())

                    def gated(g):
                        dve.wait_ge(K.y_turned.sem, K.y_turned.at(gs + g + 1))
                        for i in range(4):
                            ins = V.scalar_tensor_tensor(gt[:, i, :], fm(4 * g + i, t), K.dskip[:, layer, 4 * g + i:4 * g + i + 1],
                                                         K.bank[4][:, i * P:i * P + P], ALU.mult, ALU.add)
                        ins.then_inc(K.g_ready.inc(), 1)
                        dve.wait_ge(K.g_ready.sem, K.g_ready.own())
                        z = M.z[:, 4 * g:4 * g + 4, t * P:t * P + P]
                        V.tensor_tensor(z, z, gt[:, :, :], ALU.mult).then_inc(K.dve_step.inc(), 1)

                    for u in range(8):
                        dve.wait_ge(K.cb_ready.sem, K.cb_ready.at(units // 8 + 1))
                        dve.wait_ge(K.e_ready.sem, K.e_ready.at(units + u + 1))
                        dve.wait_ge(K.y_mm.sem, K.y_mm.at(units + u - 1))
                        ins = V.tensor_tensor(m[:, u % 2, :, :], e[:, u % 2, :, :],
                                                           cbt[:, u // 4, :].unsqueeze(1).to_broadcast([P, 4, P]), ALU.mult)
                        ins.then_inc(K.m_ready.inc(), 1)
                        if u == 5:
                            sums(0)
                    gated(0)
                    sums(1)
                    gated(1)
                    units += 8
                    gs += 2
    K.end_phase()



MIX_ORDER = [(0, 1), (1, 1), (0, 0), (1, 0), (2, 0), (2, 1), (3, 0), (3, 1)]


def mix_out(K, M, layer, last, following):
    nc = K.nc
    tok = LATENT if last else FULL
    t0, tn = tok
    with ExitStack() as mem:
        def sb(name, shape, dt=F32):
            return mem.enter_context(nc.sbuf_tensor(f"{name}_{layer}", shape, dt))
        xh, xl = sb("out_xh", [P, 16, TOK], F32R), sb("out_xl", [P, 16, TOK], F32R)
        y = sb("mix_y", [P, 8, TOK])
        out = OutProduct(K, K.w_out[layer], (8, 8), MIX_ORDER, lambda k: xh[:, k, :], lambda k: xl[:, k, :],
                         tok, tok, y, 0, 0, 8, 2, True)
        block = mem.enter_context(nc.Block(no_gpsimd_drain=True))
        gain = K.par[:, layer, 2, 100:108]
        conv = lambda i: (M.yc if i < GRP_T else M.ys)[:, i % GRP_T, t0:t0 + tn]

        @block.sync
        def _(sp):
            out.sp(sp, following)

        @block.tensor
        def _(pe):
            def norm(n):
                if n in (1, 2):
                    for j in range(4 * n - 4, 4 * n):
                        stats_pe(K, pe, K.sq[:, j % 2, :], tok, j, 8, j)
                elif n == 3:
                    rstd_pe(K, pe, tok, 1)
            out.pe(pe, lambda pair: None, norm, {0: (K.xl_ready, 0), 4: (K.xl_ready, 8)})

        @block.scalar
        def _(act):
            weight_hi(K, act, 0, 0, 0, 8, 0)
            for i in range(8):
                nc.scalar.activation(xh[:, 8 + i, t0:t0 + tn], conv(i), ACT.Copy).then_inc(K.xh_ready.inc(), 1)
                if i == 4:
                    weight_hi(K, act, 0, 0, 1, 8, 1)
            for j in range(8):
                act.wait_ge(K.stat_done.sem, K.stat_done.at(j - 1))
                ins = nc.scalar.activation(K.sq[:, j % 2, 0:tn], M.z[:, j, t0:t0 + tn], ACT.Square)
                ins.then_inc(K.sq_ready.inc(), 1)
                if j == 3:
                    weight_hi(K, act, 0, 1, 0, 8, 2)
            rstd_act(K, act, tok, 1)
            weight_hi(K, act, 0, 1, 1, 8, 3)
            for j in range(8):
                act.wait_ge(K.yn_ready.sem, K.yn_ready.at(j + 1))
                ins = nc.scalar.activation(xh[:, j, t0:t0 + tn], M.z[:, j, t0:t0 + tn], ACT.Copy, scale=gain[:, j:j + 1])
                ins.then_inc(K.xh_ready.inc(), 1)
                if j in (0, 5):
                    weight_hi(K, act, 1, 0, j // 5, 8, 4 + j // 5)
            out.act(act, skip=6)

        @block.vector
        def _(dve):
            def normed(j):
                z = M.z[:, j, t0:t0 + tn]
                nc.vector.tensor_tensor(z, z, K.bank[6][:, 0:tn], ALU.mult).then_inc(K.yn_ready.inc(), 1)

            weight_lo(K, dve, 0, 0, 8, 0)
            for i in range(8):
                dve.wait_ge(K.xh_ready.sem, K.xh_ready.at(i + 1))
                ins = nc.vector.tensor_tensor(xl[:, 8 + i, t0:t0 + tn], conv(i), r32(xh[:, 8 + i, t0:t0 + tn]), ALU.subtract)
                ins.then_inc(K.xl_ready.inc(), 1)
                if i == 5:
                    weight_lo(K, dve, 0, 1, 8, 1)
            post_gain_dve(K, dve, layer, 1, 1.0)
            weight_lo(K, dve, 1, 0, 8, 2)
            rstd_dve(K, dve, tok, 8 * P, 8, 1)
            weight_lo(K, dve, 1, 1, 8, 3)
            dve.wait_ge(K.rb_ready.sem, K.rb_ready.at(1))
            normed(0)
            for j in range(8):
                if j < 7:
                    normed(j + 1)
                if j in (0, 5):
                    weight_lo(K, dve, 0, j // 5, 8, 4 + j // 5)
                dve.wait_ge(K.xh_ready.sem, K.xh_ready.at(9 + j))
                dve.wait_ge(K.yn_ready.sem, K.yn_ready.at(j + 1))
                ins = nc.vector.scalar_tensor_tensor(xl[:, j, t0:t0 + tn], M.z[:, j, t0:t0 + tn], gain[:, j:j + 1],
                                                     r32(xh[:, j, t0:t0 + tn]), ALU.mult, ALU.subtract)
                ins.then_inc(K.xl_ready.inc(), 1)
            out.dve(dve, skip=6)
    K.end_phase()


def mixer(K, layer, last, following):
    nc = K.nc
    M = Kern()
    with ExitStack() as mem:
        def sb(name, shape, dt=F32):
            return mem.enter_context(nc.sbuf_tensor(f"{name}_{layer}", shape, dt))
        M.xbc = sb("xbc", [P, XBC_T, TOK])
        M.z = sb("z", [P, Z_T, TOK])
        M.yc, M.ys = sb("yc", [P, GRP_T, TOK]), sb("ys", [P, GRP_T, TOK])
        M.dt = sb("dt_raw", [P, TT, 32])
        w_out_first = [(panel_src(K.w_out[layer], 8 * part, 8, 2 * P * pair), 8) for pair, part in MIX_ORDER[:2]]
        project(K, M, layer, last, w_out_first)
        if K.stop == "proj":
            return
        scan(K, M, layer, last)
        mix_out(K, M, layer, last, following)



PACKS = 3


def param_rows(K, layer):
    I = K.inputs
    rows = lambda ap: ap.rearrange("(a p) -> a p", p=P)
    return [
        (0, 0, rows(I["b_mod"][layer])),
        (0, 72, I["norm_pre"][layer].rearrange("w (a p) -> (w a) p", p=P)),
        (0, 96, I["norm_post"][layer].rearrange("w (a p) -> (w a) p", p=P)),
        (1, 0, I["conf_conv_w"][layer].rearrange("k (a p) -> (k a) p", p=P)),
        (2, 0, I["ssd_conv_w"][layer].rearrange("k (a p) -> (k a) p", p=P)),
        (2, 60, rows(I["ssd_conv_b"][layer])),
        (2, 72, rows(I["conf_conv_b"][layer])),
        (2, 76, rows(I["conf_ln_g"][layer])),
        (2, 80, rows(I["conf_ln_b"][layer])),
        (2, 84, I["sc_conv_w"][layer].rearrange("k (a p) -> (k a) p", p=P)),
        (2, 96, rows(I["sc_conv_b"][layer])),
        (2, 100, rows(I["ssd_norm"][layer])),
    ]


PACK_ROWS = (120, 124, 108)


def opening(K, following):
    nc, I = K.nc, K.inputs
    L = K.layers
    with ExitStack() as mem:
        xt = mem.enter_context(nc.sbuf_tensor("xt", [P, TT, 8 * P], F32))
        pr = mem.enter_context(nc.sbuf_tensor("pr", [P, L * PACKS, P], F32))
        cr = mem.enter_context(nc.sbuf_tensor("cr", [16, P], F32))
        block = mem.enter_context(nc.Block(no_gpsimd_drain=True))
        x_tiles = [I["ctx"][0, t * P:(t + 1) * P, :] for t in range(2)] + [I["x"][0, t * P:(t + 1) * P, :] for t in range(2)]

        @block.sync
        def _(sp):
            sp.dma_start(cr[0:8, :], I["c_ctx"].rearrange("(a p) -> a p", p=P)).then_inc(K.cond_in.inc(16), 16)
            sp.dma_start(cr[8:16, :], I["c"][0].rearrange("(a p) -> a p", p=P)).then_inc(K.cond_in.inc(16), 16)
            for n in range(2):
                load_panel(K, sp, n, panel_src(K.w_mod[0], 0, 8, 2 * P * n), 8)
            for n in range(2, 8):
                sp.wait_ge(K.mod_lo.sem, K.mod_lo.at(2 * n - 2))
                load_panel(K, sp, n % 2, panel_src(K.w_mod[0], 0, 8, 2 * P * n), 8)
            for slot, panel in enumerate(following):
                sp.wait_ge(K.mod_lo.sem, K.mod_lo.at(14 + 2 * slot))
                load_panel(K, sp, slot, *panel)

        @block.gpsimd
        def _(pool):
            def select(out, pattern, base, mult, op, fill, after):
                pool.wait_ge(K.const_step.sem, after)
                return nc.gpsimd.affine_select(out=out, in_=out, compare_op=op, fill=fill, base=base,
                                               pattern=pattern, channel_multiplier=mult)
            nc.gpsimd.memset(K.ones[:, :], 1.0).then_inc(K.const_step.inc(), 1)
            nc.gpsimd.memset(K.ident[:, :], 0.0).then_inc(K.const_step.inc(), 1)
            nc.gpsimd.memset(K.tri[:, 0, :], 1.0).then_inc(K.const_step.inc(), 1)
            nc.gpsimd.memset(K.tri[:, 1, :], 1.0).then_inc(K.const_step.inc(), 1)
            nc.gpsimd.memset(K.mask[:, 0, :], 0.0).then_inc(K.const_step.inc(), 1)
            nc.gpsimd.memset(K.mask[:, 1, :], 0.0).then_inc(K.const_step.inc(), 1)
            nc.gpsimd.memset(K.identb[:, :], 0.0).then_inc(K.const_step.inc(), 1)
            nc.gpsimd.memset(K.cond[:, :].bitcast(F32), 0.0).then_inc(K.const_step.inc(), 1)
            nc.gpsimd.memset(K.fold[:, :], 0.0).then_inc(K.const_step.inc(), 1)
            n = K.const_step.count
            line = [[-1, P]]
            select(K.ident[:, :], line, 0, 1, ALU.not_equal, 1.0, n).then_inc(K.const_step.inc(), 1)
            select(K.identb[:, :], line, 0, 1, ALU.not_equal, 1.0, n).then_inc(K.const_step.inc(), 1)
            select(K.fold[:, :], [[-1, 2]], 0, 1, ALU.not_equal, 1.0, n).then_inc(K.const_step.inc(), 1)
            select(K.fold[:, :], [[-1, 2]], -2, 1, ALU.not_equal, 1.0, n + 3).then_inc(K.const_step.inc(), 1)
            for d, (step, mult) in enumerate((([[1, P]], -1), (line, 1))):
                select(K.tri[:, d, :], step, 0, mult, ALU.is_ge, 0.0, n).then_inc(K.const_step.inc(), 1)
                select(K.mask[:, d, :], step, 0, mult, ALU.is_ge, NEG, n).then_inc(K.const_step.inc(), 1)

        @block.tensor
        def _(pe):
            pe.wait_ge(K.const_step.sem, K.const_step.at(17))
            pe.wait_ge(K.cond_in.sem, K.cond_in.at(32))
            nc.tensor.transpose(K.bank[0][:, 0:16], cr[:, :], K.ident[0:16, 0:16]).then_inc(K.turn.inc(), 1)
            pe.wait_ge(K.params_in.sem, K.params_in.at(16 * L * len(param_rows(K, 0))))
            for n in range(L * PACKS):
                rows = PACK_ROWS[n % PACKS]
                if n >= 2:
                    pe.wait_ge(K.turned.sem, K.turned.at(n))
                ins = nc.tensor.transpose(K.bank[1 + n % 2][:, 0:rows], pr[0:rows, n, :], K.ident[0:rows, 0:rows])
                ins.then_inc(K.turn.inc(), 1)
            pe.wait_ge(K.x_in.sem, K.x_in.at(16 * TT))
            for j in range(8):
                if j >= 4:
                    pe.wait_ge(K.res_ready.sem, K.res_ready.at(j - 3))
                elif j == 0:
                    pe.wait_ge(K.turned.sem, K.turned.at(1 + L * PACKS))
                for t in range(TT):
                    ins = nc.tensor.transpose(K.bank[j % 4][:, t * P:t * P + P], xt[:, t, j * P:j * P + P], K.ident[:, :])
                ins.then_inc(K.turn.inc(), 1)
            next_rms_pe(K, pe, FULL, 0, 1)
            pe.wait_ge(K.cond_ready.sem, K.cond_ready.at(1))
            for h in range(16):
                mod_mm(K, pe, h, h % 2, h // 2, K.split[:, :, h % 2])
                if h % 2 and h > 1:
                    mod_fold(K, pe, h // 2 - 1)
            mod_fold(K, pe, 7)

        @block.scalar
        def _(act):
            for layer in range(L):
                for pack, row, src in param_rows(K, layer):
                    act.dma_start(pr[row:row + src.shape[0], layer * PACKS + pack, :], src).then_inc(K.params_in.inc(16), 16)
            for t in range(TT):
                act.dma_start(xt[:, t, :], x_tiles[t]).then_inc(K.x_in.inc(16), 16)
            for layer in range(L):
                row = I["ssd_d"][layer].rearrange("(o h) -> o h", o=1).to_broadcast([P, 16])
                act.dma_start(K.dload[:, layer, :], row).then_inc(K.small_in.inc(16), 16)
            for layer in range(L):
                for src, dst in ((I["ssd_dt_bias"], K.dtb), (I["ssd_a_log"], K.alog)):
                    row = src[layer].rearrange("(o d) h -> o (d h)", o=1).to_broadcast([P, 32])
                    act.dma_start(dst[:, layer, :], row).then_inc(K.small_in.inc(16), 16)
            act.wait_ge(K.turn.sem, K.turn.at(1))
            act.wait_ge(K.const_step.sem, K.const_step.at(17))
            ins = nc.scalar.activation(K.condf[:, :, :], K.bank[0][:, 0:16].rearrange("p (s k) -> p k s", k=8), ACT.Silu)
            ins.then_inc(K.act_step.inc(), 1)
            act.wait_ge(K.act_step.sem, K.act_step.own())
            cond = K.cond[:, 0:32].rearrange("p (k c) -> p k c", c=4)
            nc.scalar.activation(cond[:, :, 0:2], K.condf[:, :, :], ACT.Copy).then_inc(K.turned.inc(), 1)
            for n in range(L * PACKS):
                act.wait_ge(K.turn.sem, K.turn.at(2 + n))
                rows = PACK_ROWS[n % PACKS]
                ins = nc.scalar.activation(K.par[:, n // PACKS, n % PACKS, 0:rows], K.bank[1 + n % 2][:, 0:rows], ACT.Copy)
                ins.then_inc(K.turned.inc(), 1)
            for j in range(8):
                act.wait_ge(K.turn.sem, K.turn.at(2 + L * PACKS + j))
                ins = nc.scalar.activation(K.res[:, j, :], K.bank[j % 4][:, :], ACT.Copy)
                ins.then_inc(K.res_ready.inc(), 1)
            next_rms_act(K, act, FULL, 0, 1)
            for h in range(16):
                act.wait_ge(K.raw_full[h // 2 % 2].sem, K.raw_full[h // 2 % 2].landed(h // 4 + 1))
                act.wait_ge(K.mod_mm.sem, K.mod_mm.at(h - 1))
                ins = nc.scalar.activation(K.wh[:, h % 2, :, :], K.raw[:, h // 2 % 2, :, h % 2 * P:h % 2 * P + P], ACT.Copy)
                ins.then_inc(K.mod_hi_done.inc(), 1)
                if h % 2 == 0 and h:
                    mod_row(K, act, h // 2 - 1)
            mod_row(K, act, 7)

        @block.vector
        def _(dve):
            dve.wait_ge(K.turned.sem, K.turned.at(1))
            cond = K.cond[:, 0:32].rearrange("p (k c) -> p k c", c=4)
            ins = nc.vector.tensor_tensor(cond[:, :, 2:4], K.condf[:, :, :], r32(cond[:, :, 0:2]), ALU.subtract)
            ins.then_inc(K.cond_ready.inc(), 1)
            dve.wait_ge(K.turned.sem, K.turned.at(1 + L * PACKS))
            next_rms_dve(K, dve, FULL, 0, 1)
            for h in range(16):
                dve.wait_ge(K.mod_hi_done.sem, K.mod_hi_done.at(h + 1))
                ins = nc.vector.tensor_tensor(K.wl[:, h % 2, :, :], K.raw[:, h // 2 % 2, :, h % 2 * P:h % 2 * P + P],
                                                          r32(K.wh[:, h % 2, :, :]), ALU.subtract)
                ins.then_inc(K.mod_lo.inc(), 1)
                if h % 2 == 0 and h >= 4:
                    mod_out(K, dve, 0, h - 4, h // 2 - 2)
            for panel in (6, 7):
                mod_out(K, dve, 0, 2 * panel, panel)
            dve.wait_ge(K.small_in.sem, K.small_in.at(16 * 3 * L))
            for half in range(2):
                h = slice(64 * half, 64 * half + 64)
                d = K.dload[h, :, :].rearrange("p l (j two) -> p l two j", two=2)[:, :, half, :]
                nc.vector.tensor_copy(K.dskip[h, :, :], d).then_inc(K.small_seen.inc(), 1)
    K.end_phase()


def closing(K):
    nc = K.nc
    with ExitStack() as mem:
        ot = mem.enter_context(nc.sbuf_tensor("ot", [P, 2, 8 * P], F32))
        block = mem.enter_context(nc.Block(no_gpsimd_drain=True))

        @block.tensor
        def _(pe):
            for t in range(2):
                for g in range(2):
                    for q in range(4):
                        j = 4 * g + q
                        ins = nc.tensor.transpose(K.bank[2 * t + g][:, q * P:q * P + P],
                                                  K.res[:, j, CTX + t * P:CTX + t * P + P], K.ident[:, :])
                    ins.then_inc(K.turn.inc(), 1)

        @block.scalar
        def _(act):
            for n in range(4):
                act.wait_ge(K.turn.sem, K.turn.at(n + 1))
                ins = nc.scalar.activation(ot[:, n // 2, n % 2 * 512:n % 2 * 512 + 512], K.bank[n][:, :], ACT.Copy)
                ins.then_inc(K.turned.inc(), 1)

        @block.sync
        def _(sp):
            for t in range(2):
                sp.wait_ge(K.turned.sem, K.turned.at(2 * t + 2))
                sp.dma_start(K.out[0, t * P:(t + 1) * P, :], ot[:, t, :]).then_inc(K.stored.inc(16), 16)
            sp.wait_ge(K.stored.sem, K.stored.at(32))
    K.end_phase()



def hybrid_block(nc, inputs, out, stop=None):
    K = Kern()
    K.nc, K.inputs, K.out = nc, inputs, out
    K.stop = stop
    K.layers = inputs["w_mod"].shape[0]
    K.d_ff = inputs["ffn_w_gate"].shape[3]
    K.w_mod, K.w_gate, K.w_up, K.w_down = (inputs[n] for n in ("w_mod", "ffn_w_gate", "ffn_w_up", "ffn_w_down"))
    K.w_in, K.w_out = inputs["w_in"], inputs["w_out"]
    assert inputs["w_mod"].shape[1] == 8 * P and K.d_ff % (2 * P) == 0 and 16 * P < K.d_ff <= 24 * P
    L = K.layers
    with ExitStack() as ctx:
        def sb(name, shape, dt=F32):
            return ctx.enter_context(nc.sbuf_tensor(name, shape, dt))

        K.signals = []

        def signal(name):
            K.signals.append(Signal(ctx.enter_context(nc.semaphore(name))))
            return K.signals[-1]

        K.a_exp = signal("a_exp")
        K.act_read = signal("act_read")
        K.act_step = signal("act_step")
        K.b_ready = signal("b_ready")
        K.b_turned = signal("b_turned")
        K.cb_mm = signal("cb_mm")
        K.cb_ready = signal("cb_ready")
        K.cent_ready = signal("cent_ready")
        K.cond_in = signal("cond_in")
        K.cond_ready = signal("cond_ready")
        K.const_step = signal("const_step")
        K.conv_done = signal("conv_done")
        K.cum_read = signal("cum_read")
        K.cum_ready = signal("cum_ready")
        K.decay_ready = signal("decay_ready")
        K.diag_ready = signal("diag_ready")
        K.diff_ready = signal("diff_ready")
        K.dt_abs = signal("dt_abs")
        K.dt_exp = signal("dt_exp")
        K.dt_ln = signal("dt_ln")
        K.dt_out = signal("dt_out")
        K.dt_raw = signal("dt_raw")
        K.dt_ready = signal("dt_ready")
        K.dt_u = signal("dt_u")
        K.dtw_hi = signal("dtw_hi")
        K.dtw_in = signal("dtw_in")
        K.dtw_ready = signal("dtw_ready")
        K.dve_read = signal("dve_read")
        K.dve_step = signal("dve_step")
        K.e_ready = signal("e_ready")
        K.g_ready = signal("g_ready")
        K.half_done = signal("half_done")
        K.hh_done = signal("hh_done")
        K.hi_done = signal("hi_done")
        K.hl_done = signal("hl_done")
        K.ln_ready = signal("ln_ready")
        K.lo_done = signal("lo_done")
        K.m_ready = signal("m_ready")
        K.mean_ready = signal("mean_ready")
        K.mod_evac = signal("mod_evac")
        K.mod_fold = signal("mod_fold")
        K.mod_hi_done = signal("mod_hi_done")
        K.mod_lo = signal("mod_lo")
        K.mod_mm = signal("mod_mm")
        K.mod_row = signal("mod_row")
        K.ms_ready = signal("ms_ready")
        K.off_mm = signal("off_mm")
        K.off_used = signal("off_used")
        K.pads_zero = signal("pads_zero")
        K.params_in = signal("params_in")
        K.pgain_ready = signal("pgain_ready")
        K.prod_done = signal("prod_done")
        K.rb_ready = signal("rb_ready")
        K.res_ready = signal("res_ready")
        K.rstd_ready = signal("rstd_ready")
        K.silu_done = signal("silu_done")
        K.small_in = signal("small_in")
        K.small_seen = signal("small_seen")
        K.sq_ready = signal("sq_ready")
        K.st_ready = signal("st_ready")
        K.stat_done = signal("stat_done")
        K.state_mm = signal("state_mm")
        K.stored = signal("stored")
        K.turn = signal("turn")
        K.turned = signal("turned")
        K.uh_ready = signal("uh_ready")
        K.ul_ready = signal("ul_ready")
        K.un_ready = signal("un_ready")
        K.x_in = signal("x_in")
        K.xbc_conv = signal("xbc_conv")
        K.xbc_out = signal("xbc_out")
        K.xd_ready = signal("xd_ready")
        K.xs_turned = signal("xs_turned")
        K.xw_ready = signal("xw_ready")
        K.y_mm = signal("y_mm")
        K.y_ready = signal("y_ready")
        K.y_turned = signal("y_turned")
        K.xh_ready = signal("xh_ready")
        K.xl_ready = signal("xl_ready")
        K.yn_ready = signal("yn_ready")
        K.ytm_ready = signal("ytm_ready")
        K.raw_full = [signal(f"raw_full{n}") for n in range(2)]
        K.mod_full = signal("mod_full")
        K.bank = [ctx.enter_context(nc.psum_tensor(f"bank{n}", [P, 512], F32)) for n in range(8)]
        K.res = sb("res", [P, 8, TOK])
        K.raw = sb("raw", [P, 2, 8, 2 * P])
        K.split = sb("split", [P, 2, 2, 8, P], F32R)
        K.wh, K.wl = K.split[:, 0], K.split[:, 1]
        K.sq = sb("sq", [P, 2, TOK])
        K.diag = K.sq[:, 0, :].rearrange("p (t n) -> p t n", n=P)
        K.par = sb("par", [P, L, PACKS, P])
        K.mod = sb("mod", [P, L, 72, 2])
        K.condf = sb("condf", [P, 8, 2])
        K.cond = sb("cond", [P, 28 + P], F32R)
        K.rows = sb("rows", [4, 4 * P])
        K.fold = sb("fold", [4, 2])
        K.gain, K.pgain = sb("gain", [P, 8, 2]), sb("pgain", [P, 8, 2])
        K.ms, K.rstd = sb("ms", [P, TT]), sb("rstd", [P, TT])
        K.ident, K.ones = sb("ident", [P, P]), sb("ones", [P, P])
        K.identb = sb("identb", [P, P], BF16)
        K.tri = sb("tri", [P, 2, P])
        K.mask = sb("mask", [P, 2, P], BF16)
        K.dskip = sb("dskip", [P, L, 8])
        K.dload = sb("dload", [P, L, 16])
        K.dtb, K.alog = sb("dtb", [P, L, 32]), sb("alog", [P, L, 32])

        def ff_first(layer, ff):
            return [(panel_src(w[layer, ff], 0, 8, 0), 8) for w in (K.w_gate, K.w_up)]

        opening(K, ff_first(0, 0))
        for layer in range(L):
            last = layer == L - 1
            feed_forward(K, layer, 0, FULL, layer, 16 if layer == 0 else 68, layer == 0,
                         12 if layer == 0 else 4, mixer_first(K, layer))
            if stop == "ff":
                break
            mixer(K, layer, last, ff_first(layer, 1))
            if stop in ('mix', 'proj'):
                break
            after = ff_first(layer + 1, 0) if not last else []
            feed_forward(K, layer, 2, LATENT if last else FULL, None if last else layer + 1, 0, not last,
                         0 if last else 24, after)
            if stop == "layer":
                break
        closing(K)


NAMES = ["x", "c", "ctx", "c_ctx", "w_mod", "b_mod", "norm_pre", "norm_post", "ffn_w_gate", "ffn_w_up", "ffn_w_down",
         "w_in", "ssd_conv_w", "ssd_conv_b", "ssd_dt_bias", "ssd_a_log", "ssd_d", "ssd_norm", "conf_conv_w",
         "conf_conv_b", "conf_ln_g", "conf_ln_b", "sc_conv_w", "sc_conv_b", "w_out"]


def kernel(**inputs):
    import numpy as np
    import concourse.bacc as bacc
    from concourse.bass_utils import run_bass_kernel_spmd

    nc = bacc.Bacc("TRN2", target_bir_lowering=False, num_devices=1)
    arrays, aps = {}, {}
    for name in NAMES:
        a = np.ascontiguousarray(inputs[name])
        arrays[f"in_{name}"] = a
        aps[name] = nc.dram_tensor(f"in_{name}", a.shape, mybir.dt.from_np(a.dtype), kind="ExternalInput").ap()
    out = nc.dram_tensor("out_x", inputs["x"].shape, F32, kind="ExternalOutput").ap()
    hybrid_block(nc, aps, out)
    return run_bass_kernel_spmd(nc, [arrays], core_ids=[0]).results[0]["out_x"]
```

```python
from contextlib import ExitStack

import concourse.bass as bass
from concourse import mybir

F32 = mybir.dt.float32
F32R = mybir.dt.float32r
BF16 = mybir.dt.bfloat16
ALU = mybir.AluOpType
ACT = mybir.ActivationFunctionType

P = 128
CTX = 256
TOK = 512
TT = TOK // P
GRID = 64
EPS = 1e-6
NEG = -1e30
FULL = (0, TOK)
LATENT = (CTX, TOK - CTX)


class Signal:

    def __init__(self, sem):
        self.sem, self.base, self.count = sem, 0, 0

    def inc(self, n=1):
        self.count += n
        return self.sem

    def at(self, k):
        return k + self.base if not isinstance(k, int) or k > 0 else self.base

    def landed(self, k):
        return 16 * k + self.base

    def own(self, but=0):
        return self.count - but


class Kern:

    def end_phase(self, split_ahead=True):
        for s in self.signals:
            s.base = s.count
        if split_ahead:
            for s in (self.hi_done, self.lo_done):
                s.base -= 2

    def loop(self, eng, first, end):
        return CountedLoop(self, eng, first, end)


class CountedLoop:

    def __init__(self, K, eng, first, end):
        self.K, self.trips, self.fori = K, end - first, eng.Fori(first, end)

    def __enter__(self):
        self.before = [s.count for s in self.K.signals]
        return self.fori.__enter__()

    def __exit__(self, *exc):
        for s, b in zip(self.K.signals, self.before):
            s.count += (s.count - b) * (self.trips - 1)
        return self.fori.__exit__(*exc)


def r32(ap):
    return ap.bitcast(F32)



def panel_src(w, k0, kn, c0):
    return w[k0 * P:(k0 + kn) * P, bass.ds(c0, 2 * P)].rearrange("(k p) n -> p k n", p=P)


def load_panel(K, sp, slot, src, kn):
    sp.dma_start(K.raw[:, slot, 0:kn, :], src).then_inc(K.raw_full[slot].inc(16), 16)


def weight_hi(K, act, panel_k, slot, half, kn, nth):
    act.wait_ge(K.raw_full[slot].sem, K.raw_full[slot].landed(panel_k))
    act.wait_ge(K.half_done.sem, K.half_done.at(nth - 1))
    ins = K.nc.scalar.activation(K.wh[:, half, 0:kn, :], K.raw[:, slot, 0:kn, half * P:half * P + P],
                                 ACT.Copy)
    ins.then_inc(K.hi_done.inc(), 1)


def weight_lo(K, dve, slot, half, kn, nth):
    dve.wait_ge(K.hi_done.sem, K.hi_done.at(nth + 1))
    ins = K.nc.vector.tensor_tensor(K.wl[:, half, 0:kn, :], K.raw[:, slot, 0:kn, half * P:half * P + P],
                                    r32(K.wh[:, half, 0:kn, :]), ALU.subtract)
    ins.then_inc(K.lo_done.inc(), 1)


def split_ahead_act(K, act):
    act.wait_ge(K.raw_full[0].sem, K.raw_full[0].own())
    act.wait_ge(K.half_done.sem, K.half_done.own())
    for half in range(2):
        ins = K.nc.scalar.activation(K.wh[:, half, :, :], K.raw[:, 0, :, half * P:half * P + P], ACT.Copy)
        ins.then_inc(K.hi_done.inc(), 1)


def split_ahead_dve(K, dve):
    for half in range(2):
        dve.wait_ge(K.hi_done.sem, K.hi_done.own(1 - half))
        ins = K.nc.vector.tensor_tensor(K.wl[:, half, :, :], K.raw[:, 0, :, half * P:half * P + P],
                                        r32(K.wh[:, half, :, :]), ALU.subtract)
        ins.then_inc(K.lo_done.inc(), 1)


def product_half(K, pe, bank, half, kn, xh, xl, tok, first, last, nth, ready=None, after_k=None):
    t0, tn = tok
    pe.wait_ge(K.lo_done.sem, K.lo_done.at(nth + 1))
    for k in range(kn):
        if ready:
            pe.wait_ge(ready[0].sem, ready[0].at(ready[1] + k + 1))
        h, l = xh(k)[:, t0:t0 + tn], xl(k)[:, t0:t0 + tn]
        K.nc.tensor.matmul(bank[:, 0:tn], K.wh[:, half, k, :], h, start=first and k == 0, stop=False)
        K.nc.tensor.matmul(bank[:, 0:tn], K.wh[:, half, k, :], l, start=False, stop=False)
        ins = K.nc.tensor.matmul(bank[:, 0:tn], K.wl[:, half, k, :], h, start=False, stop=last and k == kn - 1)
        if after_k and k < kn - 1:
            after_k(k)
    ins.then_inc(K.half_done.inc(), 1)


def product_first_pair(K, pe, banks, uh, ul, tok):
    t0, tn = tok
    behind = 3
    pe.wait_ge(K.lo_done.sem, K.lo_done.at(2))
    for step in range(8 + behind):
        for half, k in ((0, step), (1, step - behind)):
            if not 0 <= k < 8:
                continue
            pe.wait_ge(K.ul_ready.sem, K.ul_ready.at(k + 1))
            h, l, bank = uh[:, k, t0:t0 + tn], ul[:, k, t0:t0 + tn], banks[half]
            K.nc.tensor.matmul(bank[:, 0:tn], K.wh[:, half, k, :], h, start=k == 0, stop=False)
            K.nc.tensor.matmul(bank[:, 0:tn], K.wh[:, half, k, :], l, start=False, stop=False)
            ins = K.nc.tensor.matmul(bank[:, 0:tn], K.wl[:, half, k, :], h, start=False, stop=k == 7)
            if k == 7:
                ins.then_inc(K.half_done.inc(), 1)



def load_mod(K, sp, w_mod, q, panel):
    sp.wait_ge(K.mod_lo.sem, K.mod_lo.at(2 * panel))
    sp.dma_start(K.raw_mod[:, :, :], panel_src(w_mod, 0, 8, P * q)).then_inc(K.mod_full.inc(16), 16)


def mod_hi(K, act, h, parity, panel):
    act.wait_ge(K.mod_full.sem, K.mod_full.landed(panel + 1))
    act.wait_ge(K.mod_mm.sem, K.mod_mm.at(h))
    ins = K.nc.scalar.activation(K.mod_split[:, 0], K.raw_mod[:, :, parity * P:parity * P + P], ACT.Copy)
    ins.then_inc(K.mod_hi_done.inc(), 1)


def mod_lo(K, dve, h, parity):
    dve.wait_ge(K.mod_hi_done.sem, K.mod_hi_done.at(h + 1))
    ins = K.nc.vector.tensor_tensor(K.mod_split[:, 1], K.raw_mod[:, :, parity * P:parity * P + P],
                                    r32(K.mod_split[:, 0]), ALU.subtract)
    ins.then_inc(K.mod_lo.inc(), 1)


def mod_mm(K, pe, h, parity, panel, split):
    pe.wait_ge(K.mod_lo.sem, K.mod_lo.at(h + 1))
    pe.wait_ge(K.mod_row.sem, K.mod_row.at(panel))
    for k in range(8):
        cond = K.cond[:, 4 * k:4 * k + P]
        out = K.bank[4][:, parity * 2 * P:(parity + 1) * 2 * P].rearrange("p (w n) -> p w n", w=2)
        ins = K.nc.tensor.matmul(out, cond, split[:, :, k, :], start=k == 0, stop=k == 7)
    ins.then_inc(K.mod_mm.inc(), 1)


def mod_row(K, dve, panel):
    dve.wait_ge(K.mod_mm.sem, K.mod_mm.at(2 * panel + 2))
    dve.wait_ge(K.mod_fold.sem, K.mod_fold.at(panel))
    parts = K.bank[4][0:4, :].rearrange("p (t w n) -> p w t n", w=2, n=P)
    rows = K.rows[:, :].rearrange("p (t n) -> p t n", n=P)
    K.nc.vector.tensor_copy(rows, parts[:, 0]).then_inc(K.mod_row_hi.inc(), 1)
    dve.wait_ge(K.mod_row_hi.sem, K.mod_row_hi.at(panel + 1))
    K.nc.vector.tensor_tensor(rows, rows, parts[:, 1], ALU.add).then_inc(K.mod_row.inc(), 1)


def mod_fold(K, pe, panel):
    pe.wait_ge(K.mod_row.sem, K.mod_row.at(panel + 1))
    pe.wait_ge(K.mod_evac.sem, K.mod_evac.at(panel))
    for t in range(2):
        ins = K.nc.tensor.matmul(K.bank[7][:, 2 * t:2 * t + 2], K.rows[:, t * P:t * P + P], K.fold[:, :],
                                 start=True, stop=True)
    ins.then_inc(K.mod_fold.inc(), 1)


def mod_out(K, dve, layer, q, panel):
    dve.wait_ge(K.mod_fold.sem, K.mod_fold.at(panel + 1))
    bias = K.par[:, layer, 0, bass.ds(q, 2)].unsqueeze(2).to_broadcast([P, 2, 2])
    ins = K.nc.vector.tensor_tensor(K.mod[:, layer, bass.ds(q, 2), :],
                                    K.bank[7][:, 0:4].rearrange("p (q s) -> p q s", s=2), bias, ALU.add)
    ins.then_inc(K.mod_evac.inc(), 1)



def stats_pe(K, pe, src, tok, j, n, nth):
    pe.wait_ge(K.sq_ready.sem, K.sq_ready.at(nth + 1))
    for t in range(tok[1] // P):
        ins = K.nc.tensor.matmul(K.bank[5][:, t:t + 1], src[:, t * P:t * P + P], K.ones[:, 0:1],
                                 start=j == 0 and t == 0, stop=j == n - 1, skip_group_check=True)
    ins.then_inc(K.stat_done.inc(), 1)


def rstd_dve(K, dve, tok, width, stats, nth):
    n = tok[1] // P
    dve.wait_ge(K.stat_done.sem, K.stat_done.at(stats))
    ins = K.nc.vector.tensor_scalar(K.ms[:, 0:n], K.bank[5][:, 0:n], 1.0 / width, EPS, ALU.mult, ALU.add)
    ins.then_inc(K.dve_step.inc(), 1)
    dve.wait_ge(K.dve_step.sem, K.dve_step.own())
    K.nc.vector.reciprocal(K.ms[:, 0:n], K.ms[:, 0:n]).then_inc(K.ms_ready.inc(), 1)
    dve.wait_ge(K.rstd_ready.sem, K.rstd_ready.at(nth))
    ins = K.nc.vector.tensor_tensor(
        K.diag[:, 0:n, :], K.ident[:, :].unsqueeze(1).to_broadcast([P, n, P]),
        K.rstd[:, 0:n].unsqueeze(2).to_broadcast([P, n, P]), ALU.mult)
    ins.then_inc(K.diag_ready.inc(), 1)


def rstd_act(K, act, tok, nth):
    n = tok[1] // P
    act.wait_ge(K.ms_ready.sem, K.ms_ready.at(nth))
    K.nc.scalar.activation(K.rstd[:, 0:n], K.ms[:, 0:n], ACT.Sqrt).then_inc(K.rstd_ready.inc(), 1)


def rstd_pe(K, pe, tok, nth):
    n = tok[1]
    pe.wait_ge(K.diag_ready.sem, K.diag_ready.at(nth))
    ins = K.nc.tensor.matmul(K.bank[6][:, 0:n], K.ones[:, :],
                             K.diag[:, 0:n // P, :].rearrange("p t n -> p (t n)"), start=True, stop=True)
    ins.then_inc(K.rb_ready.inc(), 1)



def next_rms_act(K, act, tok, stats, nth):
    t0, tn = tok
    for j in range(8):
        act.wait_ge(K.res_ready.sem, K.res_ready.at(j + 1))
        act.wait_ge(K.stat_done.sem, K.stat_done.at(stats + j - 1))
        ins = K.nc.scalar.activation(K.sq[:, j % 2, 0:tn], K.res[:, j, t0:t0 + tn], ACT.Square)
        ins.then_inc(K.sq_ready.inc(), 1)
    rstd_act(K, act, tok, nth)


def next_rms_pe(K, pe, tok, stats, nth):
    for j in range(8):
        stats_pe(K, pe, K.sq[:, j % 2, :], tok, j, 8, stats + j)
    rstd_pe(K, pe, tok, nth)


def next_rms_dve(K, dve, tok, stats, nth):
    rstd_dve(K, dve, tok, 1024, stats + 8, nth)



def prenorm_act(K, act, layer, which, tok, un_buf, uh):
    t0, tn = tok
    for j in range(8):
        un = un_buf[:, j % 2, :]
        act.wait_ge(K.un_ready.sem, K.un_ready.at(j + 1))
        for s in range(2):
            if s * CTX >= t0:
                a = s * CTX - t0
                ins = K.nc.scalar.activation(un[:, a:a + CTX], un[:, a:a + CTX], ACT.Identity, scale=K.gain[:, j, s:s + 1],
                                             bias=K.mod[:, layer, 24 * which + j, s:s + 1])
                ins.then_inc(K.act_step.inc(), 1)
        act.wait_ge(K.act_step.sem, K.act_step.own())
        K.nc.scalar.activation(uh[:, j, t0:t0 + tn], un[:, 0:tn], ACT.Copy).then_inc(K.uh_ready.inc(), 1)


def prenorm_dve(K, dve, layer, which, tok, un_buf, uh, ul):
    t0, tn = tok
    nc = K.nc

    def normed(j):
        dve.wait_ge(K.ul_ready.sem, K.ul_ready.own())
        ins = nc.vector.tensor_tensor(un_buf[:, j % 2, 0:tn], K.res[:, j, t0:t0 + tn], K.bank[6][:, 0:tn], ALU.mult)
        ins.then_inc(K.un_ready.inc(), 1)

    scale = K.mod[:, layer, 8 * (3 * which + 1):8 * (3 * which + 2), :]
    nc.vector.tensor_scalar(K.gain[:, :, :], scale, 1.0, None, ALU.add).then_inc(K.dve_step.inc(), 1)
    dve.wait_ge(K.dve_step.sem, K.dve_step.own())
    g = K.par[:, layer, 0, 72 + 8 * which:80 + 8 * which].unsqueeze(2).to_broadcast([P, 8, 2])
    nc.vector.tensor_tensor(K.gain[:, :, :], K.gain[:, :, :], g, ALU.mult).then_inc(K.dve_step.inc(), 1)
    dve.wait_ge(K.dve_step.sem, K.dve_step.own())
    normed(0)
    for j in range(8):
        if j < 7:
            normed(j + 1)
        dve.wait_ge(K.uh_ready.sem, K.uh_ready.at(j + 1))
        ins = nc.vector.tensor_tensor(ul[:, j, t0:t0 + tn], un_buf[:, j % 2, 0:tn], r32(uh[:, j, t0:t0 + tn]), ALU.subtract)
        ins.then_inc(K.ul_ready.inc(), 1)



def post_gain_dve(K, dve, layer, which, weight):
    nc = K.nc
    gate = K.mod[:, layer, 8 * (3 * which + 2):8 * (3 * which + 3), :]
    nc.vector.tensor_scalar(K.pgain[:, :, :], gate, weight, None, ALU.mult).then_inc(K.dve_step.inc(), 1)
    dve.wait_ge(K.dve_step.sem, K.dve_step.own())
    g = K.par[:, layer, 0, 96 + 8 * which:104 + 8 * which].unsqueeze(2).to_broadcast([P, 8, 2])
    nc.vector.tensor_tensor(K.pgain[:, :, :], K.pgain[:, :, :], g, ALU.mult).then_inc(K.pgain_ready.inc(), 1)


def post_tile_act(K, act, bank, j, tok, y, stats):
    t0, tn = tok
    if stats + j >= 2:
        act.wait_ge(K.stat_done.sem, K.stat_done.at(stats + j - 1))
    K.nc.scalar.activation(K.sq[:, j % 2, 0:tn], bank[:, 0:tn], ACT.Square).then_inc(K.sq_ready.inc(), 1)
    for s in range(2):
        if s * CTX >= t0:
            a = s * CTX - t0
            ins = K.nc.scalar.activation(y[:, j, a:a + CTX], bank[:, a:a + CTX], ACT.Copy, scale=K.pgain[:, j, s:s + 1])
    ins.then_inc(K.y_ready.inc(), 1)


POOL_TILES = 5


def residual_dve(K, dve, tok, y, stats, nth, norm_follows):
    t0, tn = tok

    def normed(tiles):
        for j in tiles:
            K.nc.vector.tensor_tensor(y[:, j, 0:tn], y[:, j, 0:tn], K.bank[6][:, 0:tn], ALU.mult).then_inc(K.yr_ready.inc(), 1)

    def add(tiles):
        for j in tiles:
            dve.wait_ge(K.yr_ready.sem, K.yr_ready.at(j + 1))
            ins = K.nc.vector.tensor_tensor(K.res[:, j, t0:t0 + tn], K.res[:, j, t0:t0 + tn], y[:, j, 0:tn], ALU.add)
            ins.then_inc(K.res_tail.inc(), 1)

    def pair(i):
        if norm_follows:
            dve.wait_ge(K.square_ready.sem, K.square_ready.at(2 * i + 2))
            ins = K.nc.vector.tensor_tensor(y[:, 2 * i, 0:tn], y[:, 2 * i, 0:tn], y[:, 2 * i + 1, 0:tn], ALU.add)
            ins.then_inc(K.pair_ready.inc(), 1)

    rstd_dve(K, dve, tok, 1024, stats, nth)
    dve.wait_ge(K.y_ready.sem, K.y_ready.at(8))
    dve.wait_ge(K.rb_ready.sem, K.rb_ready.at(nth))
    normed(range(6))
    pair(0)
    normed((6, 7))
    add(range(POOL_TILES, 6))
    pair(1)
    add((6, 7))
    pair(2)
    pair(3)


def residual_pool(K, pool, tok, y):
    t0, tn = tok
    for j in range(POOL_TILES):
        pool.wait_ge(K.yr_ready.sem, K.yr_ready.at(j + 1))
        ins = K.nc.gpsimd.tensor_tensor(K.res[:, j, t0:t0 + tn], K.res[:, j, t0:t0 + tn], y[:, j, 0:tn], ALU.add)
        ins.then_inc(K.res_ready.inc(), 1)



def residual_rms_act(K, act, tok, y, nth):
    t0, tn = tok
    for j in range(8):
        if j < POOL_TILES:
            act.wait_ge(K.res_ready.sem, K.res_ready.at(j + 1))
        else:
            act.wait_ge(K.res_tail.sem, K.res_tail.at(j + 1 - POOL_TILES))
        ins = K.nc.scalar.activation(y[:, j, 0:tn], K.res[:, j, t0:t0 + tn], ACT.Square)
        ins.then_inc(K.square_ready.inc(), 1)
    rstd_act(K, act, tok, nth)


def residual_rms_dve(K, dve, tok, stats, nth):
    split_ahead_dve(K, dve)
    rstd_dve(K, dve, tok, 1024, stats + 4, nth)


def residual_rms_pe(K, pe, tok, y, nth):
    for i in range(4):
        pe.wait_ge(K.pair_ready.sem, K.pair_ready.at(i + 1))
        for t in range(tok[1] // P):
            ins = K.nc.tensor.matmul(K.bank[5][:, t:t + 1], y[:, 2 * i, t * P:t * P + P], K.ones[:, 0:1],
                                     start=i == 0 and t == 0, stop=i == 3, skip_group_check=True)
        ins.then_inc(K.stat_done.inc(), 1)
    rstd_pe(K, pe, tok, nth)


class OutProduct:

    def __init__(self, K, w, parts, order, xh, xl, tok, xtok, y, halves, panels, stats, norms, norm_follows, mods=0,
                 mod_h=0, mod_layer=0, mod_q=0):
        self.K, self.w, self.parts, self.xh, self.xl, self.tok, self.xtok, self.y = K, w, parts, xh, xl, tok, xtok, y
        self.order = order
        self.halves, self.panels, self.stats, self.norms = halves, panels, stats, norms
        self.mods, self.mod_h, self.mod_layer, self.mod_q = mods, mod_h, mod_layer, mod_q
        self.norm_follows = norm_follows
        self.kstart = [sum(parts[:n]) for n in range(len(parts))]
        self.n_panels = len(order)
        self.first = [p == min(q for q in range(len(order)) if order[q][0] == order[p][0]) for p in range(len(order))]
        self.last = [p == max(q for q in range(len(order)) if order[q][0] == order[p][0]) for p in range(len(order))]

    def src(self, p):
        pair, part = self.order[p]
        return panel_src(self.w, self.kstart[part], self.parts[part], 2 * P * pair), self.parts[part]

    def sp(self, sp, following):
        K = self.K
        for p in range(self.n_panels):
            if p < self.mods // 2:
                load_mod(K, sp, K.w_mod[self.mod_layer], self.mod_q + 2 * p, self.mod_h // 2 + p)
            if p + 2 < self.n_panels:
                src, kn = self.src(p + 2)
            elif p + 2 - self.n_panels < len(following):
                src, kn = following[p + 2 - self.n_panels]
            else:
                continue
            sp.wait_ge(K.lo_done.sem, K.lo_done.at(self.halves + 2 * p + 2))
            load_panel(K, sp, p % 2, src, kn)

    def pe(self, pe, bank_free, before, ready):
        K, n = self.K, 0
        for p, (pair, part) in enumerate(self.order):
            k0 = self.kstart[part]
            for half in range(2):
                j = 2 * pair + half
                if self.first[p] and pair >= 2:
                    pe.wait_ge(K.y_ready.sem, K.y_ready.at(j - 3))
                elif self.first[p]:
                    bank_free(pair)
                before(n)
                product_half(K, pe, K.bank[2 * (pair % 2) + half], half, self.parts[part], lambda k: self.xh(k0 + k),
                             lambda k: self.xl(k0 + k), self.xtok, self.first[p], self.last[p], self.halves + n,
                             ready.get(n))
                h = self.mod_h + n
                if n < self.mods:
                    mod_mm(K, pe, h, half, h // 2, K.mod_split)
                if half == 1 and 2 <= h and n <= self.mods:
                    mod_fold(K, pe, h // 2 - 1)
                if self.last[p] and pair >= 1:
                    stats_pe(K, pe, K.sq[:, half, :], self.tok, j - 2, 8, self.stats + j - 2)
                n += 1
        if self.mods:
            mod_fold(K, pe, (self.mod_h + self.mods) // 2 - 1)
        for j in (6, 7):
            stats_pe(K, pe, K.sq[:, j % 2, :], self.tok, j, 8, self.stats + j)
        rstd_pe(K, pe, self.tok, self.norms)
        if self.norm_follows:
            residual_rms_pe(K, pe, self.tok, self.y, self.norms + 1)

    def act(self, act, skip=0):
        K = self.K
        for n in range(2 * self.n_panels + 2):
            p, half, h = n // 2, n % 2, self.mod_h + n
            if skip <= n < 2 * self.n_panels:
                weight_hi(K, act, self.panels + p // 2, p % 2, half, self.parts[self.order[p][1]], self.halves + n)
            if n == 0:
                act.wait_ge(K.pgain_ready.sem, K.pgain_ready.at(1))
            if 1 <= n <= self.mods:
                mod_hi(K, act, h - 1, 1 - half, (h - 1) // 2)
            if n >= 2 and self.last[p - 1]:
                j = 2 * self.order[p - 1][0] + half
                act.wait_ge(K.half_done.sem, K.half_done.at(self.halves + n - 1))
                post_tile_act(K, act, K.bank[2 * (j // 2 % 2) + j % 2], j, self.tok, self.y, self.stats)
        rstd_act(K, act, self.tok, self.norms)
        if self.norm_follows:
            split_ahead_act(K, act)
            residual_rms_act(K, act, self.tok, self.y, self.norms + 1)

    def dve(self, dve, skip=0):
        K = self.K
        for n in range(2 * self.n_panels + 2):
            p, half, h = n // 2, n % 2, self.mod_h + n
            if skip <= n < 2 * self.n_panels:
                weight_lo(K, dve, p % 2, half, self.parts[self.order[p][1]], self.halves + n)
            if 1 <= n <= self.mods:
                mod_lo(K, dve, h - 1, 1 - half)
            if half == 1 and h - 1 >= 2 and n <= self.mods + 1 and self.mods:
                mod_row(K, dve, (h - 1) // 2 - 1)
            if 1 <= n <= self.mods:
                if half == 1 and (h - 1) // 2 >= 2:
                    self.mod_out(dve, (h - 1) // 2 - 2)
        if self.mods:
            for back in (2, 1):
                self.mod_out(dve, (self.mod_h + self.mods) // 2 - back)
        residual_dve(K, dve, self.tok, self.y, self.stats + 8, self.norms, self.norm_follows)
        if self.norm_follows:
            residual_rms_dve(K, dve, self.tok, self.stats + 8, self.norms + 1)

    def mod_out(self, dve, panel):
        mod_out(self.K, dve, self.mod_layer, self.mod_q + 2 * panel - self.mod_h, panel)



def feed_forward(K, layer, which, tok, mod_layer, mod_q, mods_loop, mods_down, following):
    nc = K.nc
    ff = which // 2
    w_gate, w_up, w_down = K.w_gate[layer, ff], K.w_up[layer, ff], K.w_down[layer, ff]
    w_mod = K.w_mod[mod_layer] if mod_layer is not None else None
    t0, tn = tok
    FT = K.d_ff // P
    pairs = FT // 2
    with ExitStack() as mem:
        tag = f"{layer}{which}"
        if mods_loop or mods_down:
            K.raw_mod = mem.enter_context(nc.sbuf_tensor("raw_mod" + tag, [P, 8, 2 * P], F32))
            K.mod_split = mem.enter_context(nc.sbuf_tensor("mod_split" + tag, [P, 2, 8, P], F32R))
        hh = mem.enter_context(nc.sbuf_tensor("hh" + tag, [P, FT, tn], F32R))
        hl = mem.enter_context(nc.sbuf_tensor("hl" + tag, [P, FT, tn], F32R))
        with ExitStack() as up_mem:
            uh = up_mem.enter_context(nc.sbuf_tensor("uh" + tag, [P, 8, TOK], F32R))
            ul = up_mem.enter_context(nc.sbuf_tensor("ul" + tag, [P, 8, TOK], F32R))
            sil = up_mem.enter_context(nc.sbuf_tensor("sil" + tag, [P, 2, TOK], F32))
            hf = up_mem.enter_context(nc.sbuf_tensor("hf" + tag, [P, 2, TOK], F32))
        y = mem.enter_context(nc.sbuf_tensor("y" + tag, [P, 8, TOK], F32))
        out = OutProduct(K, w_down, (8, 8, FT - 16), [(pair, part) for pair in range(4) for part in range(3)], lambda k: hh[:, k, :], lambda k: hl[:, k, :], tok, (0, tn), y,
                         4 * pairs, pairs, 0, 1, bool(following), mods_down, 4 * pairs if mods_loop else 0, mod_layer,
                         mod_q + (4 * pairs if mods_loop else 0))
        block = mem.enter_context(nc.Block(no_gpsimd_drain=True))

        @block.sync
        def _(sp):
            def next_panels(i, gate, up):
                sp.wait_ge(K.lo_done.sem, K.lo_done.at(4 * i + 2))
                load_panel(K, sp, 0, *gate)
                if mods_loop:
                    load_mod(K, sp, w_mod, mod_q + 4 * i + 2, 2 * i + 1)
                sp.wait_ge(K.lo_done.sem, K.lo_done.at(4 * i + 4))
                load_panel(K, sp, 1, *up)

            if mods_loop:
                load_mod(K, sp, w_mod, mod_q, 0)
            with K.loop(sp, 0, pairs - 1) as i:
                next_panels(i, (panel_src(w_gate, 0, 8, 2 * P * i + 2 * P), 8), (panel_src(w_up, 0, 8, 2 * P * i + 2 * P), 8))
                if mods_loop:
                    load_mod(K, sp, w_mod, mod_q + 4 * i + 4, 2 * i + 2)
            next_panels(pairs - 1, out.src(0), out.src(1))
            out.sp(sp, following)

        @block.tensor
        def _(pe):
            def trip(i, first):
                for half in range(4):
                    if half % 2 == 0:
                        pe.wait_ge((K.silu_done, K.prod_done)[half // 2].sem, (K.silu_done, K.prod_done)[half // 2].at(2 * i))
                    if first and half == 0:
                        product_first_pair(K, pe, K.bank, uh, ul, tok)
                    elif not (first and half == 1):
                        product_half(K, pe, K.bank[half], half % 2, 8, lambda k: uh[:, k, :], lambda k: ul[:, k, :], tok,
                                     True, True, 4 * i + half)
                    if mods_loop:
                        mod_mm(K, pe, 4 * i + half, half % 2, 2 * i + half // 2, K.mod_split)
                        if half % 2 and not (first and half == 1):
                            mod_fold(K, pe, 2 * i - 1 + half // 2)
            trip(0, True)
            with K.loop(pe, 1, pairs) as i:
                trip(i, False)

            def bank_free(pair):
                read = (K.silu_done, K.prod_done)[pair]
                pe.wait_ge(read.sem, read.at(FT))

            def hidden_there(n):
                if n in (0, 4):
                    pe.wait_ge(K.hl_done.sem, K.hl_done.at(16 if n == 0 else FT))
            out.pe(pe, bank_free, hidden_there, {})

        @block.gpsimd
        def _(pool):
            residual_pool(K, pool, tok, y)

        @block.scalar
        def _(act):
            prenorm_act(K, act, layer, which, tok, sil, uh)

            def hidden_hi(f, at):
                act.wait_ge(K.prod_done.sem, K.prod_done.at(f + 1))
                ins = nc.scalar.activation(hh[:, bass.ds(f, 1), :].rearrange("p a n -> p (a n)"), hf[:, at, 0:tn], ACT.Copy)
                ins.then_inc(K.hh_done.inc(), 1)

            def silu(i, j):
                act.wait_ge(K.half_done.sem, K.half_done.at(4 * i + j + 1))
                act.wait_ge(K.prod_done.sem, K.prod_done.at(2 * i + j - 1))
                nc.scalar.activation(sil[:, j, 0:tn], K.bank[j][:, 0:tn], ACT.Silu).then_inc(K.silu_done.inc(), 1)

            def mod(i, n):
                if mods_loop:
                    mod_hi(K, act, 4 * i + n, n % 2, 2 * i + n // 2)

            def trip(i, first, last):
                if not first:
                    weight_hi(K, act, i, 0, 1, 8, 4 * i + 1)
                mod(i, 0)
                if not first:
                    hidden_hi(2 * i - 1, 1)
                weight_hi(K, act, i, 1, 0, 8, 4 * i + 2)
                mod(i, 1)
                silu(i, 0)
                weight_hi(K, act, i, 1, 1, 8, 4 * i + 3)
                mod(i, 2)
                silu(i, 1)
                if not last:
                    weight_hi(K, act, i + 1, 0, 0, 8, 4 * i + 4)
                else:
                    weight_hi(K, act, pairs, 0, 0, out.parts[0], 4 * pairs)
                mod(i, 3)
                hidden_hi(2 * i, 0)

            trip(0, True, False)
            with K.loop(act, 1, pairs - 1) as i:
                trip(i, False, False)
            trip(pairs - 1, False, True)
            weight_hi(K, act, pairs, 0, 1, out.parts[0], 4 * pairs + 1)
            hidden_hi(FT - 1, 1)
            out.act(act, skip=2)

        @block.vector
        def _(dve):
            prenorm_dve(K, dve, layer, which, tok, sil, uh, ul)

            def product(i, j):
                dve.wait_ge(K.silu_done.sem, K.silu_done.at(2 * i + j + 1))
                dve.wait_ge(K.half_done.sem, K.half_done.at(4 * i + 2 + j + 1))
                ins = nc.vector.tensor_tensor(hf[:, j, 0:tn], sil[:, j, 0:tn], K.bank[2 + j][:, 0:tn], ALU.mult)
                ins.then_inc(K.prod_done.inc(), 1)

            def hidden_lo(f, at):
                dve.wait_ge(K.hh_done.sem, K.hh_done.at(f + 1))
                h = bass.ds(f, 1)
                ins = nc.vector.tensor_tensor(hl[:, h, :].rearrange("p a n -> p (a n)"), hf[:, at, 0:tn],
                                              r32(hh[:, h, :]).rearrange("p a n -> p (a n)"), ALU.subtract)
                ins.then_inc(K.hl_done.inc(), 1)

            def mod(i, n, first):
                if mods_loop:
                    mod_lo(K, dve, 4 * i + n, n % 2)
                    if n == 2 or n == 0 and not first:
                        mod_row(K, dve, 2 * i - 1 + n // 2)
                    if n % 2 == 0 and not first:
                        mod_out(K, dve, mod_layer, mod_q + 2 * (2 * i - 2 + n // 2), 2 * i - 2 + n // 2)

            def trip(i, first, last):
                if not first:
                    weight_lo(K, dve, 0, 1, 8, 4 * i + 1)
                mod(i, 0, first)
                if not first:
                    hidden_lo(2 * i - 1, 1)
                weight_lo(K, dve, 1, 0, 8, 4 * i + 2)
                mod(i, 1, first)
                weight_lo(K, dve, 1, 1, 8, 4 * i + 3)
                mod(i, 2, first)
                if not last:
                    weight_lo(K, dve, 0, 0, 8, 4 * i + 4)
                else:
                    weight_lo(K, dve, 0, 0, out.parts[0], 4 * pairs)
                mod(i, 3, first)
                product(i, 0)
                hidden_lo(2 * i, 0)
                product(i, 1)

            trip(0, True, False)
            with K.loop(dve, 1, pairs - 1) as i:
                trip(i, False, False)
            trip(pairs - 1, False, True)
            weight_lo(K, dve, 0, 1, out.parts[0], 4 * pairs + 1)
            hidden_lo(FT - 1, 1)
            post_gain_dve(K, dve, layer, which, 0.5)
            out.dve(dve, skip=2)
    K.end_phase(bool(following))


CHUNKS = 2


class ScanPlan:

    def __init__(self, last):
        self.seqs = (0, 1)
        self.with_y = {0: not last, 1: True}
        self.states = {0: [(0, 0), (1, 0), (1, 1), (0, 1)], 1: [(0, 0), (1, 1)]}

    @staticmethod
    def prev(seq, c, d):
        first = c == 0 if d == 0 else c == 1
        if first:
            return None if seq == 0 else "init"
        return "mid"



XBC_T, Z_T, GRP_T = 12, 8, 4
DT0 = XBC_T * P
Z0 = DT0 + 32
CONF0 = Z0 + Z_T * P
SC0 = CONF0 + 2 * GRP_T * P
CONF_HALO, SC_TAPS, XBC_TAPS, CONF_TAPS = 15, 3, 5, 31

HALVES = [(kind, 2 * pair + half) for kind, pair in
          (("gate", 0), ("value", 0),
           ("xbc", 0), ("xbc", 1), ("xbc", 2), ("xbc", 3), ("xbc", 4), ("xbc", 5),
           ("sc_c", 0), ("sc_h", 0), ("gate", 1), ("value", 1), ("sc_b", 0), ("sc_c", 1), ("sc_h", 1), ("sc_b", 1),
           ("z", 0), ("z", 1), ("z", 2), ("z", 3)) for half in range(2)]
COLUMN = {"value": CONF0, "gate": CONF0 + GRP_T * P, "z": Z0, "sc_b": SC0, "sc_c": SC0 + GRP_T * P,
          "sc_h": SC0 + 2 * GRP_T * P, "xbc": 0}
READER = {"gate": "act", "z": "act", "sc_c": "act", "xbc": "act", "value": "dve", "sc_h": "dve", "sc_b": "dve"}
NH = len(HALVES)
FIRST_VALUE = [HALVES.index(("value", t)) for t in range(0, GRP_T, 2)]
XBC_AT = HALVES.index(("xbc", 0))
DT_AT = 6
SCAN_AT = XBC_AT + XBC_T + 2
TAPS_XBC, TAPS_DT, TAPS_SCAN = (1, 1), (8, 8), (3, 3)
SCAN_LEAD = 2
Z_AT = HALVES.index(("z", 0))
LN_MEAN, LN_SQ = 34, 36


def reads(n, who):
    return sum(READER[kind] == who for kind, _ in HALVES[:n + 1])


def gate_used(n):
    return reads(max(i for i in range(n) if HALVES[i][0] in ("value", "sc_h")), "dve")


def w_in_panel(K, layer, p):
    kind, tile = HALVES[2 * p]
    return panel_src(K.w_in[layer], 0, 8, COLUMN[kind] + P * tile), 8


def mixer_first(K, layer):
    return [w_in_panel(K, layer, 0), w_in_panel(K, layer, 1)]


def mix_in(K, M, layer, last, following):
    nc = K.nc
    plan = ScanPlan(last)
    part = LATENT if last else FULL
    p0, pn = part
    steps_per_half = 2 if last else 4
    with ExitStack() as mem:
        def sb(name, shape, dt=F32):
            return mem.enter_context(nc.sbuf_tensor(f"{name}_{layer}", shape, dt))
        uh, ul = sb("mix_uh", [P, 8, TOK], F32R), sb("mix_ul", [P, 8, TOK], F32R)
        cpad = sb("conf_pad", [P, 2, TOK // GRID, GRID + 2 * CONF_HALO])
        conf = M.yc
        spc = sb("sc_pad_ctx", [P, 2, CTX + 2])
        spx = sb("sc_pad_x", [P, 2, TOK - CTX + 2 * GRID])
        gate = sb("gate", [P, 2, TOK])
        with ExitStack() as early:
            def sb_early(name, shape, dt=F32):
                return early.enter_context(nc.sbuf_tensor(f"{name}_{layer}", shape, dt))
            bpad = sb_early("xbc_pad", [P, 2, 2, CTX + 4])
            acc = sb_early("conv_acc", [P, 2, TOK])
            wdt = sb_early("wdt", [P, 8, 32])
            wdh, wdl = sb_early("wdh", [P, 8, 32], F32R), sb_early("wdl", [P, 8, 32], F32R)
        xd = sb("xd", [P, CHUNKS, 2, HEADS, HD])
        spare = K.sq[:, :, :].rearrange("p b n -> p (b n)")
        n_small = TT * 2 * HEADS
        t_abs, t_e, t_u, t_ln, t_d, dt, a = (
            spare[:, n * n_small:(n + 1) * n_small].rearrange("p (t d h) -> p t d h", t=TT, d=2) for n in range(7))
        ea = spare[:, 7 * n_small:7 * n_small + 2 * HEADS]
        t_z = t_abs
        cum = sb("cum", [P, 2, TT, HEADS])
        neg = sb("neg_cum", [P, 2, TT, HEADS])
        tot = sb("tot", [P, TT, 2, HEADS])
        dec = sb("dec", [P, TT, 2, HEADS])
        ecum, etot = sb("exp_cum", [P, 2, TT, HEADS]), sb("exp_tot", [P, TT, 2, HEADS])
        xw = sb("xw", [P, HEADS, HD])
        btm = sb("b_tm", [P, CHUNKS, 2 * P])
        init = sb("state_init", [P, 2, HEADS, HD])
        mid = sb("state_mid", [P, 2, HEADS, HD])
        cbt = sb("cb", [P, 2, P])
        e = sb("decay", [P, 2, 4, P])
        m = sb("weights", [P, 2, 4, P])
        ytm = sb("y_tm", [P, HEADS, HD])
        tmp = sb("off", [P, GH, HD])
        block = mem.enter_context(nc.Block(no_gpsimd_drain=True))
        par = K.par[:, layer]
        bh = lambda ap, n: ap.unsqueeze(2).to_broadcast([P, n, HD])
        fm = lambda tile, t: M.xbc[:, tile, t * P:t * P + P]
        state = {"init": init, "mid": mid}

        @block.sync
        def _(sp):
            src = K.w_in[layer][:, DT0:DT0 + 32].rearrange("(k p) n -> p k n", p=P)
            sp.dma_start(wdt[:, :, :], src).then_inc(K.dtw_in.inc(16), 16)
            for p in range(NH // 2):
                panel = w_in_panel(K, layer, p + 2) if p + 2 < NH // 2 else following[p + 2 - NH // 2]
                sp.wait_ge(K.lo_done.sem, K.lo_done.at(2 * p + 2))
                load_panel(K, sp, p % 2, *panel)

        @block.gpsimd
        def _(pool):
            for pad in (cpad, spc, spx, bpad):
                nc.gpsimd.memset(pad[:], 0.0).then_inc(K.pads_zero.inc(), 1)
            turns = states = 0
            for seq in plan.seqs:
                turns += CHUNKS
                for c, d in plan.states[seq]:
                    pool.wait_ge(K.decay_ready.sem, K.decay_ready.at(1))
                    pool.wait_ge(K.xd_ready.sem, K.xd_ready.at(4 * turns))
                    pool.wait_ge(K.state_mm.sem, K.state_mm.at(states))
                    for g in range(2):
                        heads = slice(GH * g, GH * g + GH)
                        ins = nc.gpsimd.tensor_tensor(xw[:, heads, :], xd[:, c, d, heads, :], bh(dec[:, 2 * seq + c, d, heads], GH), ALU.mult)
                        ins.then_inc(K.xw_ready.inc(), 1)
                    states += 1

        @block.tensor
        def _(pe):
            def scan_steps():
                pe.wait_ge(K.cum_read.sem, K.cum_read.at(1))
                pe.wait_ge(K.xbc_out.sem, K.xbc_out.at(XBC_T))
                turns = states = units = offs = gs = 0
                for seq in plan.seqs:
                    for c in range(CHUNKS):
                        t = 2 * seq + c
                        pe.wait_ge(K.ytm_ready.sem, K.ytm_ready.at(gs))
                        pe.wait_ge(K.xd_ready.sem, K.xd_ready.at(4 * turns))
                        for j in range(8):
                            ins = nc.tensor.transpose(K.bank[4 + j // 4][:, j % 4 * P:j % 4 * P + P], fm(j, t), K.ident[:, :])
                        ins.then_inc(K.xs_turned.inc(), 1)
                        pe.wait_ge(K.g_ready.sem, K.g_ready.at(gs))
                        pe.wait_ge(K.cb_ready.sem, K.cb_ready.at(units // 8))
                        pe.wait_ge(K.b_ready.sem, K.b_ready.at(turns))
                        for g in range(2):
                            ins = nc.tensor.transpose(K.bank[7][:, g * P:g * P + P], fm(8 + g, t), K.ident[:, :])
                        ins.then_inc(K.b_turned.inc(), 1)
                        turns += 1
                        yield
                    yield
                    pe.wait_ge(K.b_ready.sem, K.b_ready.at(turns))
                    pe.wait_ge(K.e_ready.sem, K.e_ready.at(units))
                    for c, d in plan.states[seq]:
                        pe.wait_ge(K.st_ready.sem, K.st_ready.at(states))
                        for g in range(2):
                            pe.wait_ge(K.xw_ready.sem, K.xw_ready.at(2 * states + g + 1))
                            ins = nc.tensor.matmul(K.bank[2 + g][:, :], btm[:, c, g * P:g * P + P],
                                                   xw[:, GH * g:GH * g + GH, :].rearrange("p h n -> p (h n)"), start=True, stop=True)
                        ins.then_inc(K.state_mm.inc(), 1)
                        states += 1
                        yield
                    pe.wait_ge(K.st_ready.sem, K.st_ready.at(states))
                    if not plan.with_y[seq]:
                        continue
                    pe.wait_ge(K.xd_ready.sem, K.xd_ready.at(4 * turns))
                    for c in range(CHUNKS):
                        t = 2 * seq + c
                        entering = [d for d in range(2) if plan.prev(seq, c, d)]
                        pe.wait_ge(K.cb_ready.sem, K.cb_ready.at(units // 8))
                        pe.wait_ge(K.g_ready.sem, K.g_ready.at(gs))
                        for g in range(2):
                            ins = nc.tensor.matmul(K.bank[7][:, g * P:g * P + P], fm(8 + g, t), fm(10 + g, t), start=True, stop=True)
                        ins.then_inc(K.cb_mm.inc(), 1)

                        def decay(u):
                            d, h = u % 2, 4 * (u // 2)
                            bank = K.bank[2 + u % 2]
                            pe.wait_ge(K.e_ready.sem, K.e_ready.at(units + u - 1))
                            nc.tensor.matmul(bank[:, :], K.identb[:, :], K.mask[:, d, :].unsqueeze(1).to_broadcast([P, 4, P]),
                                             start=True, stop=False, skip_group_check=True)
                            for i in range(4):
                                ins = nc.tensor.matmul(bank[:, i * P:i * P + P], a[:, t, d, h + i:h + i + 1].to_broadcast([P, P]),
                                                       K.tri[:, d, :], start=False, stop=True, skip_group_check=True)
                            ins.then_inc(K.diff_ready.inc(), 1)

                        decay(0)
                        decay(1)

                        def y_turn(g):
                            pe.wait_ge(K.ytm_ready.sem, K.ytm_ready.at(gs + g + 1))
                            pe.wait_ge(K.g_ready.sem, K.g_ready.at(gs + g))
                            for i in range(4):
                                h = GH * g + 2 * i
                                ins = nc.tensor.transpose(K.bank[7][:, i * P:i * P + P],
                                                          ytm[:, h:h + 2, :].rearrange("p h n -> p (h n)"), K.ident[:, :])
                            ins.then_inc(K.y_turned.inc(), 1)

                        yield
                        for u in range(8):
                            g = u // 4
                            if u // 2 % 2 < len(entering) and u % 2 == 0:
                                d = entering[u // 2 % 2]
                                pe.wait_ge(K.off_used.sem, K.off_used.at(offs))
                                ins = nc.tensor.matmul(
                                    K.bank[6][:, :], fm(10 + g, t),
                                    state[plan.prev(seq, c, d)][:, d, GH * g:GH * g + GH, :].rearrange("p h n -> p (h n)"),
                                    start=True, stop=True)
                                ins.then_inc(K.off_mm.inc(), 1)
                                offs += 1
                            pe.wait_ge(K.m_ready.sem, K.m_ready.at(units + u + 1))
                            if u % 4 == 0:
                                pe.wait_ge(K.ytm_ready.sem, K.ytm_ready.at(gs + g - 1))
                            for i in range(4):
                                h = 4 * (u // 2) + i
                                ins = nc.tensor.matmul(K.bank[4 + g][:, (h - GH * g) * HD:(h - GH * g + 1) * HD], m[:, u % 2, i, :],
                                                       xd[:, c, u % 2, h, :], start=u % 4 == 0 and i == 0, stop=u % 4 >= 2,
                                                       skip_group_check=True)
                            ins.then_inc(K.y_mm.inc(), 1)
                            if u + 2 < 8:
                                decay(u + 2)
                            if u == 6:
                                y_turn(0)
                            yield
                        y_turn(1)
                        yield
                        units += 8
                        gs += 2

            scan = scan_steps()

            def scan_step(k):
                if k % 2 == 0 and k // 2 < steps_per_half:
                    next(scan, None)

            for n, (kind, tile) in enumerate(HALVES):
                if n >= 2:
                    who = READER[HALVES[n - 2][0]]
                    read = K.act_read if who == "act" else K.dve_read
                    pe.wait_ge(read.sem, read.at(reads(n - 2, who)))
                if n == Z_AT:
                    for _ in scan:
                        pass
                if n == 0:
                    product_first_pair(K, pe, K.bank, uh, ul, part)
                elif n > 1:
                    product_half(K, pe, K.bank[n % 2], n % 2, 8, lambda k: uh[:, k, :], lambda k: ul[:, k, :],
                                 FULL if kind == "xbc" else part, True, True, n, None,
                                 scan_step if SCAN_AT <= n < Z_AT else None)
                if n == DT_AT:
                    pe.wait_ge(K.dtw_ready.sem, K.dtw_ready.at(1))
                    for t in range(TT):
                        for k in range(8):
                            tok = slice(t * P, t * P + P)
                            for x, w in ((uh, wdh), (ul, wdh), (uh, wdl)):
                                ins = nc.tensor.matmul(K.bank[4][:, 32 * t:32 * t + 32], x[:, k, tok], w[:, k, :],
                                                       start=k == 0 and w is wdh and x is uh, stop=k == 7 and w is wdl)
                    ins.then_inc(K.dt_raw.inc(), 1)
                if n == DT_AT + 4:
                    pe.wait_ge(K.dt_ready.sem, K.dt_ready.at(1))
                    for d in range(2):
                        nc.tensor.matmul(K.bank[4][:, 64 * d:64 * d + 64], K.tri[:, d, :], a[:, :, d, :], start=True, stop=True)
                    ins = nc.tensor.matmul(K.bank[4][:, P:2 * P], K.ones[:, :], a[:, :, :, :].rearrange("p t d h -> p (t d h)"),
                                           start=True, stop=True)
                    ins.then_inc(K.cum_ready.inc(), 1)
                if n == LN_MEAN:
                    pe.wait_ge(K.conv_done.sem, K.conv_done.at(GRP_T))
                    for t in range(GRP_T):
                        ins = nc.tensor.matmul(K.bank[7][:, 0:pn], K.ones[:, :], conf[:, t, p0:p0 + pn], start=t == 0, stop=t == GRP_T - 1)
                    ins.then_inc(K.mean_ready.inc(), 1)
                if n in (LN_SQ, LN_SQ + 1):
                    for t in (0, 1) if n == LN_SQ else (2, 3):
                        stats_pe(K, pe, K.sq[:, t % 2, :], part, t, GRP_T, t)
            rstd_pe(K, pe, part, 1)

        @block.scalar
        def _(act):
            flat = lambda ap: ap.rearrange("p t d h -> p (t d h)")

            def scan_steps():
                turns = units = 0
                for seq in plan.seqs:
                    yield
                    for c in range(CHUNKS):
                        act.wait_ge(K.b_turned.sem, K.b_turned.at(turns + 1))
                        nc.scalar.activation(btm[:, c, :], K.bank[7][:, 0:2 * P], ACT.Copy).then_inc(K.b_ready.inc(), 1)
                        turns += 1
                        yield
                    yield from (None,) * len(plan.states[seq])
                    if not plan.with_y[seq]:
                        continue
                    for c in range(CHUNKS):
                        t = 2 * seq + c
                        yield
                        act.wait_ge(K.cb_mm.sem, K.cb_mm.at(units // 8 + 1))
                        act.wait_ge(K.m_ready.sem, K.m_ready.at(units))
                        ins = nc.scalar.activation(cbt[:, :, :].rearrange("p g l -> p (g l)"), K.bank[7][:, 0:2 * P], ACT.Copy)
                        ins.then_inc(K.cb_ready.inc(), 1)
                        for u in range(8):
                            act.wait_ge(K.diff_ready.sem, K.diff_ready.at(units + u + 1))
                            act.wait_ge(K.m_ready.sem, K.m_ready.at(units + u - 1))
                            for i in range(4):
                                h = 4 * (u // 2) + i
                                ins = nc.scalar.activation(e[:, u % 2, i, :], K.bank[2 + u % 2][:, i * P:i * P + P], ACT.Exp,
                                                           bias=neg[:, u % 2, t, h:h + 1])
                            ins.then_inc(K.e_ready.inc(), 1)
                            yield
                        yield
                        units += 8

            scan = scan_steps()
            prenorm_act(K, act, layer, 1, FULL, acc, uh)
            act.wait_ge(K.pads_zero.sem, K.pads_zero.at(4))
            for n in range(NH + 2):
                if 2 <= n < NH:
                    weight_hi(K, act, n // 4, n // 2 % 2, n % 2, 8, n)
                if n == 2:
                    act.wait_ge(K.dtw_in.sem, K.dtw_in.at(16))
                    nc.scalar.activation(wdh[:, :, :], wdt[:, :, :], ACT.Copy).then_inc(K.dtw_hi.inc(), 1)
                if n >= 2:
                    kind, tile = HALVES[n - 2]
                    bank = K.bank[n % 2]
                    if READER[kind] == "act":
                        act.wait_ge(K.half_done.sem, K.half_done.at(n - 1))
                    if kind in ("gate", "sc_c"):
                        if n - 2 > FIRST_VALUE[0]:
                            act.wait_ge(K.dve_read.sem, K.dve_read.at(gate_used(n - 2)))
                        ins = nc.scalar.activation(gate[:, tile % 2, 0:pn], bank[:, 0:pn], ACT.Sigmoid if kind == "gate" else ACT.Copy)
                        ins.then_inc(K.act_read.inc(), 1)
                    elif kind == "z":
                        act.wait_ge(K.dve_read.sem, K.dve_read.at(gate_used(n - 2)))
                        act.wait_ge(K.z_used.sem, K.z_used.at(tile - 1))
                        ins = nc.scalar.activation(gate[:, tile % 2, 0:pn], bank[:, 0:pn], ACT.Silu)
                        ins.then_inc(K.act_read.inc(), 1)
                    elif kind == "xbc":
                        if tile >= 2:
                            act.wait_ge(K.xbc_conv.sem, K.xbc_conv.at(tile - 1))
                        act.wait_ge(K.xbc_out.sem, K.xbc_out.own())
                        nc.scalar.activation(acc[:, tile % 2, :], bank[:, :], ACT.Identity, scale=par[:, 2, 24 + tile:25 + tile],
                                             bias=par[:, 2, 60 + tile:61 + tile])
                        ins = nc.scalar.activation(bpad[:, tile % 2, :, 2:2 + CTX],
                                                   bank[:, :].rearrange("p (s n) -> p s n", s=2), ACT.Copy)
                        ins.then_inc(K.act_read.inc(), 1)
                if XBC_AT + 3 <= n < XBC_AT + XBC_T + 3:
                    tile = n - 3 - XBC_AT
                    act.wait_ge(K.xbc_conv.sem, K.xbc_conv.at(tile + 1))
                    nc.scalar.activation(M.xbc[:, tile, :], acc[:, tile % 2, :], ACT.Silu).then_inc(K.xbc_out.inc(), 1)
                if n == DT_AT + 3:
                    act.wait_ge(K.dt_abs.sem, K.dt_abs.at(1))
                    nc.scalar.activation(flat(t_e[:]), flat(t_abs[:]), ACT.Exp, scale=-1.0).then_inc(K.dt_exp.inc(), 1)
                    nc.scalar.activation(ea[:, :], K.alog[:, layer, :], ACT.Exp).then_inc(K.a_exp.inc(), 1)
                    act.wait_ge(K.dt_u.sem, K.dt_u.at(1))
                    nc.scalar.activation(flat(t_ln[:]), flat(t_u[:]), ACT.Ln).then_inc(K.dt_ln.inc(), 1)
                if n == DT_AT + 5:
                    act.wait_ge(K.cum_read.sem, K.cum_read.at(1))
                    nc.scalar.activation(flat(dec[:]), flat(dec[:]), ACT.Exp)
                    nc.scalar.activation(flat(ecum[:]), flat(cum[:]), ACT.Exp)
                    nc.scalar.activation(flat(etot[:]), flat(tot[:]), ACT.Exp).then_inc(K.decay_ready.inc(), 1)
                if n in (LN_SQ, LN_SQ + 1):
                    for t in (0, 1) if n == LN_SQ else (2, 3):
                        act.wait_ge(K.cent_ready.sem, K.cent_ready.at(t + 1))
                        act.wait_ge(K.stat_done.sem, K.stat_done.at(t - 1))
                        ins = nc.scalar.activation(K.sq[:, t % 2, 0:pn], conf[:, t, p0:p0 + pn], ACT.Square)
                        ins.then_inc(K.sq_ready.inc(), 1)
                if SCAN_AT < n <= Z_AT:
                    for _ in range(steps_per_half + (SCAN_LEAD if n == SCAN_AT + 1 else 0)):
                        next(scan, None)
                if n == Z_AT:
                    for _ in scan:
                        pass
            rstd_act(K, act, part, 1)
            split_ahead_act(K, act)
            for t in range(GRP_T):
                act.wait_ge(K.ln_ready.sem, K.ln_ready.at(t + 1))
                ins = nc.scalar.activation(conf[:, t, p0:p0 + pn], conf[:, t, p0:p0 + pn], ACT.Silu,
                                           scale=par[:, 2, 76 + t:77 + t], bias=par[:, 2, 80 + t:81 + t])
                ins.then_inc(K.act_step.inc(), 1)

        @block.vector
        def _(dve):
            V = nc.vector
            flat = lambda ap: ap.rearrange("p t d h -> p (t d h)")

            def scan_steps():
                dve.wait_ge(K.xbc_out.sem, K.xbc_out.at(XBC_T))
                turns = states = units = offs = gs = 0
                for seq in plan.seqs:
                    yield
                    for c in range(CHUNKS):
                        dve.wait_ge(K.xs_turned.sem, K.xs_turned.at(turns + 1))
                        for d in range(2):
                            for g in range(2):
                                ins = V.tensor_tensor(
                                    xd[:, c, d, GH * g:GH * g + GH, :], K.bank[4 + g][:, :].rearrange("p (h n) -> p h n", n=HD),
                                    bh(dt[:, 2 * seq + c, d, GH * g:GH * g + GH], GH), ALU.mult)
                                ins.then_inc(K.xd_ready.inc(), 1)
                        turns += 1
                        yield
                    for c, d in plan.states[seq]:
                        prev = plan.prev(seq, c, d)
                        target = mid if (c == 0) == (d == 0) else init
                        if prev:
                            dve.wait_ge(K.decay_ready.sem, K.decay_ready.at(1))
                            dve.wait_ge(K.st_ready.sem, K.st_ready.own())
                            ins = V.tensor_tensor(target[:, d, :, :], state[prev][:, d, :, :], bh(etot[:, 2 * seq + c, d, :], HEADS), ALU.mult)
                            ins.then_inc(K.dve_step.inc(), 1)
                            dve.wait_ge(K.dve_step.sem, K.dve_step.own())
                        dve.wait_ge(K.state_mm.sem, K.state_mm.at(states + 1))
                        for g in range(2):
                            half = target[:, d, GH * g:GH * g + GH, :].rearrange("p h n -> p (h n)")
                            ins = V.tensor_tensor(half, half, K.bank[2 + g][:, :], ALU.add) if prev else V.tensor_copy(half, K.bank[2 + g][:, :])
                        ins.then_inc(K.st_ready.inc(), 1)
                        states += 1
                        yield
                    if not plan.with_y[seq]:
                        continue
                    for c in range(CHUNKS):
                        t = 2 * seq + c
                        entering = [d for d in range(2) if plan.prev(seq, c, d)]

                        def gated(g):
                            dve.wait_ge(K.y_turned.sem, K.y_turned.at(gs + g + 1))
                            for i in range(4):
                                ins = V.scalar_tensor_tensor(fm(4 * g + i, t), fm(4 * g + i, t), K.dskip[:, layer, 4 * g + i:4 * g + i + 1],
                                                             K.bank[7][:, i * P:i * P + P], ALU.mult, ALU.add)
                            ins.then_inc(K.g_ready.inc(), 1)

                        def within(g):
                            y = ytm[:, GH * g:GH * g + GH, :].rearrange("p h n -> p (h n)")
                            dve.wait_ge(K.y_mm.sem, K.y_mm.at(units + 4 * g + 4))
                            dve.wait_ge(K.off_used.sem, K.off_used.own())
                            dve.wait_ge(K.dve_step.sem, K.dve_step.own())
                            V.tensor_tensor(y, y, K.bank[4 + g][:, :], ALU.add).then_inc(K.ytm_ready.inc(), 1)

                        yield
                        for u in range(8):
                            dve.wait_ge(K.cb_ready.sem, K.cb_ready.at(units // 8 + 1))
                            dve.wait_ge(K.e_ready.sem, K.e_ready.at(units + u + 1))
                            dve.wait_ge(K.y_mm.sem, K.y_mm.at(units + u - 1))
                            ins = V.tensor_tensor(m[:, u % 2, :, :], e[:, u % 2, :, :],
                                                  cbt[:, u // 4, :].unsqueeze(1).to_broadcast([P, 4, P]), ALU.mult)
                            ins.then_inc(K.m_ready.inc(), 1)
                            g = u // 4
                            if u // 2 % 2 < len(entering) and u % 2 == 1:
                                d = entering[u // 2 % 2]
                                y = ytm[:, GH * g:GH * g + GH, :]
                                first = u // 2 % 2 == 0
                                dve.wait_ge(K.off_mm.sem, K.off_mm.at(offs + 1))
                                dve.wait_ge(K.y_turned.sem, K.y_turned.at(gs + g - 1))
                                ins = V.tensor_tensor(y if first else tmp[:, :, :], K.bank[6][:, :].rearrange("p (h n) -> p h n", n=HD),
                                                      bh(ecum[:, d, t, GH * g:GH * g + GH], GH), ALU.mult)
                                ins.then_inc(K.off_used.inc(), 1)
                                offs += 1
                                if not first:
                                    dve.wait_ge(K.off_used.sem, K.off_used.own())
                                    V.tensor_tensor(y, y, tmp[:, :, :], ALU.add).then_inc(K.dve_step.inc(), 1)
                            if u == 4:
                                within(0)
                            if u == 7:
                                gated(0)
                                within(1)
                            yield
                        yield
                        gated(1)
                        units += 8
                        gs += 2

            scan = scan_steps()

            def taps(tensors, steps, signal=None):
                for k in steps:
                    for i, (out, src, weights, bias) in enumerate(tensors):
                        if k == 0:
                            ins = nc.vector.tensor_scalar(out, src(k), weights(k), bias, ALU.mult, ALU.add)
                        else:
                            dve.wait_ge(K.dve_step.sem, K.dve_step.own(len(tensors) - 1 - (i if signal else 0)))
                            ins = nc.vector.scalar_tensor_tensor(out, src(k), weights(k), out, ALU.mult, ALU.add)
                        ins.then_inc((signal or K.dve_step).inc(), 1)

            def conf_taps(pair, k):
                tensors = []
                for t in (2 * pair, 2 * pair + 1):
                    weights = lambda k, t=t: par[:, 1, 4 * k + t:4 * k + t + 1]
                    bias = par[:, 2, 72 + t:73 + t]
                    tensors.append((conf[:, t, p0:p0 + pn].rearrange("p (r c) -> p r c", c=GRID),
                                    lambda k, t=t: cpad[:, t % 2, p0 // GRID:, k:k + GRID], weights, bias))
                taps(tensors, [k], K.conv_done if k == CONF_TAPS - 1 else None)

            prenorm_dve(K, dve, layer, 1, FULL, acc, uh, ul)
            conv = [(pair, k) for pair in range(GRP_T // 2) for k in range(CONF_TAPS)]

            def conf_next(n):
                if conv and n > FIRST_VALUE[conv[0][0]] + 2:
                    pair, k = conv.pop(0)
                    if k == 0:
                        dve.wait_ge(K.dve_read.sem, K.dve_read.own())
                    conf_taps(pair, k)

            for n in range(NH + 2):
                if 2 <= n < NH:
                    weight_lo(K, dve, n // 2 % 2, n % 2, 8, n)
                if n == 2:
                    dve.wait_ge(K.dtw_hi.sem, K.dtw_hi.at(1))
                    ins = nc.vector.tensor_tensor(wdl[:, :, :], wdt[:, :, :], r32(wdh[:, :, :]), ALU.subtract)
                    ins.then_inc(K.dtw_ready.inc(), 1)
                    dve.wait_ge(K.pads_zero.sem, K.pads_zero.at(4))
                if n >= 2:
                    kind, tile = HALVES[n - 2]
                    bank = K.bank[n % 2]
                    if READER[kind] == "dve":
                        dve.wait_ge(K.half_done.sem, K.half_done.at(n - 1))
                    if kind == "value" and tile >= 2:
                        dve.wait_ge(K.conv_done.sem, K.conv_done.own())
                        dve.wait_ge(K.dve_step.sem, K.dve_step.own())
                    if kind in ("value", "sc_h"):
                        dve.wait_ge(K.act_read.sem, K.act_read.at(reads(n - 4, "act")))
                        g = gate[:, tile % 2, :]
                        if kind == "value":
                            rows = cpad[:, tile % 2]
                            src, g = (v[:, 0:pn].rearrange("p (r c) -> p r c", c=GRID) for v in (bank, g))
                            if not last:
                                n_c = CTX // GRID
                                for out, tokens in ((rows[:, 1:n_c, 0:CONF_HALO], (slice(0, n_c - 1), slice(GRID - CONF_HALO, GRID))),
                                                    (rows[:, 0:n_c - 1, CONF_HALO + GRID:], (slice(1, n_c), slice(0, CONF_HALO)))):
                                    ins = nc.vector.tensor_tensor(out, src[:, tokens[0], tokens[1]], g[:, tokens[0], tokens[1]], ALU.mult)
                                    ins.then_inc(K.dve_step.inc(), 1)
                            ins = nc.vector.tensor_tensor(rows[:, p0 // GRID:, CONF_HALO:CONF_HALO + GRID], src, g, ALU.mult)
                        else:
                            if not last:
                                ins = nc.vector.tensor_tensor(spc[:, tile % 2, 1:1 + CTX], bank[:, 0:CTX], g[:, 0:CTX], ALU.mult)
                                ins.then_inc(K.dve_step.inc(), 1)
                            ins = nc.vector.tensor_tensor(spx[:, tile % 2, GRID:GRID + CTX], bank[:, CTX - p0:TOK - p0],
                                                          g[:, CTX - p0:TOK - p0], ALU.mult)
                        ins.then_inc(K.dve_read.inc(), 1)
                    elif kind == "sc_b":
                        j, buf = tile, tile % 2
                        dve.wait_ge(K.dve_read.sem, K.dve_read.own())
                        weights, bias = lambda k: par[:, 2, 84 + 4 * k + j:85 + 4 * k + j], par[:, 2, 96 + j:97 + j]
                        ctx = (M.ys[:, j, 0:CTX], lambda k: spc[:, buf, k:k + CTX], weights, bias)
                        lat = (M.ys[:, j, CTX:TOK], lambda k: spx[:, buf, k * GRID:k * GRID + CTX], weights, bias)
                        taps([lat] if last else [ctx, lat], range(SC_TAPS))
                        dve.wait_ge(K.dve_step.sem, K.dve_step.own())
                        ins = nc.vector.tensor_tensor(M.ys[:, j, p0:p0 + pn], M.ys[:, j, p0:p0 + pn], bank[:, 0:pn], ALU.mult)
                        ins.then_inc(K.dve_read.inc(), 1)
                if n == DT_AT + 2:
                    dve.wait_ge(K.dt_raw.sem, K.dt_raw.at(1))
                    bias = K.dtb[:, layer, :].unsqueeze(1).to_broadcast([P, TT, 32])
                    ins = nc.vector.tensor_tensor(M.dt[:, :, :], K.bank[4][:, 0:P].rearrange("p (t h) -> p t h", t=TT), bias, ALU.add)
                    ins.then_inc(K.dt_out.inc(), 1)
                if n == DT_AT + 3:
                    dve.wait_ge(K.dt_out.sem, K.dt_out.own())
                    raw = M.dt[:, :, :].rearrange("p t h -> p (t h)")
                    V.scalar_tensor_tensor(flat(t_abs[:]), raw, -1.0, raw, ALU.mult, ALU.max).then_inc(K.dt_abs.inc(), 1)
                    dve.wait_ge(K.dt_exp.sem, K.dt_exp.at(1))
                    V.tensor_scalar(flat(t_u[:]), flat(t_e[:]), 1.0, None, ALU.add).then_inc(K.dt_u.inc(), 1)
                    dve.wait_ge(K.dt_u.sem, K.dt_u.own())
                    V.tensor_scalar(flat(t_d[:]), flat(t_u[:]), -1.0, None, ALU.add).then_inc(K.dve_step.inc(), 1)
                    dve.wait_ge(K.dve_step.sem, K.dve_step.own())
                    V.tensor_scalar(flat(t_z[:]), flat(t_d[:]), 0.0, None, ALU.is_equal).then_inc(K.dve_step.inc(), 1)
                    dve.wait_ge(K.dve_step.sem, K.dve_step.own())
                    V.tensor_tensor(flat(t_d[:]), flat(t_d[:]), flat(t_z[:]), ALU.add).then_inc(K.dve_step.inc(), 1)
                    dve.wait_ge(K.dve_step.sem, K.dve_step.own())
                    V.reciprocal(flat(t_d[:]), flat(t_d[:])).then_inc(K.dve_step.inc(), 1)
                    dve.wait_ge(K.dve_step.sem, K.dve_step.own())
                    V.tensor_tensor(flat(t_d[:]), flat(t_d[:]), flat(t_e[:]), ALU.mult).then_inc(K.dve_step.inc(), 1)
                    dve.wait_ge(K.dve_step.sem, K.dve_step.own())
                    dve.wait_ge(K.dt_ln.sem, K.dt_ln.at(1))
                    V.tensor_tensor(flat(t_ln[:]), flat(t_ln[:]), flat(t_d[:]), ALU.mult).then_inc(K.dve_step.inc(), 1)
                    dve.wait_ge(K.dve_step.sem, K.dve_step.own())
                    V.tensor_tensor(flat(t_z[:]), flat(t_z[:]), flat(t_e[:]), ALU.mult).then_inc(K.dve_step.inc(), 1)
                    dve.wait_ge(K.dve_step.sem, K.dve_step.own())
                    V.tensor_tensor(flat(t_ln[:]), flat(t_ln[:]), flat(t_z[:]), ALU.add).then_inc(K.dve_step.inc(), 1)
                    dve.wait_ge(K.dve_step.sem, K.dve_step.own())
                    ins = V.scalar_tensor_tensor(flat(dt[:]), raw, 0.0, flat(t_ln[:]), ALU.max, ALU.add)
                    ins.then_inc(K.dve_step.inc(), 1)
                    dve.wait_ge(K.dve_step.sem, K.dve_step.own())
                    dve.wait_ge(K.a_exp.sem, K.a_exp.at(1))
                    ins = V.scalar_tensor_tensor(a[:].rearrange("p t d h -> p t (d h)"), dt[:].rearrange("p t d h -> p t (d h)"), -1.0,
                                                 ea[:, :].unsqueeze(1).to_broadcast([P, TT, 32]), ALU.mult, ALU.mult)
                    ins.then_inc(K.dt_ready.inc(), 1)
                if n == DT_AT + 5:
                    dve.wait_ge(K.cum_ready.sem, K.cum_ready.at(1))
                    V.tensor_copy(flat(cum[:]), K.bank[4][:, 0:P]).then_inc(K.dve_step.inc(), 1)
                    dve.wait_ge(K.dve_step.sem, K.dve_step.own())
                    V.tensor_copy(flat(tot[:]), K.bank[4][:, P:2 * P]).then_inc(K.dve_step.inc(), 1)
                    dve.wait_ge(K.dve_step.sem, K.dve_step.own())
                    V.tensor_scalar(flat(neg[:]), flat(cum[:]), -1.0, None, ALU.mult).then_inc(K.dve_step.inc(), 1)
                    dve.wait_ge(K.dve_step.sem, K.dve_step.own())
                    for d in range(2):
                        ins = V.tensor_tensor(dec[:, :, d, :], tot[:, :, d, :], neg[:, d, :, :], ALU.add)
                    ins.then_inc(K.cum_read.inc(), 1)
                if n <= SCAN_AT:
                    for _ in range(TAPS_DT[last] if n == DT_AT + 2 else TAPS_XBC[last]):
                        conf_next(n)
                if n == SCAN_AT + 1:
                    for _ in range(SCAN_LEAD):
                        next(scan, None)
                for q in range(4):
                    if SCAN_AT < n <= Z_AT and q < steps_per_half:
                        next(scan, None)
                    if n > SCAN_AT and q < (TAPS_SCAN[last] if n <= Z_AT else 4):
                        conf_next(n)
                if n == Z_AT:
                    for _ in scan:
                        pass
                if n == LN_SQ:
                    dve.wait_ge(K.mean_ready.sem, K.mean_ready.at(1))
                    for t in range(GRP_T):
                        ins = nc.vector.scalar_tensor_tensor(conf[:, t, p0:p0 + pn], K.bank[7][:, 0:pn], -1.0 / (GRP_T * P),
                                                             conf[:, t, p0:p0 + pn], ALU.mult, ALU.add)
                        ins.then_inc(K.cent_ready.inc(), 1)
                if n >= 2 and HALVES[n - 2][0] == "z":
                    tile = HALVES[n - 2][1]
                    dve.wait_ge(K.act_read.sem, K.act_read.at(reads(n - 2, "act")))
                    dve.wait_ge(K.g_ready.sem, K.g_ready.own())
                    y = M.xbc[:, tile, p0:p0 + pn]
                    V.tensor_tensor(y, y, gate[:, tile % 2, 0:pn], ALU.mult).then_inc(K.z_used.inc(), 1)
                if n >= 2 and HALVES[n - 2][0] == "xbc":
                    t = HALVES[n - 2][1]
                    dve.wait_ge(K.act_read.sem, K.act_read.at(reads(n - 2, "act")))
                    view = acc[:, t % 2, :].rearrange("p (s n) -> p s n", s=2)
                    for k in (0, 1, 3, 4):
                        if k:
                            ins.then_inc(K.dve_step.inc(), 1)
                            dve.wait_ge(K.dve_step.sem, K.dve_step.own())
                        ins = nc.vector.scalar_tensor_tensor(view, bpad[:, t % 2, :, k:k + CTX], par[:, 2, 12 * k + t:12 * k + t + 1],
                                                             view, ALU.mult, ALU.add)
                    ins.then_inc(K.xbc_conv.inc(), 1)
            rstd_dve(K, dve, part, GRP_T * P, GRP_T, 1)
            dve.wait_ge(K.rb_ready.sem, K.rb_ready.at(1))
            for t in range(GRP_T):
                ins = nc.vector.tensor_tensor(conf[:, t, p0:p0 + pn], conf[:, t, p0:p0 + pn], K.bank[6][:, 0:pn], ALU.mult)
                ins.then_inc(K.ln_ready.inc(), 1)
            split_ahead_dve(K, dve)
    K.end_phase()



HEADS, HD, GH = 16, 64, 8

MIX_ORDER = [(0, 1), (1, 1), (0, 0), (1, 0), (2, 0), (2, 1), (3, 0), (3, 1)]


def mix_out(K, M, layer, last, following):
    nc = K.nc
    tok = LATENT if last else FULL
    t0, tn = tok
    with ExitStack() as mem:
        def sb(name, shape, dt=F32):
            return mem.enter_context(nc.sbuf_tensor(f"{name}_{layer}", shape, dt))
        xh, xl = sb("out_xh", [P, 16, TOK], F32R), sb("out_xl", [P, 16, TOK], F32R)
        y = sb("mix_y", [P, 8, TOK])
        out = OutProduct(K, K.w_out[layer], (8, 8), MIX_ORDER, lambda k: xh[:, k, :], lambda k: xl[:, k, :],
                         tok, tok, y, 0, 0, 8, 2, True)
        block = mem.enter_context(nc.Block(no_gpsimd_drain=True))
        gain = K.par[:, layer, 2, 100:108]
        conv = lambda i: (M.yc if i < GRP_T else M.ys)[:, i % GRP_T, t0:t0 + tn]

        @block.sync
        def _(sp):
            out.sp(sp, following)

        @block.tensor
        def _(pe):
            def norm(n):
                if n in (1, 2):
                    for j in range(4 * n - 4, 4 * n):
                        stats_pe(K, pe, K.sq[:, j % 2, :], tok, j, 8, j)
                elif n == 3:
                    rstd_pe(K, pe, tok, 1)
            out.pe(pe, lambda pair: None, norm, {0: (K.xl_ready, 0), 4: (K.xl_ready, 8)})

        @block.gpsimd
        def _(pool):
            residual_pool(K, pool, tok, y)

        @block.scalar
        def _(act):
            for i in range(8):
                nc.scalar.activation(xh[:, 8 + i, t0:t0 + tn], conv(i), ACT.Copy).then_inc(K.xh_ready.inc(), 1)
            for j in range(8):
                act.wait_ge(K.stat_done.sem, K.stat_done.at(j - 1))
                ins = nc.scalar.activation(K.sq[:, j % 2, 0:tn], M.xbc[:, j, t0:t0 + tn], ACT.Square)
                ins.then_inc(K.sq_ready.inc(), 1)
                if j == 3:
                    weight_hi(K, act, 0, 1, 0, 8, 2)
            rstd_act(K, act, tok, 1)
            weight_hi(K, act, 0, 1, 1, 8, 3)
            for j in range(8):
                act.wait_ge(K.yn_ready.sem, K.yn_ready.at(j + 1))
                ins = nc.scalar.activation(xh[:, j, t0:t0 + tn], M.xbc[:, j, t0:t0 + tn], ACT.Copy, scale=gain[:, j:j + 1])
                ins.then_inc(K.xh_ready.inc(), 1)
                if j in (0, 5):
                    weight_hi(K, act, 1, 0, j // 5, 8, 4 + j // 5)
            out.act(act, skip=6)

        @block.vector
        def _(dve):
            def normed(j):
                z = M.xbc[:, j, t0:t0 + tn]
                nc.vector.tensor_tensor(z, z, K.bank[6][:, 0:tn], ALU.mult).then_inc(K.yn_ready.inc(), 1)

            for i in range(8):
                dve.wait_ge(K.xh_ready.sem, K.xh_ready.at(i + 1))
                ins = nc.vector.tensor_tensor(xl[:, 8 + i, t0:t0 + tn], conv(i), r32(xh[:, 8 + i, t0:t0 + tn]), ALU.subtract)
                ins.then_inc(K.xl_ready.inc(), 1)
            post_gain_dve(K, dve, layer, 1, 1.0)
            weight_lo(K, dve, 1, 0, 8, 2)
            rstd_dve(K, dve, tok, 8 * P, 8, 1)
            weight_lo(K, dve, 1, 1, 8, 3)
            dve.wait_ge(K.rb_ready.sem, K.rb_ready.at(1))
            normed(0)
            for j in range(8):
                if j < 7:
                    normed(j + 1)
                if j in (0, 5):
                    weight_lo(K, dve, 0, j // 5, 8, 4 + j // 5)
                dve.wait_ge(K.xh_ready.sem, K.xh_ready.at(9 + j))
                dve.wait_ge(K.yn_ready.sem, K.yn_ready.at(j + 1))
                ins = nc.vector.scalar_tensor_tensor(xl[:, j, t0:t0 + tn], M.xbc[:, j, t0:t0 + tn], gain[:, j:j + 1],
                                                     r32(xh[:, j, t0:t0 + tn]), ALU.mult, ALU.subtract)
                ins.then_inc(K.xl_ready.inc(), 1)
            out.dve(dve, skip=6)
    K.end_phase()


def mixer(K, layer, last, following):
    nc = K.nc
    M = Kern()
    with ExitStack() as mem:
        def sb(name, shape, dt=F32):
            return mem.enter_context(nc.sbuf_tensor(f"{name}_{layer}", shape, dt))
        M.xbc = sb("xbc", [P, XBC_T, TOK])
        M.yc, M.ys = sb("yc", [P, GRP_T, TOK]), sb("ys", [P, GRP_T, TOK])
        M.dt = sb("dt_raw", [P, TT, 32])
        w_out_first = [(panel_src(K.w_out[layer], 8 * part, 8, 2 * P * pair), 8) for pair, part in MIX_ORDER[:2]]
        mix_in(K, M, layer, last, w_out_first)
        mix_out(K, M, layer, last, following)



PACKS = 3


def param_rows(K, layer):
    I = K.inputs
    rows = lambda ap: ap.rearrange("(a p) -> a p", p=P)
    return [
        (0, 0, rows(I["b_mod"][layer])),
        (0, 72, I["norm_pre"][layer].rearrange("w (a p) -> (w a) p", p=P)),
        (0, 96, I["norm_post"][layer].rearrange("w (a p) -> (w a) p", p=P)),
        (1, 0, I["conf_conv_w"][layer].rearrange("k (a p) -> (k a) p", p=P)),
        (2, 0, I["ssd_conv_w"][layer].rearrange("k (a p) -> (k a) p", p=P)),
        (2, 60, rows(I["ssd_conv_b"][layer])),
        (2, 72, rows(I["conf_conv_b"][layer])),
        (2, 76, rows(I["conf_ln_g"][layer])),
        (2, 80, rows(I["conf_ln_b"][layer])),
        (2, 84, I["sc_conv_w"][layer].rearrange("k (a p) -> (k a) p", p=P)),
        (2, 96, rows(I["sc_conv_b"][layer])),
        (2, 100, rows(I["ssd_norm"][layer])),
    ]


PACK_ROWS = (120, 124, 108)


def opening(K, following):
    nc, I = K.nc, K.inputs
    L = K.layers
    with ExitStack() as mem:
        xt = mem.enter_context(nc.sbuf_tensor("xt", [P, TT, 8 * P], F32))
        pr = mem.enter_context(nc.sbuf_tensor("pr", [P, L * PACKS, P], F32))
        cr = mem.enter_context(nc.sbuf_tensor("cr", [16, P], F32))
        stage = mem.enter_context(nc.sbuf_tensor("stage", [P, 6, 8, 2 * P], F32))
        split = mem.enter_context(nc.sbuf_tensor("mod_split", [P, 4, 2, 8, P], F32R))
        block = mem.enter_context(nc.Block(no_gpsimd_drain=True))
        x_tiles = [I["ctx"][0, t * P:(t + 1) * P, :] for t in range(2)] + [I["x"][0, t * P:(t + 1) * P, :] for t in range(2)]


        def raw_mod(h):
            panel = K.raw[:, h // 2] if h < 4 else stage[:, h // 2 - 2]
            return panel[:, :, h % 2 * P:h % 2 * P + P]

        @block.sync
        def _(sp):
            sp.dma_start(cr[0:8, :], I["c_ctx"].rearrange("(a p) -> a p", p=P)).then_inc(K.cond_in.inc(16), 16)
            sp.dma_start(cr[8:16, :], I["c"][0].rearrange("(a p) -> a p", p=P)).then_inc(K.cond_in.inc(16), 16)
            for pack, row, src in param_rows(K, 0)[1::2]:
                sp.dma_start(pr[row:row + src.shape[0], pack, :], src).then_inc(K.params_in.inc(16), 16)
            for n in range(2):
                load_panel(K, sp, n, panel_src(K.w_mod[0], 0, 8, 2 * P * n), 8)
            for n in range(6):
                src = panel_src(K.w_mod[0], 0, 8, 2 * P * (n + 2))
                sp.dma_start(stage[:, n, :, :], src).then_inc(K.stage_full[n].inc(16), 16)
            for layer in range(1, L):
                for pack, row, src in param_rows(K, layer):
                    dst = pr[row:row + src.shape[0], layer * PACKS + pack, :]
                    sp.dma_start(dst, src).then_inc(K.params_late.inc(16), 16)
            for layer in range(L):
                row = I["ssd_d"][layer].rearrange("(o h) -> o h", o=1).to_broadcast([P, 16])
                sp.dma_start(K.dload[:, layer, :], row).then_inc(K.small_in.inc(16), 16)
                for src, dst in ((I["ssd_dt_bias"], K.dtb), (I["ssd_a_log"], K.alog)):
                    row = src[layer].rearrange("(o d) h -> o (d h)", o=1).to_broadcast([P, 32])
                    sp.dma_start(dst[:, layer, :], row).then_inc(K.small_in.inc(16), 16)
            for slot, panel in enumerate(following):
                sp.wait_ge(K.mod_lo.sem, K.mod_lo.at(2 + 2 * slot))
                load_panel(K, sp, slot, *panel)

        @block.gpsimd
        def _(pool):
            def select(out, pattern, base, mult, op, fill, after):
                pool.wait_ge(K.const_step.sem, after)
                return nc.gpsimd.affine_select(out=out, in_=out, compare_op=op, fill=fill, base=base,
                                               pattern=pattern, channel_multiplier=mult)
            nc.gpsimd.memset(K.ones[:, :], 1.0).then_inc(K.const_step.inc(), 1)
            nc.gpsimd.memset(K.ident[:, :], 0.0).then_inc(K.const_step.inc(), 1)
            nc.gpsimd.memset(K.tri[:, 0, :], 1.0).then_inc(K.const_step.inc(), 1)
            nc.gpsimd.memset(K.tri[:, 1, :], 1.0).then_inc(K.const_step.inc(), 1)
            nc.gpsimd.memset(K.mask[:, 0, :], 0.0).then_inc(K.const_step.inc(), 1)
            nc.gpsimd.memset(K.mask[:, 1, :], 0.0).then_inc(K.const_step.inc(), 1)
            nc.gpsimd.memset(K.identb[:, :], 0.0).then_inc(K.const_step.inc(), 1)
            nc.gpsimd.memset(K.cond[:, :].bitcast(F32), 0.0).then_inc(K.const_step.inc(), 1)
            nc.gpsimd.memset(K.fold[:, :], 0.0).then_inc(K.const_step.inc(), 1)
            n = K.const_step.count
            line = [[-1, P]]
            select(K.ident[:, :], line, 0, 1, ALU.not_equal, 1.0, n).then_inc(K.const_step.inc(), 1)
            select(K.identb[:, :], line, 0, 1, ALU.not_equal, 1.0, n).then_inc(K.const_step.inc(), 1)
            select(K.fold[:, :], [[-1, 2]], 0, 1, ALU.not_equal, 1.0, n).then_inc(K.const_step.inc(), 1)
            select(K.fold[:, :], [[-1, 2]], -2, 1, ALU.not_equal, 1.0, n + 3).then_inc(K.const_step.inc(), 1)
            for d, (step, mult) in enumerate((([[1, P]], -1), (line, 1))):
                select(K.tri[:, d, :], step, 0, mult, ALU.is_ge, 0.0, n).then_inc(K.const_step.inc(), 1)
                select(K.mask[:, d, :], step, 0, mult, ALU.is_ge, NEG, n).then_inc(K.const_step.inc(), 1)

        @block.tensor
        def _(pe):
            def params(layer):
                for n in range(PACKS):
                    rows = PACK_ROWS[n]
                    at = layer * PACKS + n
                    if layer:
                        pe.wait_ge(K.res_ready.sem, K.res_ready.at(8))
                    if at >= 2:
                        pe.wait_ge(K.turned.sem, K.turned.at(at))
                    ins = nc.tensor.transpose(K.bank[1 + at % 2][:, 0:rows], pr[0:rows, at, :], K.ident[0:rows, 0:rows])
                    ins.then_inc(K.turn.inc(), 1)

            def mods(first):
                for h in range(first, first + 8):
                    mod_mm(K, pe, h, h % 2, h // 2, split[:, h % 4])
                    if h % 2 and h > 1:
                        mod_fold(K, pe, h // 2 - 1)

            pe.wait_ge(K.const_step.sem, K.const_step.at(17))
            pe.wait_ge(K.cond_in.sem, K.cond_in.at(32))
            nc.tensor.transpose(K.bank[0][:, 0:16], cr[:, :], K.ident[0:16, 0:16]).then_inc(K.turn.inc(), 1)
            pe.wait_ge(K.params_in.sem, K.params_in.at(16 * len(param_rows(K, 0))))
            params(0)
            pe.wait_ge(K.cond_ready.sem, K.cond_ready.at(1))
            mods(0)
            pe.wait_ge(K.x_in.sem, K.x_in.at(16 * TT))
            for j in range(8):
                if j >= 4:
                    pe.wait_ge(K.res_ready.sem, K.res_ready.at(j - 3))
                elif j == 0:
                    pe.wait_ge(K.turned.sem, K.turned.at(1 + PACKS))
                for t in range(TT):
                    ins = nc.tensor.transpose(K.bank[j % 4][:, t * P:t * P + P], xt[:, t, j * P:j * P + P], K.ident[:, :])
                ins.then_inc(K.turn.inc(), 1)
            next_rms_pe(K, pe, FULL, 0, 1)
            pe.wait_ge(K.params_late.sem, K.params_late.at(16 * (L - 1) * len(param_rows(K, 0))))
            for layer in range(1, L):
                params(layer)
            mods(8)
            mod_fold(K, pe, 7)

        @block.scalar
        def _(act):
            def params(layer):
                for n in range(PACKS):
                    rows, at = PACK_ROWS[n], layer * PACKS + n
                    act.wait_ge(K.turn.sem, K.turn.at(2 + at + (8 if layer else 0)))
                    ins = nc.scalar.activation(K.par[:, layer, n, 0:rows], K.bank[1 + at % 2][:, 0:rows], ACT.Copy)
                    ins.then_inc(K.turned.inc(), 1)

            def mods(first):
                for h in range(first, first + 8):
                    full = K.raw_full[h // 2] if h < 4 else K.stage_full[h // 2 - 2]
                    act.wait_ge(full.sem, full.landed(1))
                    act.wait_ge(K.mod_mm.sem, K.mod_mm.at(h - 3))
                    ins = nc.scalar.activation(split[:, h % 4, 0], raw_mod(h), ACT.Copy)
                    ins.then_inc(K.mod_hi_done.inc(), 1)

            for pack, row, src in param_rows(K, 0)[0::2]:
                act.dma_start(pr[row:row + src.shape[0], pack, :], src).then_inc(K.params_in.inc(16), 16)
            for t in range(TT):
                act.dma_start(xt[:, t, :], x_tiles[t]).then_inc(K.x_in.inc(16), 16)
            act.wait_ge(K.turn.sem, K.turn.at(1))
            act.wait_ge(K.const_step.sem, K.const_step.at(17))
            ins = nc.scalar.activation(K.condf[:, :, :], K.bank[0][:, 0:16].rearrange("p (s k) -> p k s", k=8), ACT.Silu)
            ins.then_inc(K.act_step.inc(), 1)
            act.wait_ge(K.act_step.sem, K.act_step.own())
            cond = K.cond[:, 0:32].rearrange("p (k c) -> p k c", c=4)
            nc.scalar.activation(cond[:, :, 0:2], K.condf[:, :, :], ACT.Copy).then_inc(K.turned.inc(), 1)
            params(0)
            mods(0)
            for j in range(8):
                act.wait_ge(K.turn.sem, K.turn.at(2 + PACKS + j))
                nc.scalar.activation(K.res[:, j, :], K.bank[j % 4][:, :], ACT.Copy).then_inc(K.res_ready.inc(), 1)
            next_rms_act(K, act, FULL, 0, 1)
            for layer in range(1, L):
                params(layer)
            mods(8)
            split_ahead_act(K, act)

        @block.vector
        def _(dve):
            dve.wait_ge(K.turned.sem, K.turned.at(1))
            cond = K.cond[:, 0:32].rearrange("p (k c) -> p k c", c=4)
            ins = nc.vector.tensor_tensor(cond[:, :, 2:4], K.condf[:, :, :], r32(cond[:, :, 0:2]), ALU.subtract)
            ins.then_inc(K.cond_ready.inc(), 1)
            dve.wait_ge(K.turned.sem, K.turned.at(1 + PACKS))
            for h in range(16):
                if h == 8:
                    next_rms_dve(K, dve, FULL, 0, 1)
                dve.wait_ge(K.mod_hi_done.sem, K.mod_hi_done.at(h + 1))
                ins = nc.vector.tensor_tensor(split[:, h % 4, 1], raw_mod(h), r32(split[:, h % 4, 0]), ALU.subtract)
                ins.then_inc(K.mod_lo.inc(), 1)
                if h % 2 == 0 and h >= 2:
                    mod_row(K, dve, h // 2 - 1)
                if h % 2 == 0 and h >= 4:
                    mod_out(K, dve, 0, h - 4, h // 2 - 2)
            mod_row(K, dve, 7)
            split_ahead_dve(K, dve)
            for panel in (6, 7):
                mod_out(K, dve, 0, 2 * panel, panel)
            dve.wait_ge(K.small_in.sem, K.small_in.at(16 * 3 * L))
            for half in range(2):
                h = slice(64 * half, 64 * half + 64)
                d = K.dload[h, :, :].rearrange("p l (j two) -> p l two j", two=2)[:, :, half, :]
                nc.vector.tensor_copy(K.dskip[h, :, :], d).then_inc(K.small_seen.inc(), 1)
    K.end_phase()


def closing(K):
    nc = K.nc
    with ExitStack() as mem:
        ot = mem.enter_context(nc.sbuf_tensor("ot", [P, 2, 8 * P], F32))
        block = mem.enter_context(nc.Block(no_gpsimd_drain=True))

        @block.tensor
        def _(pe):
            pe.wait_ge(K.res_ready.sem, K.res_ready.own())
            for t in range(2):
                for g in range(2):
                    for q in range(4):
                        j = 4 * g + q
                        ins = nc.tensor.transpose(K.bank[2 * t + g][:, q * P:q * P + P],
                                                  K.res[:, j, CTX + t * P:CTX + t * P + P], K.ident[:, :])
                    ins.then_inc(K.turn.inc(), 1)

        @block.scalar
        def _(act):
            for n in range(4):
                act.wait_ge(K.turn.sem, K.turn.at(n + 1))
                ins = nc.scalar.activation(ot[:, n // 2, n % 2 * 512:n % 2 * 512 + 512], K.bank[n][:, :], ACT.Copy)
                ins.then_inc(K.turned.inc(), 1)

        @block.sync
        def _(sp):
            for t in range(2):
                sp.wait_ge(K.turned.sem, K.turned.at(2 * t + 2))
                sp.dma_start(K.out[0, t * P:(t + 1) * P, :], ot[:, t, :]).then_inc(K.stored.inc(16), 16)
            sp.wait_ge(K.stored.sem, K.stored.at(32))
    K.end_phase()



def hybrid_block(nc, inputs, out):
    K = Kern()
    K.nc, K.inputs, K.out = nc, inputs, out
    K.layers = inputs["w_mod"].shape[0]
    K.d_ff = inputs["ffn_w_gate"].shape[3]
    K.w_mod, K.w_gate, K.w_up, K.w_down = (inputs[n] for n in ("w_mod", "ffn_w_gate", "ffn_w_up", "ffn_w_down"))
    K.w_in, K.w_out = inputs["w_in"], inputs["w_out"]
    assert inputs["w_mod"].shape[1] == 8 * P and K.d_ff % (2 * P) == 0 and 16 * P < K.d_ff <= 24 * P
    L = K.layers
    with ExitStack() as ctx:
        def sb(name, shape, dt=F32):
            return ctx.enter_context(nc.sbuf_tensor(name, shape, dt))

        K.signals = []

        def signal(name):
            K.signals.append(Signal(ctx.enter_context(nc.semaphore(name))))
            return K.signals[-1]

        K.a_exp = signal("a_exp")
        K.act_read = signal("act_read")
        K.act_step = signal("act_step")
        K.b_ready = signal("b_ready")
        K.b_turned = signal("b_turned")
        K.cb_mm = signal("cb_mm")
        K.cb_ready = signal("cb_ready")
        K.cent_ready = signal("cent_ready")
        K.cond_in = signal("cond_in")
        K.cond_ready = signal("cond_ready")
        K.const_step = signal("const_step")
        K.conv_done = signal("conv_done")
        K.cum_read = signal("cum_read")
        K.cum_ready = signal("cum_ready")
        K.decay_ready = signal("decay_ready")
        K.diag_ready = signal("diag_ready")
        K.diff_ready = signal("diff_ready")
        K.dt_abs = signal("dt_abs")
        K.dt_exp = signal("dt_exp")
        K.dt_ln = signal("dt_ln")
        K.dt_out = signal("dt_out")
        K.dt_raw = signal("dt_raw")
        K.dt_ready = signal("dt_ready")
        K.dt_u = signal("dt_u")
        K.dtw_hi = signal("dtw_hi")
        K.dtw_in = signal("dtw_in")
        K.dtw_ready = signal("dtw_ready")
        K.dve_read = signal("dve_read")
        K.dve_step = signal("dve_step")
        K.e_ready = signal("e_ready")
        K.g_ready = signal("g_ready")
        K.half_done = signal("half_done")
        K.hh_done = signal("hh_done")
        K.hi_done = signal("hi_done")
        K.hl_done = signal("hl_done")
        K.ln_ready = signal("ln_ready")
        K.lo_done = signal("lo_done")
        K.m_ready = signal("m_ready")
        K.mean_ready = signal("mean_ready")
        K.mod_evac = signal("mod_evac")
        K.mod_fold = signal("mod_fold")
        K.mod_hi_done = signal("mod_hi_done")
        K.mod_lo = signal("mod_lo")
        K.mod_mm = signal("mod_mm")
        K.mod_row = signal("mod_row")
        K.mod_row_hi = signal("mod_row_hi")
        K.ms_ready = signal("ms_ready")
        K.off_mm = signal("off_mm")
        K.off_used = signal("off_used")
        K.pads_zero = signal("pads_zero")
        K.params_in = signal("params_in")
        K.params_late = signal("params_late")
        K.pgain_ready = signal("pgain_ready")
        K.prod_done = signal("prod_done")
        K.rb_ready = signal("rb_ready")
        K.res_ready = signal("res_ready")
        K.res_tail = signal("res_tail")
        K.yr_ready = signal("yr_ready")
        K.square_ready = signal("square_ready")
        K.pair_ready = signal("pair_ready")
        K.rstd_ready = signal("rstd_ready")
        K.silu_done = signal("silu_done")
        K.small_in = signal("small_in")
        K.small_seen = signal("small_seen")
        K.sq_ready = signal("sq_ready")
        K.st_ready = signal("st_ready")
        K.stat_done = signal("stat_done")
        K.state_mm = signal("state_mm")
        K.stored = signal("stored")
        K.turn = signal("turn")
        K.turned = signal("turned")
        K.uh_ready = signal("uh_ready")
        K.ul_ready = signal("ul_ready")
        K.un_ready = signal("un_ready")
        K.x_in = signal("x_in")
        K.xbc_conv = signal("xbc_conv")
        K.xbc_out = signal("xbc_out")
        K.xd_ready = signal("xd_ready")
        K.xs_turned = signal("xs_turned")
        K.xw_ready = signal("xw_ready")
        K.y_mm = signal("y_mm")
        K.y_ready = signal("y_ready")
        K.y_turned = signal("y_turned")
        K.z_used = signal("z_used")
        K.xh_ready = signal("xh_ready")
        K.xl_ready = signal("xl_ready")
        K.yn_ready = signal("yn_ready")
        K.ytm_ready = signal("ytm_ready")
        K.raw_full = [signal(f"raw_full{n}") for n in range(2)]
        K.mod_full = signal("mod_full")
        K.stage_full = [signal(f"stage_full{n}") for n in range(6)]
        K.bank = [ctx.enter_context(nc.psum_tensor(f"bank{n}", [P, 512], F32)) for n in range(8)]
        K.res = sb("res", [P, 8, TOK])
        K.raw = sb("raw", [P, 2, 8, 2 * P])
        K.split = sb("split", [P, 2, 2, 8, P], F32R)
        K.wh, K.wl = K.split[:, 0], K.split[:, 1]
        K.sq = sb("sq", [P, 2, TOK])
        K.diag = K.sq[:, 0, :].rearrange("p (t n) -> p t n", n=P)
        K.par = sb("par", [P, L, PACKS, P])
        K.mod = sb("mod", [P, L, 72, 2])
        K.condf = sb("condf", [P, 8, 2])
        K.cond = sb("cond", [P, 28 + P], F32R)
        K.rows = sb("rows", [4, 2 * P])
        K.fold = sb("fold", [4, 2])
        K.gain, K.pgain = sb("gain", [P, 8, 2]), sb("pgain", [P, 8, 2])
        K.ms, K.rstd = sb("ms", [P, TT]), sb("rstd", [P, TT])
        K.ident, K.ones = sb("ident", [P, P]), sb("ones", [P, P])
        K.identb = sb("identb", [P, P], BF16)
        K.tri = sb("tri", [P, 2, P])
        K.mask = sb("mask", [P, 2, P], BF16)
        K.dskip = sb("dskip", [P, L, 8])
        K.dload = sb("dload", [P, L, 16])
        K.dtb, K.alog = sb("dtb", [P, L, 32]), sb("alog", [P, L, 32])

        def ff_first(layer, ff):
            return [(panel_src(w[layer, ff], 0, 8, 0), 8) for w in (K.w_gate, K.w_up)]

        opening(K, ff_first(0, 0))
        for layer in range(L):
            last = layer == L - 1
            feed_forward(K, layer, 0, FULL, layer, 16 if layer == 0 else 68, layer == 0,
                         12 if layer == 0 else 4, mixer_first(K, layer))
            mixer(K, layer, last, ff_first(layer, 1))
            after = ff_first(layer + 1, 0) if not last else []
            feed_forward(K, layer, 2, LATENT if last else FULL, None if last else layer + 1, 0, not last,
                         0 if last else 24, after)
        closing(K)


NAMES = ["x", "c", "ctx", "c_ctx", "w_mod", "b_mod", "norm_pre", "norm_post", "ffn_w_gate", "ffn_w_up", "ffn_w_down",
         "w_in", "ssd_conv_w", "ssd_conv_b", "ssd_dt_bias", "ssd_a_log", "ssd_d", "ssd_norm", "conf_conv_w",
         "conf_conv_b", "conf_ln_g", "conf_ln_b", "sc_conv_w", "sc_conv_b", "w_out"]


def kernel(**inputs):
    import numpy as np
    import concourse.bacc as bacc
    from concourse.bass_utils import run_bass_kernel_spmd

    nc = bacc.Bacc("TRN2", target_bir_lowering=False, num_devices=1)
    arrays, aps = {}, {}
    for name in NAMES:
        a = np.ascontiguousarray(inputs[name])
        arrays[f"in_{name}"] = a
        aps[name] = nc.dram_tensor(f"in_{name}", a.shape, mybir.dt.from_np(a.dtype), kind="ExternalInput").ap()
    out = nc.dram_tensor("out_x", inputs["x"].shape, F32, kind="ExternalOutput").ap()
    hybrid_block(nc, aps, out)
    return run_bass_kernel_spmd(nc, [arrays], core_ids=[0]).results[0]["out_x"]
```
